# Optimizing a Trainium2 kernel written in Bass

```python
import math
import jax, jax.numpy as jnp
from jax import lax
import numpy as np

D_MODEL = 1024
BATCH = 1
SEQ = 256
DEPTH = 2

HEAD_DIM = 64
BRANCH_WIDTH = D_MODEL
N_BRANCH = 3
SSM_INNER = BRANCH_WIDTH
SSM_HEAD_DIM = 64
SSM_HEADS = SSM_INNER // SSM_HEAD_DIM
SSM_GROUPS = 4
SSM_HEADS_PER_GROUP = SSM_HEADS // SSM_GROUPS
SSM_STATE = 128
SSM_CONV_DIM = SSM_INNER + 2 * SSM_GROUPS * SSM_STATE
CONV_WIDTH = 4
SSD_CHUNK = 128
SWA_HEADS = BRANCH_WIDTH // HEAD_DIM
SWA_KV_HEADS = 4
SWA_GROUP = SWA_HEADS // SWA_KV_HEADS
SWA_WINDOW = 128
SWA_BLOCK = 128
FOX_HEADS = BRANCH_WIDTH // HEAD_DIM
FOX_BLOCK = 128
ROPE_THETA = 10000.0
NORM_EPS = 1e-6
IN_SIZES = (SSM_CONV_DIM, SSM_INNER, SSM_HEADS,
            SWA_HEADS * HEAD_DIM, SWA_KV_HEADS * HEAD_DIM, SWA_KV_HEADS * HEAD_DIM, BRANCH_WIDTH,
            FOX_HEADS * HEAD_DIM, FOX_HEADS * HEAD_DIM, FOX_HEADS * HEAD_DIM, FOX_HEADS, BRANCH_WIDTH,
            N_BRANCH * D_MODEL)
N_IN = sum(IN_SIZES)


def rms_norm(x, w):
    xf = x.astype(jnp.float32)
    y = xf * lax.rsqrt(jnp.mean(xf * xf, axis=-1, keepdims=True) + NORM_EPS)
    return (y * w.astype(jnp.float32)).astype(x.dtype)

def grouped_rms_norm(y, w, groups):
    b, s, d = y.shape
    yf = y.astype(jnp.float32).reshape(b, s, groups, d // groups)
    yf = yf * lax.rsqrt(jnp.mean(yf * yf, axis=-1, keepdims=True) + NORM_EPS)
    return (yf.reshape(b, s, d) * w.astype(jnp.float32)).astype(y.dtype)

def rope(x, cos, sin):
    half = x.shape[-1] // 2
    x1, x2 = x[..., :half], x[..., half:]
    c, s = cos[None, :, None, :], sin[None, :, None, :]
    return jnp.concatenate([x1 * c - x2 * s, x2 * c + x1 * s], axis=-1)

def causal_depthwise_conv(u, w, bias):
    c = u.shape[-1]
    out = lax.conv_general_dilated(u, w[:, None, :], window_strides=(1,),
                                   padding=[(CONV_WIDTH - 1, 0)],
                                   dimension_numbers=('NWC', 'WIO', 'NWC'),
                                   feature_group_count=c)
    return out + bias

def ssd_chunked_scan(xh, dt, a, bm, cm):
    b, s, g, r, p = xh.shape
    n = bm.shape[-1]
    nc, l = s // SSD_CHUNK, SSD_CHUNK
    dtype = xh.dtype
    x = xh.reshape(b, nc, l, g, r, p)
    dtc = dt.reshape(b, nc, l, g, r)
    x_dt = x * dtc[..., None]
    bc = bm.reshape(b, nc, l, g, n)
    cc = cm.reshape(b, nc, l, g, n)
    a_dt = jnp.transpose(dtc.astype(jnp.float32) * a.astype(jnp.float32), (0, 3, 4, 1, 2))
    a_cum = jnp.cumsum(a_dt, axis=-1)
    idx = jnp.arange(l)
    causal = idx[:, None] >= idx[None, :]
    seg = a_cum[..., :, None] - a_cum[..., None, :]
    decay = jnp.where(causal, jnp.exp(jnp.where(causal, seg, 0.0)), 0.0).astype(dtype)
    cb = jnp.einsum('bclgn,bcsgn->bgcls', cc, bc)
    y_diag = jnp.einsum('bgrcls,bcsgrp->bclgrp', cb[:, :, None] * decay, x_dt)
    decay_states = jnp.exp(a_cum[..., -1:] - a_cum).astype(dtype)
    states = jnp.einsum('bcsgn,bgrcs,bcsgrp->bcgrpn', bc, decay_states, x_dt)
    chunk_decay = jnp.exp(a_cum[..., -1]).astype(dtype)

    def step(h, inp):
        st, dec = inp
        return h * dec[..., None, None] + st, h

    h0 = jnp.zeros((b, g, r, p, n), dtype)
    _, prev = lax.scan(step, h0, (jnp.moveaxis(states, 1, 0), jnp.moveaxis(chunk_decay, -1, 0)))
    prev = jnp.moveaxis(prev, 0, 1)
    y_off = jnp.einsum('bclgn,bcgrpn,bgrcl->bclgrp', cc, prev, jnp.exp(a_cum).astype(dtype))
    return (y_diag + y_off).reshape(b, s, g, r, p)

def mamba2_branch(xbc, z, dt_raw, conv_w, conv_b, dt_bias, a_log, d_skip, norm_w):
    b, s, _ = xbc.shape
    xbc = jax.nn.silu(causal_depthwise_conv(xbc, conv_w, conv_b))
    gn = SSM_GROUPS * SSM_STATE
    xs, bm, cm = jnp.split(xbc, [SSM_INNER, SSM_INNER + gn], axis=-1)
    xh = xs.reshape(b, s, SSM_GROUPS, SSM_HEADS_PER_GROUP, SSM_HEAD_DIM)
    dt = jax.nn.softplus(dt_raw + dt_bias).reshape(b, s, SSM_GROUPS, SSM_HEADS_PER_GROUP)
    a = -jnp.exp(a_log).reshape(SSM_GROUPS, SSM_HEADS_PER_GROUP)
    y = ssd_chunked_scan(xh, dt, a,
                         bm.reshape(b, s, SSM_GROUPS, SSM_STATE),
                         cm.reshape(b, s, SSM_GROUPS, SSM_STATE))
    y = y + d_skip.reshape(SSM_GROUPS, SSM_HEADS_PER_GROUP)[:, :, None] * xh
    y = y.reshape(b, s, SSM_INNER) * jax.nn.silu(z)
    return grouped_rms_norm(y, norm_w, SSM_GROUPS)

def sliding_window_branch(q, k, v, z, sinks, cos, sin):
    b, s, _ = q.shape
    nb, blk = s // SWA_BLOCK, SWA_BLOCK
    q = rope(q.reshape(b, s, SWA_HEADS, HEAD_DIM), cos, sin)
    k = rope(k.reshape(b, s, SWA_KV_HEADS, HEAD_DIM), cos, sin)
    v = v.reshape(b, s, SWA_KV_HEADS, HEAD_DIM)
    qb = q.reshape(b, nb, blk, SWA_KV_HEADS, SWA_GROUP, HEAD_DIM)
    pad = ((0, 0), (blk, 0), (0, 0), (0, 0))
    kp, vp = jnp.pad(k, pad)[:, :s], jnp.pad(v, pad)[:, :s]
    kb = jnp.concatenate([kp.reshape(b, nb, blk, SWA_KV_HEADS, HEAD_DIM),
                          k.reshape(b, nb, blk, SWA_KV_HEADS, HEAD_DIM)], axis=2)
    vb = jnp.concatenate([vp.reshape(b, nb, blk, SWA_KV_HEADS, HEAD_DIM),
                          v.reshape(b, nb, blk, SWA_KV_HEADS, HEAD_DIM)], axis=2)
    scores = jnp.einsum('bnqkgd,bnskd->bnkgqs', qb, kb).astype(jnp.float32) * (HEAD_DIM ** -0.5)
    qi = jnp.arange(blk)[:, None]
    sj = jnp.arange(2 * blk)[None, :]
    diff = qi + blk - sj
    band = (diff >= 0) & (diff < SWA_WINDOW)
    key_pos = jnp.arange(nb)[:, None, None] * blk - blk + sj[None]
    mask = band[None] & (key_pos >= 0)
    scores = jnp.where(mask[None, :, None, None], scores, -jnp.inf)
    sink = jnp.broadcast_to(sinks.astype(jnp.float32).reshape(1, 1, SWA_KV_HEADS, SWA_GROUP, 1, 1),
                            scores.shape[:-1] + (1,))
    probs = jax.nn.softmax(jnp.concatenate([scores, sink], axis=-1), axis=-1)[..., :-1]
    out = jnp.einsum('bnkgqs,bnskd->bnqkgd', probs.astype(v.dtype), vb)
    return out.reshape(b, s, SWA_HEADS * HEAD_DIM) * jax.nn.silu(z)

def forgetting_attention_branch(q, k, v, f_logit, z, f_bias):
    b, s, _ = q.shape
    q = q.reshape(b, s, FOX_HEADS, HEAD_DIM)
    k = k.reshape(b, s, FOX_HEADS, HEAD_DIM)
    v = v.reshape(b, s, FOX_HEADS, HEAD_DIM)
    log_f = jax.nn.log_sigmoid((f_logit + f_bias).astype(jnp.float32))
    cum = jnp.transpose(jnp.cumsum(log_f, axis=1), (0, 2, 1))
    scale = HEAD_DIM ** -0.5
    outs = []
    for i in range(s // FOX_BLOCK):
        start, end = i * FOX_BLOCK, (i + 1) * FOX_BLOCK
        sc = jnp.einsum('bqhd,bkhd->bhqk', q[:, start:end], k[:, :end]).astype(jnp.float32) * scale
        sc = sc + cum[:, :, start:end, None] - cum[:, :, None, :end]
        causal = (start + jnp.arange(FOX_BLOCK))[:, None] >= jnp.arange(end)[None, :]
        sc = jnp.where(causal[None, None], sc, -jnp.inf)
        probs = jax.nn.softmax(sc, axis=-1).astype(v.dtype)
        outs.append(jnp.einsum('bhqk,bkhd->bqhd', probs, v[:, :end]))
    out = jnp.concatenate(outs, axis=1)
    return out.reshape(b, s, FOX_HEADS * HEAD_DIM) * jax.nn.silu(z)

def first_inputs(seed: int = 0) -> dict:
    key = jax.random.key(seed)
    ks = jax.random.split(key, 16)
    L, D, W = DEPTH, D_MODEL, BRANCH_WIDTH
    x = jax.random.normal(ks[0], (BATCH, SEQ, D), jnp.float32)
    norm_w = 1.0 + 0.1 * jax.random.normal(ks[1], (L, D), jnp.float32)
    w_in = jax.random.normal(ks[2], (L, D, N_IN), jnp.float32) * D ** -0.5
    conv_w = jax.random.normal(ks[3], (L, CONV_WIDTH, SSM_CONV_DIM), jnp.float32) * CONV_WIDTH ** -0.5
    conv_b = 0.01 * jax.random.normal(ks[4], (L, SSM_CONV_DIM), jnp.float32)
    u = jax.random.uniform(ks[5], (L, SSM_HEADS), jnp.float32)
    dt0 = jnp.exp(u * (math.log(0.1) - math.log(0.001)) + math.log(0.001))
    dt_bias = dt0 + jnp.log(-jnp.expm1(-dt0))
    a_log = jnp.log(jax.random.uniform(ks[6], (L, SSM_HEADS), jnp.float32, minval=1.0, maxval=16.0))
    d_skip = 1.0 + 0.1 * jax.random.normal(ks[7], (L, SSM_HEADS), jnp.float32)
    ssm_norm_w = 1.0 + 0.1 * jax.random.normal(ks[8], (L, SSM_INNER), jnp.float32)
    sinks = 0.5 * jax.random.normal(ks[9], (L, SWA_HEADS), jnp.float32)
    f_bias = 3.0 + 0.5 * jax.random.normal(ks[10], (L, FOX_HEADS), jnp.float32)
    gate_bias = 0.1 * jax.random.normal(ks[11], (L, N_BRANCH, D), jnp.float32)
    w_proj = jax.random.normal(ks[12], (L, N_BRANCH, W, D), jnp.float32) * W ** -0.5
    w_out = jax.random.normal(ks[13], (L, D, D), jnp.float32) * D ** -0.5
    final_norm_w = 1.0 + 0.1 * jax.random.normal(ks[14], (D,), jnp.float32)
    return {"x": x, "norm_w": norm_w, "w_in": w_in, "conv_w": conv_w, "conv_b": conv_b,
            "dt_bias": dt_bias, "a_log": a_log, "d_skip": d_skip, "ssm_norm_w": ssm_norm_w,
            "sinks": sinks, "f_bias": f_bias, "gate_bias": gate_bias, "w_proj": w_proj,
            "w_out": w_out, "final_norm_w": final_norm_w}

def first_block(x, norm_w, w_in, conv_w, conv_b, dt_bias, a_log, d_skip, ssm_norm_w,
              sinks, f_bias, gate_bias, w_proj, w_out, final_norm_w):
    b, s, d = x.shape
    pos = jnp.arange(s, dtype=jnp.float32)
    inv_freq = ROPE_THETA ** (-jnp.arange(0, HEAD_DIM, 2, dtype=jnp.float32) / HEAD_DIM)
    ang = pos[:, None] * inv_freq[None, :]
    cos, sin = jnp.cos(ang).astype(x.dtype), jnp.sin(ang).astype(x.dtype)
    split_at = [int(v) for v in np.cumsum(IN_SIZES)[:-1]]
    for layer in range(DEPTH):
        h = rms_norm(x, norm_w[layer])
        proj = jnp.einsum('bsd,de->bse', h, w_in[layer])
        (a_xbc, a_z, a_dt, b_q, b_k, b_v, b_z,
         c_q, c_k, c_v, c_f, c_z, gates) = jnp.split(proj, split_at, axis=-1)
        y_a = mamba2_branch(a_xbc, a_z, a_dt, conv_w[layer], conv_b[layer], dt_bias[layer],
                            a_log[layer], d_skip[layer], ssm_norm_w[layer])
        y_b = sliding_window_branch(b_q, b_k, b_v, b_z, sinks[layer], cos, sin)
        y_c = forgetting_attention_branch(c_q, c_k, c_v, c_f, c_z, f_bias[layer])
        ys = jnp.stack([y_a, y_b, y_c], axis=2)
        branch = jnp.einsum('bsiw,iwd->bsid', ys, w_proj[layer])
        g = jax.nn.sigmoid(gates.reshape(b, s, N_BRANCH, d) + gate_bias[layer])
        merged = jnp.sum(g * branch, axis=2)
        x = x + jnp.einsum('bsd,de->bse', merged, w_out[layer])
    return rms_norm(x, final_norm_w)


DEPTH_2 = 1

MEM_LEN = 256
SSM_WIDTH = 512
SSM_GROUP = 16
SSM_GROUPS_2 = SSM_WIDTH // SSM_GROUP
SSM_STATE_2 = 64
DSA_HEADS = 8
DSA_HEAD_DIM = 64
IDX_HEADS = 4
IDX_DIM = 64
IDX_TOPK_MAX = 256
Q_BLOCK = 128
MEM_HEADS = 4
MEM_HEAD_DIM = 128
N_BRANCHES = 3
N_GROUPS = 4
EXPERTS_PER_GROUP = 8
N_EXPERTS = N_GROUPS * EXPERTS_PER_GROUP
TOP_K_EXPERTS = 2
EXPERT_FF = 512
EPS = 1e-6
IN_SPLITS = (SSM_WIDTH, DSA_HEADS * DSA_HEAD_DIM, DSA_HEAD_DIM, DSA_HEAD_DIM, IDX_HEADS * IDX_DIM, IDX_DIM, IDX_HEADS, MEM_HEADS * MEM_HEAD_DIM, N_BRANCHES * D_MODEL)
IN_COLS = sum(IN_SPLITS)


F32 = jnp.float32

def rms_norm_2(x, g):
    xf = x.astype(F32)
    y = xf * lax.rsqrt(jnp.mean(xf * xf, axis=-1, keepdims=True) + EPS)
    return (y * g.astype(F32)).astype(x.dtype)

def rope_tables(positions, dim):
    inv = 1.0 / (ROPE_THETA ** (jnp.arange(0, dim, 2, dtype=F32) / dim))
    ang = positions.astype(F32)[..., None] * inv
    return jnp.cos(ang), jnp.sin(ang)

def apply_rope(x, cos, sin):
    extra = x.ndim - cos.ndim
    cos = cos.reshape(cos.shape[:2] + (1,) * extra + cos.shape[2:])
    sin = sin.reshape(sin.shape[:2] + (1,) * extra + sin.shape[2:])
    x1, x2 = jnp.split(x.astype(F32), 2, axis=-1)
    out = jnp.concatenate([x1 * cos - x2 * sin, x2 * cos + x1 * sin], axis=-1)
    return out.astype(x.dtype)

def _ssm_combine(e1, e2):
    a1, b1 = e1
    a2, b2 = e2
    return a1 * a2, a2 * b1 + b2

def s5_branch(u, lam_re, lam_im, log_dt, b_re, b_im, c_re, c_im, d_skip, w_glu):
    bsz, seq, _ = u.shape
    uf = u.astype(F32).reshape(bsz, seq, SSM_GROUPS_2, SSM_GROUP)
    lam = lax.complex(lam_re.astype(F32), lam_im.astype(F32))
    dt = jnp.exp(log_dt.astype(F32))[:, None]
    lam_bar = jnp.exp(lam * dt)
    b = lax.complex(b_re.astype(F32), b_im.astype(F32))
    b_bar = ((lam_bar - 1.0) / lam)[..., None] * b
    bu = jnp.einsum('bsgh,gph->bsgp', uf.astype(jnp.complex64), b_bar)
    a = jnp.broadcast_to(lam_bar, (1, seq) + lam_bar.shape)
    _, states = lax.associative_scan(_ssm_combine, (a, bu), axis=1)
    c = lax.complex(c_re.astype(F32), c_im.astype(F32))
    y = jnp.real(jnp.einsum('bsgp,ghp->bsgh', states, c))
    y = y + d_skip.astype(F32).reshape(SSM_GROUPS_2, SSM_GROUP) * uf
    y = jax.nn.gelu(y.reshape(bsz, seq, SSM_WIDTH))
    y = y * jax.nn.sigmoid(y @ w_glu.astype(F32))
    return y.astype(u.dtype)

def dsa_branch(q, k, v, qi, ki, wi, pos):
    bsz, seq = pos.shape
    topk = min(IDX_TOPK_MAX, seq // 4)
    nb = seq // Q_BLOCK
    kif = ki.astype(F32)
    gather = jax.vmap(lambda src, idx: src[idx])

    def to_blocks(t):
        t = t.reshape((bsz, nb, Q_BLOCK) + t.shape[2:])
        return jnp.moveaxis(t, 1, 0)

    def block_fn(args):
        qb, qib, wib, posb = args
        sc = jnp.einsum('bqhd,bsd->bqhs', qib.astype(F32), kif) * (IDX_DIM ** -0.5)
        iscore = jnp.einsum('bqh,bqhs->bqs', wib.astype(F32), jax.nn.relu(sc))
        causal = pos[:, None, :] <= posb[:, :, None]
        iscore = jnp.where(causal, iscore, -jnp.inf)
        _, idx = lax.top_k(iscore, topk)
        ks = gather(k, idx).astype(F32)
        vs = gather(v, idx).astype(F32)
        ps = gather(pos, idx)
        s = jnp.einsum('bqhd,bqkd->bqhk', qb.astype(F32), ks) * (DSA_HEAD_DIM ** -0.5)
        valid = (ps <= posb[..., None])[:, :, None, :]
        p = jax.nn.softmax(jnp.where(valid, s, -jnp.inf), axis=-1)
        o = jnp.einsum('bqhk,bqkd->bqhd', p, vs)
        return o.astype(qb.dtype)

    out = lax.map(block_fn, (to_blocks(q), to_blocks(qi), to_blocks(wi), to_blocks(pos)))
    out = jnp.moveaxis(out, 0, 1).reshape(bsz, seq, DSA_HEADS * DSA_HEAD_DIM)
    return out

def memory_branch(qm, km, vm):
    bsz, seq = qm.shape[:2]
    s = jnp.einsum('bshd,bmhd->bhsm', qm.astype(F32), km.astype(F32)) * (MEM_HEAD_DIM ** -0.5)
    p = jax.nn.softmax(s, axis=-1)
    o = jnp.einsum('bhsm,bmhd->bshd', p, vm.astype(F32))
    return o.reshape(bsz, seq, MEM_HEADS * MEM_HEAD_DIM).astype(qm.dtype)

def hier_moe(h, w_group, b_group, w_expert, b_expert, w_gate, w_up, w_down):
    bsz, seq, d = h.shape
    t = h.reshape(-1, d)
    hf = t.astype(F32)
    g_prob = jax.nn.softmax(hf @ w_group.astype(F32) + b_group.astype(F32), axis=-1)
    g_idx = jnp.argmax(g_prob, axis=-1)
    g_gate = jnp.take_along_axis(g_prob, g_idx[:, None], axis=-1)[:, 0]
    e_logits = (hf @ w_expert.astype(F32)).reshape(-1, N_GROUPS, EXPERTS_PER_GROUP) + b_expert.astype(F32)
    e_logits = jnp.take_along_axis(e_logits, g_idx[:, None, None], axis=1)[:, 0]
    e_prob = jax.nn.softmax(e_logits, axis=-1)
    top_p, top_i = lax.top_k(e_prob, TOP_K_EXPERTS)
    top_w = g_gate[:, None] * top_p / jnp.sum(top_p, axis=-1, keepdims=True)
    global_i = g_idx[:, None] * EXPERTS_PER_GROUP + top_i
    combine = jnp.sum(jax.nn.one_hot(global_i, N_EXPERTS, dtype=F32) * top_w[..., None], axis=1)
    out = jnp.zeros(hf.shape, F32)
    for e in range(N_EXPERTS):
        hid = jax.nn.silu(t @ w_gate[e]) * (t @ w_up[e])
        out = out + combine[:, e:e + 1] * (hid @ w_down[e]).astype(F32)
    return out.reshape(bsz, seq, d).astype(h.dtype)

def hybrid_layer(x, mem, positions, g_mix, g_mem, w_in, lam_re, lam_im, log_dt, b_re, b_im, c_re, c_im, d_skip, w_glu, g_q, g_k, g_qm, g_km, w_mem_kv, w_up_ssm, w_up_dsa, w_up_mem, w_out, g_ffn, w_group, b_group, w_expert, b_expert, w_gate, w_up, w_down):
    bsz, seq, _ = x.shape
    mlen = mem.shape[1]
    h = rms_norm_2(x, g_mix)
    proj = h @ w_in
    offs = [int(o) for o in np.cumsum(IN_SPLITS)[:-1]]
    u_ssm, q, k, v, qi, ki, wi, qm, gates = jnp.split(proj, offs, axis=-1)
    cos_a, sin_a = rope_tables(positions, DSA_HEAD_DIM)
    cos_i, sin_i = rope_tables(positions, IDX_DIM)
    q = apply_rope(rms_norm_2(q.reshape(bsz, seq, DSA_HEADS, DSA_HEAD_DIM), g_q), cos_a, sin_a)
    k = apply_rope(rms_norm_2(k, g_k), cos_a, sin_a)
    qi = apply_rope(qi.reshape(bsz, seq, IDX_HEADS, IDX_DIM), cos_i, sin_i)
    ki = apply_rope(ki, cos_i, sin_i)
    wi = wi * (IDX_HEADS ** -0.5)
    qm = rms_norm_2(qm.reshape(bsz, seq, MEM_HEADS, MEM_HEAD_DIM), g_qm)
    km, vm = jnp.split(rms_norm_2(mem, g_mem) @ w_mem_kv, 2, axis=-1)
    km = rms_norm_2(km.reshape(bsz, mlen, MEM_HEADS, MEM_HEAD_DIM), g_km)
    vm = vm.reshape(bsz, mlen, MEM_HEADS, MEM_HEAD_DIM)

    y_ssm = s5_branch(u_ssm, lam_re, lam_im, log_dt, b_re, b_im, c_re, c_im, d_skip, w_glu)
    y_dsa = dsa_branch(q, k, v, qi, ki, wi, positions)
    y_mem = memory_branch(qm, km, vm)

    g_s, g_d, g_m = jnp.split(jax.nn.sigmoid(gates), N_BRANCHES, axis=-1)
    merged = g_s * (y_ssm @ w_up_ssm) + g_d * (y_dsa @ w_up_dsa) + g_m * (y_mem @ w_up_mem)
    x = x + merged @ w_out
    x = x + hier_moe(rms_norm_2(x, g_ffn), w_group, b_group, w_expert, b_expert, w_gate, w_up, w_down)
    return x

def second_inputs(seed: int = 0) -> dict:
    key = jax.random.key(seed)
    ks = iter(jax.random.split(key, 48))
    L = DEPTH_2

    def nrm(shape, scale):
        return jax.random.normal(next(ks), shape, F32) * scale

    def gain(shape):
        return 1.0 + 0.02 * jax.random.normal(next(ks), shape, F32)

    x = nrm((BATCH, SEQ, D_MODEL), 1.0)
    mem = nrm((BATCH, MEM_LEN, D_MODEL), 1.0)
    offset = jax.random.randint(next(ks), (BATCH, 1), 0, 1024, dtype=jnp.int32)
    positions = offset + jnp.arange(SEQ, dtype=jnp.int32)[None, :]
    n = jnp.arange(SSM_STATE_2, dtype=F32)
    lam_re = -0.5 + nrm((L, SSM_GROUPS_2, SSM_STATE_2), 0.01)
    lam_im = jnp.pi * n + nrm((L, SSM_GROUPS_2, SSM_STATE_2), 0.01)
    log_dt = jax.random.uniform(next(ks), (L, SSM_GROUPS_2), F32, math.log(1e-3), math.log(1e-1))
    return {
        'x': x,
        'mem': mem,
        'positions': positions,
        'g_mix': gain((L, D_MODEL)),
        'g_mem': gain((L, D_MODEL)),
        'w_in': nrm((L, D_MODEL, IN_COLS), D_MODEL ** -0.5),
        'lam_re': lam_re,
        'lam_im': lam_im,
        'log_dt': log_dt,
        'b_re': nrm((L, SSM_GROUPS_2, SSM_STATE_2, SSM_GROUP), (2 * SSM_GROUP) ** -0.5),
        'b_im': nrm((L, SSM_GROUPS_2, SSM_STATE_2, SSM_GROUP), (2 * SSM_GROUP) ** -0.5),
        'c_re': nrm((L, SSM_GROUPS_2, SSM_GROUP, SSM_STATE_2), SSM_STATE_2 ** -0.5),
        'c_im': nrm((L, SSM_GROUPS_2, SSM_GROUP, SSM_STATE_2), SSM_STATE_2 ** -0.5),
        'd_skip': nrm((L, SSM_WIDTH), 1.0),
        'w_glu': nrm((L, SSM_WIDTH, SSM_WIDTH), SSM_WIDTH ** -0.5),
        'g_q': gain((L, DSA_HEAD_DIM)),
        'g_k': gain((L, DSA_HEAD_DIM)),
        'g_qm': gain((L, MEM_HEAD_DIM)),
        'g_km': gain((L, MEM_HEAD_DIM)),
        'w_mem_kv': nrm((L, D_MODEL, 2 * MEM_HEADS * MEM_HEAD_DIM), D_MODEL ** -0.5),
        'w_up_ssm': nrm((L, SSM_WIDTH, D_MODEL), SSM_WIDTH ** -0.5),
        'w_up_dsa': nrm((L, DSA_HEADS * DSA_HEAD_DIM, D_MODEL), (DSA_HEADS * DSA_HEAD_DIM) ** -0.5),
        'w_up_mem': nrm((L, MEM_HEADS * MEM_HEAD_DIM, D_MODEL), (MEM_HEADS * MEM_HEAD_DIM) ** -0.5),
        'w_out': nrm((L, D_MODEL, D_MODEL), D_MODEL ** -0.5),
        'g_ffn': gain((L, D_MODEL)),
        'w_group': nrm((L, D_MODEL, N_GROUPS), D_MODEL ** -0.5),
        'b_group': nrm((L, N_GROUPS), 0.01),
        'w_expert': nrm((L, D_MODEL, N_EXPERTS), D_MODEL ** -0.5),
        'b_expert': nrm((L, N_GROUPS, EXPERTS_PER_GROUP), 0.01),
        'w_gate': nrm((L, N_EXPERTS, D_MODEL, EXPERT_FF), D_MODEL ** -0.5),
        'w_up': nrm((L, N_EXPERTS, D_MODEL, EXPERT_FF), D_MODEL ** -0.5),
        'w_down': nrm((L, N_EXPERTS, EXPERT_FF, D_MODEL), EXPERT_FF ** -0.5),
    }

def second_block(x, mem, positions, g_mix, g_mem, w_in, lam_re, lam_im, log_dt, b_re, b_im, c_re, c_im, d_skip, w_glu, g_q, g_k, g_qm, g_km, w_mem_kv, w_up_ssm, w_up_dsa, w_up_mem, w_out, g_ffn, w_group, b_group, w_expert, b_expert, w_gate, w_up, w_down):
    for l in range(DEPTH_2):
        x = hybrid_layer(x, mem, positions, g_mix[l], g_mem[l], w_in[l], lam_re[l], lam_im[l], log_dt[l], b_re[l], b_im[l], c_re[l], c_im[l], d_skip[l], w_glu[l], g_q[l], g_k[l], g_qm[l], g_km[l], w_mem_kv[l], w_up_ssm[l], w_up_dsa[l], w_up_mem[l], w_out[l], g_ffn[l], w_group[l], b_group[l], w_expert[l], b_expert[l], w_gate[l], w_up[l], w_down[l])
    return x


def setup_inputs(seed=0):
    out = dict(first_inputs(seed))
    for name, value in second_inputs(seed + 1).items():
        if name != "x":
            out[name + "_2"] = value
    return out


def reference(
    x, norm_w, w_in, conv_w, conv_b, dt_bias, a_log, d_skip, ssm_norm_w, sinks, f_bias,
    gate_bias, w_proj, w_out, final_norm_w, mem_2, positions_2, g_mix_2, g_mem_2, w_in_2,
    lam_re_2, lam_im_2, log_dt_2, b_re_2, b_im_2, c_re_2, c_im_2, d_skip_2, w_glu_2, g_q_2,
    g_k_2, g_qm_2, g_km_2, w_mem_kv_2, w_up_ssm_2, w_up_dsa_2, w_up_mem_2, w_out_2, g_ffn_2,
    w_group_2, b_group_2, w_expert_2, b_expert_2, w_gate_2, w_up_2, w_down_2,
):
    x = first_block(
        x, norm_w, w_in, conv_w, conv_b, dt_bias, a_log, d_skip, ssm_norm_w, sinks, f_bias,
        gate_bias, w_proj, w_out, final_norm_w,
    )
    return second_block(
        x, mem_2, positions_2, g_mix_2, g_mem_2, w_in_2, lam_re_2, lam_im_2, log_dt_2, b_re_2,
        b_im_2, c_re_2, c_im_2, d_skip_2, w_glu_2, g_q_2, g_k_2, g_qm_2, g_km_2, w_mem_kv_2,
        w_up_ssm_2, w_up_dsa_2, w_up_mem_2, w_out_2, g_ffn_2, w_group_2, b_group_2, w_expert_2,
        b_expert_2, w_gate_2, w_up_2, w_down_2,
    )


_drawn_inputs = setup_inputs


def setup_inputs(seed=0):
    import zlib

    import numpy as np

    out = dict(_drawn_inputs(seed))
    spreads = {}
    factors = {'sinks': 3.731,
     'g_mem_2': 8.0,
     'lam_re_2': 64.0,
     'log_dt_2': 173.504,
     'c_im_2': 28.816,
     'g_q_2': 26.126,
     'g_k_2': 35.378,
     'g_qm_2': 6.594,
     'g_km_2': 7.961,
     'b_group_2': 52.976,
     'b_expert_2': 36.951,
     'lam_im_2': 8.0,
     'b_re_2': 8.0,
     'b_im_2': 8.0,
     'c_re_2': 8.0,
     'w_glu_2': 4.385,
     'g_ffn_2': 6.909}
    for name, (base, spread) in spreads.items():
        noise = np.random.default_rng([zlib.crc32(name.encode()), seed]).standard_normal(out[name].shape)
        drawn = base * np.exp(spread * noise) if base else spread * noise
        out[name] = __import__('jax').numpy.asarray(drawn.astype(out[name].dtype))
    for name, factor in factors.items():
        out[name] = (out[name] * factor).astype(out[name].dtype)
    return out
```

```python
from contextlib import ExitStack

import itertools

import numpy as np

import concourse.bass as bass
from concourse import mybir

F32 = mybir.dt.float32
BF16 = mybir.dt.bfloat16
I32 = mybir.dt.int32
ALU = mybir.AluOpType
ACT = mybir.ActivationFunctionType
AX = mybir.AxisListType.X
ADD, SUB, MUL, MAX, MIN = ALU.add, ALU.subtract, ALU.mult, ALU.max, ALU.min

P = 128
D = 1024
S = 256
T = S // P
KD = D // P
TURNS = 0.15915494309189535
ROUND = 12582912.0
PI, HALF_PI = 3.1415925, 1.5707963267948966
TWO_PI = (6.28125, 0.0019350051879882812, 3.019916050561733e-07)
LATER, STRUCK = 1e37, -1e38
LAYERS = 2
CH = 512
EPS = 1e-6
NEG = -1e30

XBC, ZA, DT, KV, ZB = 0, 2048, 3072, 4112, 4624
QB, CQ, CK, CV, CF, CZ, GATES = 3088, 5648, 6672, 7696, 8720, 8736, 9760
N_IN = GATES + 3 * D
HEADS, HD = 16, 64
KVH = 4
GROUPS, RPG = 4, 4
CONV_W = 4

U2, Q2, KVI2, QM2, GATES2 = 0, 512, 1024, 1476, 1988
N_IN2 = GATES2 + 3 * D
SG, SH, SN = 32, 16, 64
ST = SG * SN // P
TOPK = min(256, S // 4)
EXP, FF = 32, 512
NGRP, EPG = 4, 8


class Step:

    def __init__(self, sem, value=None):
        self.sem, self.value, self.needed = sem, value, False


class Lane:

    def __init__(self, sem, chained):
        self.sem, self.chained, self.queue, self.last = sem, chained, [], None

    def do(self, emit, after=()):
        after = [s for s in after if s is not None]
        if self.chained and self.last is not None:
            after.append(self.last)
        step = Step(self.sem)
        for s in after:
            s.needed = True
        self.queue.append((emit, after, step))
        self.last = step
        return step

    def count(self):
        n = 0
        for _, _, step in self.queue:
            if step.needed and step.value is None:
                n += 1
                step.value = n

    def emit(self, engine):
        seen = {}
        for emit, after, step in self.queue:
            for s in after:
                if seen.get(s.sem.name, 0) < s.value:
                    engine.wait_ge(s.sem, s.value)
                    seen[s.sem.name] = s.value
            made = emit(engine)
            if step.needed and step.sem is self.sem:
                made.then_inc(self.sem, 1)


class Loads:

    def __init__(self, new_sem):
        self.new_sem, self.queue, self.sems = new_sem, [], {}

    def load(self, name, pairs, after=()):
        if name not in self.sems:
            self.sems[name] = [self.new_sem("dma_" + name), 0]
        entry = self.sems[name]
        after = [s for s in after if s is not None]
        for s in after:
            s.needed = True
        for out, src in pairs:
            entry[1] += 16
            self.queue.append((out, src, after, entry[0]))
        return Step(entry[0], entry[1])

    def emit(self, engine):
        seen = {}
        for out, src, after, sem in self.queue:
            for s in after:
                if seen.get(s.sem.name, 0) < s.value:
                    engine.wait_ge(s.sem, s.value)
                    seen[s.sem.name] = s.value
            engine.dma_start(out, src).then_inc(sem, 16)


class Ring:

    def __init__(self, slots):
        self.slots, self.readers, self.at = slots, [[] for _ in slots], 0

    def take(self):
        i = self.at % len(self.slots)
        self.at += 1
        return i, self.slots[i], self.readers[i]

    def done(self, i, steps):
        self.readers[i] = list(steps)


def bc(ap, n):
    return ap.unsqueeze(2).to_broadcast([ap.shape[0], ap.shape[1], n])


def build(nc, d, out):
    ctx = ExitStack()
    with ctx:
        def sb(name, cols, dt=F32):
            return ctx.enter_context(nc.sbuf_tensor(name, [P, cols], dt))

        def sem(name):
            return ctx.enter_context(nc.semaphore(name))

        pe, dve, act, pool = Lane(sem("pe"), False), Lane(sem("dve"), True), Lane(sem("act"), True), Lane(sem("pool"), True)
        sp = Loads(sem)

        consts = sb("consts", 1408)
        small_cols = sb("small_cols", d["cols"].shape[1])
        x_t = sb("x", T * D)
        hT_t = sb("hT", KD * S)
        merged = sb("merged", T * D)
        R = [sb(f"r{i}", T * D) for i in range(11)]
        wslots = [sb(f"w{i}", KD * CH + CH) for i in range(4)]
        small = sb("small", 1600)
        rows = sb("rows", 320)
        scratch = [sb(f"scratch{i}", CH) for i in range(3)]
        idbf = sb("ident_bf16", P, BF16)
        maskbf = sb("masks_bf16", 3 * P, BF16)
        banks = [ctx.enter_context(nc.psum_tensor(f"bank{i}", [P, CH], F32)) for i in range(8)]

        ident, upto, ones_gt = consts[:, 0:128], consts[:, 128:256], consts[:, 256:512]
        ones, above = consts[:, 256:384], consts[:, 384:512]
        causal01 = consts[:, 128:256]
        cosT = consts[:, 896:960].rearrange("p (t f) -> p t f", t=T)
        sinT = consts[:, 960:1024].rearrange("p (t f) -> p t f", t=T)
        x3 = x_t[:, :].rearrange("p (t c) -> p t c", t=T)
        m3 = merged[:, :].rearrange("p (t c) -> p t c", t=T)
        hT = hT_t[:, :].rearrange("p (k s) -> p k s", k=KD)

        wring = Ring(wslots)
        bulk = Ring(banks[0:4])
        work = Ring(banks[4:8])
        scr = Ring(scratch)

        cursor = [0]

        def stat(n):
            if cursor[0] + n > 1600:
                raise ValueError("statistics area is full")
            a = small[:, cursor[0]:cursor[0] + n]
            cursor[0] += n
            return a

        def now():
            return [l.last for l in (pe, dve, act, pool) if l.last is not None]

        def tok(ap):
            return ap.rearrange("p (t c) -> p t c", t=T)

        const_in = sp.load("consts", [(consts[:, 0:1408], d["consts"]), (small_cols[:, :], d["cols"])])
        x_in = sp.load("x", [(x_t[:, t * D:(t + 1) * D], d["x"][t * P:(t + 1) * P, :]) for t in range(T)])
        maskbf_made = dve.do(lambda v: v.tensor_copy(maskbf[:, 0:3 * P], consts[:, 512:896]), after=[const_in])
        dve.do(lambda v: v.tensor_copy(idbf[:, :], ident))
        causal_mask, window_mask = maskbf[:, 0:P], maskbf[:, P:3 * P]

        def rsqrt(r, v, scale, tmp):
            dve.do(lambda e: e.tensor_scalar(v, v, scale, EPS, MUL, ADD))
            s = act.do(lambda e: e.activation(r, v, ACT.Ln), after=[dve.last])
            s = act.do(lambda e: e.activation(r, r, ACT.Exp, scale=-0.5))
            for _ in range(2):
                dve.do(lambda e: e.tensor_tensor(tmp, r, r, MUL), after=[s])
                dve.do(lambda e: e.tensor_tensor(tmp, tmp, v, MUL))
                dve.do(lambda e: e.tensor_scalar(tmp, tmp, -0.5, 1.5, MUL, ADD))
                s = dve.do(lambda e: e.tensor_tensor(r, r, tmp, MUL))
            return s

        def recip_1p(a, after=()):
            dve.do(lambda e: e.tensor_scalar(a, a, 1.0, None, ADD), after=after)
            return dve.do(lambda e: e.reciprocal(a, a))

        def log1p_exp_neg_abs(r, x, z, q, after=()):
            dve.do(lambda e: e.scalar_tensor_tensor(r, x, -1.0, x, MUL, MAX), after=after)
            s = act.do(lambda e: e.activation(r, r, ACT.Exp, scale=-1.0), after=[dve.last])
            dve.do(lambda e: e.tensor_scalar(z, r, 2.0, None, ADD), after=[s])
            dve.do(lambda e: e.reciprocal(z, z))
            dve.do(lambda e: e.tensor_tensor(r, r, z, MUL))
            dve.do(lambda e: e.tensor_tensor(z, r, r, MUL))
            dve.do(lambda e: e.tensor_scalar(q, z, 1.0 / 17, None, MUL))
            for n in (15, 13, 11, 9, 7, 5, 3):
                dve.do(lambda e, n=n: e.scalar_tensor_tensor(q, q, 1.0 / n, z, ADD, MUL))
            dve.do(lambda e: e.scalar_tensor_tensor(q, q, 1.0, r, ADD, MUL))
            return dve.do(lambda e: e.tensor_scalar(r, q, 2.0, None, MUL))

        def transposes(blocks, emit_out, after=(), width=4):
            for b0 in range(0, len(blocks), width):
                part = blocks[b0:b0 + width]
                i, bank, readers = work.take()
                for j, blk in enumerate(part):
                    c = blk.shape[1]
                    s = pe.do(lambda e, j=j, blk=blk, c=c, bank=bank: e.transpose(
                        bank[0:c, j * P:(j + 1) * P], blk, ident), after=list(after) + readers)
                work.done(i, emit_out(b0, len(part), bank, s))

        def rms_factor(src3, after=()):
            parts, ss, r, tmp = stat(2 * T), stat(T), stat(T), stat(T)
            i, squares, readers = scr.take()
            for t in range(T):
                for h in range(2):
                    s = act.do(lambda e, t=t, h=h: e.activation(squares[:, :], src3[:, t, h * CH:(h + 1) * CH], ACT.Square,
                               accum_out=parts[:, 2 * t + h:2 * t + h + 1]), after=list(after) + readers)
            scr.done(i, [s])
            dve.do(lambda e: e.tensor_reduce(ss, parts.rearrange("p (t h) -> p t h", h=2), AX, ADD), after=[s])
            return r, rsqrt(r, ss, 1.0 / D, tmp)

        def to_hT(src3, normed3, col0, after=(), dst=None, dst_free=None):
            r, s = rms_factor(src3, after)
            for t in range(T):
                s = dve.do(lambda e, t=t: e.tensor_scalar(normed3[:, t, :], src3[:, t, :], r[:, t:t + 1], None, MUL))
            blocks = [normed3[:, t, k * P:(k + 1) * P] for t in range(T) for k in range(KD)]
            to = hT if dst is None else dst
            dst_free = hT_readers if dst is None else dst_free

            def copy_out(b0, n, bank, step):
                t, k = divmod(b0, KD)
                return [dve.do(lambda e: e.tensor_tensor(
                    to[:, k:k + n, t * P:(t + 1) * P], bank[:, 0:n * P].rearrange("p (k s) -> p k s", k=n),
                    bc(small_cols[:, col0 + k:col0 + k + n], P), MUL), after=[step, const_in] + dst_free)]
            transposes(blocks, copy_out, after=[s])
            return dve.last

        hT_readers = []

        def chunk_load(src, rows_n, n, bias=None):
            i, slot, readers = wring.take()
            k = rows_n // P
            w = slot[:, 0:k * n].rearrange("p (k n) -> p k n", k=k)
            pairs = [(w, src.rearrange("(k p) n -> p k n", p=P))]
            if bias is not None:
                pairs.append((slot[0:1, KD * CH:KD * CH + n], bias))
            s = sp.load(f"w{i}", pairs, after=readers)
            return i, slot, w, s

        def project(lhsT, src, rows_n, n, copy_out, after=(), bias=None):
            i, slot, w, loaded = chunk_load(src, rows_n, n, bias)
            k_n = rows_n // P
            got = []
            for t in range(T):
                b, bank, readers = bulk.take()
                if bias is not None:
                    pe.do(lambda e, bank=bank: e.matmul(bank[:, 0:n], ones[0:1, :], slot[0:1, KD * CH:KD * CH + n],
                          start=True, stop=False), after=[loaded, const_in] + readers)
                for k in range(k_n):
                    s = pe.do(lambda e, k=k, t=t, bank=bank: e.matmul(
                        bank[:, 0:n], lhsT[:, k, t * P:(t + 1) * P], w[:, k, :],
                        start=(k == 0 and bias is None), stop=(k == k_n - 1)),
                        after=[loaded] + readers + list(after))
                got.append((b, bank, s))
            wring.done(i, [s])
            for t, (b, bank, s) in enumerate(got):
                bulk.done(b, copy_out(t, bank, s))

        def copy_to(dst3, c0, n):
            def f(t, bank, step):
                return [act.do(lambda e: e.copy(dst3[:, t, c0:c0 + n], bank[:, 0:n]), after=[step] + wait_for)]
            wait_for = []
            f.wait_for = wait_for
            return f

        def silu_to(dst3, c0, n, free):
            def f(t, bank, step):
                i, e_t, readers = scr.take()
                s = act.do(lambda e: e.activation(e_t[:, 0:n], bank[:, 0:n], ACT.Exp, scale=-1.0), after=[step] + readers)
                recip_1p(e_t[:, 0:n], after=[s])
                s = dve.do(lambda e: e.tensor_tensor(dst3[:, t, c0:c0 + n], bank[:, 0:n], e_t[:, 0:n], MUL), after=free)
                scr.done(i, [s])
                return [s]
            return f

        def plain_to(dst3, c0, n, free, scale=None):
            def f(t, bank, step):
                if scale is None:
                    return [act.do(lambda e: e.copy(dst3[:, t, c0:c0 + n], bank[:, 0:n]), after=[step] + free)]
                return [act.do(lambda e: e.mul(dst3[:, t, c0:c0 + n], bank[:, 0:n], scale), after=[step] + free)]
            return f

        def gated_add(yT, ky, wg, wp, bias_row, first, y_ready):
            for n0 in range(0, D, CH):
                sig = {}

                def gate_out(t, bank, step):
                    i, e_t, readers = scr.take()
                    s = act.do(lambda e: e.activation(e_t[:, :], bank[:, :], ACT.Exp, scale=-1.0), after=[step] + readers)
                    recip_1p(e_t[:, :], after=[s])
                    sig[t] = (i, e_t)
                    return [s]

                def branch_out(t, bank, step):
                    i, e_t = sig[t]
                    dst = m3[:, t, n0:n0 + CH]
                    if first:
                        s = dve.do(lambda e: e.tensor_tensor(dst, bank[:, :], e_t[:, :], MUL), after=[step] + merged_readers)
                        scr.done(i, [s])
                        return [s]
                    s0 = dve.do(lambda e: e.tensor_tensor(e_t[:, :], bank[:, :], e_t[:, :], MUL), after=[step])
                    s = dve.do(lambda e: e.tensor_tensor(dst, dst, e_t[:, :], ADD))
                    scr.done(i, [s])
                    return [s0]
                project(hT, wg[:, n0:n0 + CH], D, CH, gate_out,
                        bias=None if bias_row is None else bias_row[:, n0:n0 + CH])
                yield
                project(yT, wp[:, n0:n0 + CH], ky * P, CH, branch_out, after=y_ready)
                yield

        merged_readers = []

        def out_projection(w, mT, after_free):
            blocks = [m3[:, t, k * P:(k + 1) * P] for t in range(T) for k in range(KD)]

            def copy_out(b0, n, bank, step):
                t, k = divmod(b0, KD)
                return [act.do(lambda e: e.copy(mT[:, k:k + n, t * P:(t + 1) * P],
                                                bank[:, 0:n * P].rearrange("p (k s) -> p k s", k=n)), after=[step] + after_free)]
            transposes(blocks, copy_out, after=[dve.last])
            merged_readers[:] = [pe.last]
            ready = [act.last]
            for n0 in range(0, D, CH):
                def add(t, bank, step):
                    dst = x3[:, t, n0:n0 + CH]
                    return [dve.do(lambda e: e.tensor_tensor(dst, dst, bank[:, :], ADD), after=[step])]
                project(mT, w[:, n0:n0 + CH], D, CH, add, after=ready)

        def transpose_scaled(y3, yT, n_k, ready, free, col0=None):
            blocks = [y3[:, t, k * P:(k + 1) * P] for t in range(T) for k in range(n_k)]
            width = min(4, n_k)

            def copy_out(b0, n, bank, step):
                t, k = divmod(b0, n_k)
                dst = yT[:, k:k + n, t * P:(t + 1) * P]
                src = bank[:, 0:n * P].rearrange("p (k s) -> p k s", k=n)
                if col0 is None:
                    return [act.do(lambda e: e.copy(dst, src), after=[step] + free)]
                return [dve.do(lambda e: e.tensor_tensor(dst, src, bc(small_cols[:, col0 + k:col0 + k + n], P), MUL),
                               after=[step] + free)]
            transposes(blocks, copy_out, after=ready, width=width)
            return [act.last if col0 is None else dve.last]

        def attention(units, n_heads, dv, y3, y_free, v_of, ready, p_buf, pT_buf, sink=None, zsilu3=None, z_ready=()):
            mx_all, sum_all = stat(T * n_heads), stat(T * n_heads)
            pring, ptring = Ring(p_buf), Ring(pT_buf)
            outs, filled = {}, {}
            per_bank = CH // dv
            state = []

            def stage_scores(u):
                t, h0, hn, hs, scores, keys = u
                i, bank, readers = work.take()
                for j in range(hn):
                    s = scores(h0 + j * hs, t, bank[:, j * keys:(j + 1) * keys], list(ready) + readers)
                c = t * n_heads + h0
                mx = mx_all[:, c:c + hs * (hn - 1) + 1:hs]
                s = dve.do(lambda e: e.tensor_reduce(mx, bank[:, 0:hn * keys].rearrange("p (h k) -> p h k", h=hn), AX, MAX), after=[s])
                if sink is not None:
                    dve.do(lambda e: e.tensor_tensor(mx, mx, sink[:, h0:h0 + hs * (hn - 1) + 1:hs], MAX))
                s = dve.do(lambda e: e.tensor_scalar(mx, mx, -1.0, None, MUL))
                pi, p, preaders = pring.take()
                for j in range(hn):
                    a = act.do(lambda e, j=j: e.activation(p[:, j * keys:(j + 1) * keys], bank[:, j * keys:(j + 1) * keys], ACT.Exp,
                               bias=mx[:, j:j + 1], accum_out=sum_all[:, c + j * hs:c + j * hs + 1]), after=[s] + preaders)
                work.done(i, [a])
                return pi, p, a

            def stage_transpose(u, pi, p, a):
                t, h0, hn, hs, scores, keys = u
                kb = keys // P
                n = hn * kb
                i, bank, readers = work.take()
                for j in range(n):
                    s = pe.do(lambda e, j=j: e.transpose(bank[:, j * P:(j + 1) * P], p[:, j * P:(j + 1) * P], ident), after=[a] + readers)
                pring.done(pi, [s])
                ti, pT, treaders = ptring.take()
                s = dve.do(lambda e: e.tensor_copy(pT[:, 0:n * P], bank[:, 0:n * P]), after=[s] + treaders)
                work.done(i, [s])
                return ti, pT, s

            def stage_pv(u, ti, pT, ready_pT):
                t, h0, hn, hs, scores, keys = u
                kb = keys // P
                for j in range(hn):
                    h = h0 + j * hs
                    key = (t, h // per_bank)
                    if key not in outs:
                        outs[key] = bulk.take()
                        filled[key] = 0
                    i, bank, readers = outs[key]
                    c = (h % per_bank) * dv
                    for b in range(kb):
                        s = pe.do(lambda e, j=j, b=b, bank=bank, c=c, h=h: e.matmul(
                            bank[:, c:c + dv], pT[:, (j * kb + b) * P:(j * kb + b + 1) * P], v_of(h, b),
                            start=(b == 0), stop=(b == kb - 1)), after=[ready_pT] + readers)
                    filled[key] += 1
                    if filled[key] == min(per_bank, n_heads):
                        first = h // per_bank * per_bank
                        finish(t, first, first + filled[key], i, bank, s)
                ptring.done(ti, [s])

            def finish(t, h0, h1, i, bank, s):
                c = t * n_heads
                sm, mx = sum_all[:, c + h0:c + h1], mx_all[:, c + h0:c + h1]
                n = h1 - h0
                if sink is not None:
                    es = stat(n)
                    dve.do(lambda e: e.tensor_tensor(es, sink[:, h0:h1], mx, ADD))
                    a = act.do(lambda e: e.activation(es, es, ACT.Exp), after=[dve.last])
                    dve.do(lambda e: e.tensor_tensor(sm, sm, es, ADD), after=[a])
                dve.do(lambda e: e.reciprocal(sm, sm), after=[act.last])
                dst = y3[:, t, h0 * dv:h1 * dv]
                s = dve.do(lambda e: e.tensor_tensor(dst.rearrange("p (h c) -> p h c", h=n),
                           bank[:, 0:n * dv].rearrange("p (h c) -> p h c", h=n), bc(sm, dv), MUL), after=[s] + list(y_free))
                bulk.done(i, [s])
                if zsilu3 is not None:
                    dve.do(lambda e: e.tensor_tensor(dst, dst, zsilu3[:, t, h0 * dv:h1 * dv], MUL), after=z_ready)

            a1, a2 = {}, {}
            n = len(units)
            for i in range(n + 2):
                if i < n:
                    a1[i] = stage_scores(units[i])
                if 1 <= i <= n:
                    a2[i - 1] = stage_transpose(units[i - 1], *a1.pop(i - 1))
                if i >= 2:
                    stage_pv(units[i - 2], *a2.pop(i - 2))
                yield

        def rope(dst, src, cos, sin, heads, tmp, half=HD // 2, free=()):
            def b(a):
                return a.unsqueeze(1).to_broadcast([P, heads, half])
            x1, x2 = src[:, :, 0:half], src[:, :, half:2 * half]
            t1, t2 = tmp[:, :, 0:half], tmp[:, :, half:2 * half]
            d1, d2 = dst[:, :, 0:half], dst[:, :, half:2 * half]
            dve.do(lambda e: e.tensor_tensor(t1, x2, b(sin), MUL), after=free)
            dve.do(lambda e: e.tensor_tensor(t2, x1, b(sin), MUL))
            dve.do(lambda e: e.tensor_tensor(d1, x1, b(cos), MUL))
            dve.do(lambda e: e.tensor_tensor(d2, x2, b(cos), MUL))
            dve.do(lambda e: e.tensor_tensor(d1, d1, t1, SUB))
            return dve.do(lambda e: e.tensor_tensor(d2, d2, t2, ADD))

        def together(main, side, ratio=1.0):
            due, live = 0.0, True
            for _ in main:
                due += ratio
                while live and due >= 1:
                    due -= 1
                    live = next(side, "end") != "end"
            for _ in side:
                pass

        def layer(l):
            cursor[0] = 0
            w_in, w_proj, w_out = d["w_in"][l], d["w_proj"][l], d["w_out"][l]
            col = COLS1[l]
            base = now()
            rowp = d["rows"]
            r0 = ROWS1[l]
            row_in = sp.load("rows", [(rows[:, 0:5 * 16], rowp[:, r0:r0 + 5 * 16].to_broadcast([P, 5 * 16]))], after=base)
            dt_bias, a_log, d_skip, sinks, f_bias = (rows[:, 16 * i:16 * i + 16] for i in range(5))
            normed = tok(R[9][:, :])
            to_hT(x3, normed, col["norm"], after=[x_in, dve.last])
            h_ready = [dve.last]
            free = now()

            def seq(*sections):
                for f in sections:
                    yield from f

            def plain(c0, n, dst3, dcol, fr, scale=None):
                for o in range(0, n, CH):
                    m = min(CH, n - o)
                    project(hT, w_in[:, c0 + o:c0 + o + m], D, m, plain_to(dst3, dcol + o, m, fr, scale), after=h_ready)
                    yield

            def silu(c0, n, dst3, fr):
                for o in range(0, n, CH):
                    project(hT, w_in[:, c0 + o:c0 + o + CH], D, CH, silu_to(dst3, o, CH, fr), after=h_ready)
                    yield

            xbc = [tok(R[0][:, :]), tok(R[1][:, :])]
            za = tok(R[2][:, :])
            dtr = stat(2 * 16).rearrange("p (t h) -> p t h", t=T)
            fr_ = stat(2 * 16).rearrange("p (t h) -> p t h", t=T)
            for _ in seq(plain(DT, 16, dtr, 0, free), plain(XBC, D, xbc[0], 0, free),
                         plain(XBC + D, D, xbc[1], 0, free)):
                pass

            def mamba():
                raw = [R[3][:, :].rearrange("p (k s) -> p k s", k=KD), R[4][:, :].rearrange("p (k s) -> p k s", k=KD)]
                conv = [R[0][:, :].rearrange("p (k s) -> p k s", k=KD), R[1][:, :].rearrange("p (k s) -> p k s", k=KD)]
                for half in range(2):
                    transpose_scaled(xbc[half], raw[half], KD, [act.last], free)
                    yield
                last_t = [pe.last]
                for half in range(2):
                    for k in range(KD):
                        c = half * KD + k
                        u, o = raw[half][:, k, :], conv[half][:, k, :]
                        wc = [small_cols[:, col["conv"] + w * 16 + c:col["conv"] + w * 16 + c + 1] for w in range(CONV_W)]
                        bcol = small_cols[:, col["conv_b"] + c:col["conv_b"] + c + 1]
                        dve.do(lambda e, u=u, o=o, wc=wc, bcol=bcol: e.tensor_scalar(o, u, wc[3], bcol, MUL, ADD), after=[act.last] + last_t)
                        for w in range(3):
                            sh = 3 - w
                            dve.do(lambda e, u=u, o=o, wc=wc, w=w, sh=sh: e.scalar_tensor_tensor(
                                o[:, sh:S], u[:, 0:S - sh], wc[w], o[:, sh:S], MUL, ADD))
                    src, e_t = R[half], R[3 + half]
                    a = act.do(lambda e, src=src, e_t=e_t: e.activation(e_t[:, :], src[:, :], ACT.Exp, scale=-1.0), after=[dve.last])
                    recip_1p(e_t[:, :], after=[a])
                    dve.do(lambda e, src=src, e_t=e_t: e.tensor_tensor(src[:, :], src[:, :], e_t[:, :], MUL))
                    yield
                conv_ready = [dve.last]
                xT, bcT = conv
                x_tok, xdt = tok(R[3][:, :]), tok(R[4][:, :])
                blocks = [xT[:, k, t * P:(t + 1) * P] for t in range(T) for k in range(KD)]

                def x_out(b0, n, bank, step):
                    t, k = divmod(b0, KD)
                    return [act.do(lambda e: e.copy(x_tok[:, t, k * P:(k + n) * P], bank[:, 0:n * P]), after=[step, conv_ready[0]])]
                transposes(blocks, x_out, after=conv_ready)
                b_tok = R[9][:, 0:GROUPS * P].rearrange("p (g n) -> p g n", g=GROUPS)
                blocks = [bcT[:, g, 0:P] for g in range(GROUPS)]
                transposes(blocks, lambda b0, n, bank, step: [act.do(
                    lambda e: e.copy(b_tok[:, b0:b0 + n, :], bank[:, 0:n * P].rearrange("p (g n) -> p g n", g=n)), after=[step] + free)],
                    after=conv_ready)
                x_ready = act.last
                yield
                dt, adt, z, q = (stat(32).rearrange("p (t h) -> p t h", t=T) for _ in range(4))
                na = stat(16)
                dve.do(lambda e: e.tensor_tensor(dtr, dtr, dt_bias.unsqueeze(1).to_broadcast([P, T, 16]), ADD), after=[row_in, act.last])
                s = act.do(lambda e: e.activation(na, a_log, ACT.Exp), after=[row_in])
                log1p_exp_neg_abs(dt, dtr, z, q)
                dve.do(lambda e: e.scalar_tensor_tensor(dt, dtr, 0.0, dt, MAX, ADD))
                dve.do(lambda e: e.scalar_tensor_tensor(adt, dt, -1.0, na.unsqueeze(1).to_broadcast([P, T, 16]), MUL, MUL), after=[s])
                adt_ready = dve.last
                for t in range(T):
                    dve.do(lambda e, t=t: e.tensor_tensor(xdt[:, t, :].rearrange("p (h c) -> p h c", h=HEADS),
                           x_tok[:, t, :].rearrange("p (h c) -> p h c", h=HEADS), bc(dt[:, t, :], HD), MUL), after=[x_ready])
                xdt_ready = dve.last
                i, bank, readers = work.take()
                pe.do(lambda e: e.matmul(bank[:, 0:16], above, adt[:, 0, :], start=True, stop=True), after=[adt_ready] + readers)
                s = pe.do(lambda e: e.matmul(bank[:, 16:32], upto, adt[:, 1, :], start=True, stop=True))
                decs = stat(32)
                s = act.do(lambda e: e.activation(decs, bank[:, 0:32], ACT.Exp), after=[s])
                work.done(i, [s])
                to_end, from_start = decs[:, 0:16], decs[:, 16:32]
                xds = R[9][:, CH:CH + D]
                dve.do(lambda e: e.tensor_tensor(xds.rearrange("p (h c) -> p h c", h=HEADS), xdt[:, 0, :].rearrange("p (h c) -> p h c", h=HEADS),
                       bc(to_end, HD), MUL), after=[s] + free)
                state = R[10][:, 0:D]
                for g in range(0, GROUPS, 2):
                    i, bank, readers = work.take()
                    for j in range(2):
                        s = pe.do(lambda e, g=g, j=j, bank=bank: e.matmul(bank[:, j * 256:(j + 1) * 256], b_tok[:, g + j, :],
                                  xds[:, (g + j) * 256:(g + j + 1) * 256], start=True, stop=True), after=[dve.last, x_ready] + readers)
                    s = act.do(lambda e, g=g, bank=bank: e.copy(state[:, g * 256:(g + 2) * 256], bank[:, :]), after=[s] + free)
                    work.done(i, [s])
                state_ready = act.last
                yield
                cb = R[10][:, D:2 * D].rearrange("p (t g l) -> p t g l", t=T, g=GROUPS)
                for t in range(T):
                    i, bank, readers = work.take()
                    for g in range(GROUPS):
                        s = pe.do(lambda e, t=t, g=g, bank=bank: e.matmul(bank[:, g * P:(g + 1) * P], bcT[:, g, t * P:(t + 1) * P],
                                  bcT[:, GROUPS + g, t * P:(t + 1) * P], start=True, stop=True), after=conv_ready + readers)
                    s = dve.do(lambda e, t=t, bank=bank: e.tensor_tensor(cb[:, t, :, :], bank[:, :].rearrange("p (g l) -> p g l", g=GROUPS),
                               causal01.unsqueeze(1).to_broadcast([P, GROUPS, P]), MUL), after=[s] + free)
                    work.done(i, [s])
                yield
                y = tok(R[0][:, :])
                ya_free = [act.last, dve.last]
                lhs_ring, m_ring = Ring([R[9][:, 0:CH], R[9][:, CH:2 * CH]]), Ring([R[9][:, 2 * CH:3 * CH], R[9][:, 3 * CH:4 * CH]])
                lhs_ring.readers = [[pe.last], [pe.last]]
                todo, pend = [(t, g) for t in range(T) for g in range(GROUPS)], []
                for n in range(len(todo) + 1):
                    if n < len(todo):
                        t, g = todo[n]
                        li, lhs, lr = lhs_ring.take()
                        lhs3 = lhs.rearrange("p (r k) -> p r k", r=RPG)
                        s = dve.do(lambda e, t=t, g=g, lhs3=lhs3: e.tensor_tensor(lhs3, above.unsqueeze(1).to_broadcast([P, RPG, P]),
                                   bc(adt[:, t, g * RPG:(g + 1) * RPG], P), MUL), after=lr)
                        i, bank, readers = work.take()
                        for r in range(RPG):
                            s2 = pe.do(lambda e, r=r, lhs3=lhs3, bank=bank: e.matmul(bank[:, r * P:(r + 1) * P], lhs3[:, r, :], upto,
                                       start=True, stop=True), after=[s] + readers)
                        lhs_ring.done(li, [s2])
                        mi, m, mr = m_ring.take()
                        s3 = act.do(lambda e, m=m, bank=bank: e.activation(m, bank[:, :], ACT.Exp), after=[s2] + mr)
                        work.done(i, [s3])
                        s4 = dve.do(lambda e, m=m, t=t, g=g: e.tensor_tensor(m.rearrange("p (r l) -> p r l", r=RPG), m.rearrange("p (r l) -> p r l", r=RPG),
                                    cb[:, t, g, :].unsqueeze(1).to_broadcast([P, RPG, P]), MUL), after=[s3])
                        pend.append((t, g, mi, m, s4))
                    if n >= 1:
                        t, g, mi, m, s4 = pend.pop(0)
                        i, bank, readers = work.take()
                        for r in range(RPG):
                            h = g * RPG + r
                            s = pe.do(lambda e, r=r, h=h, t=t, m=m, bank=bank: e.matmul(bank[:, r * HD:(r + 1) * HD], m[:, r * P:(r + 1) * P],
                                      xdt[:, t, h * HD:(h + 1) * HD], start=True, stop=True), after=[s4, xdt_ready] + readers)
                        m_ring.done(mi, [s])
                        if t == 1:
                            s = pe.do(lambda e, g=g, bank=bank: e.matmul(bank[:, 256:512], bcT[:, GROUPS + g, P:2 * P],
                                      state[:, g * 256:(g + 1) * 256], start=True, stop=True), after=[state_ready])
                        yg = y[:, t, g * 256:(g + 1) * 256]
                        xg = x_tok[:, t, g * 256:(g + 1) * 256]

                        def v(a):
                            return a.rearrange("p (r c) -> p r c", r=RPG)
                        s = dve.do(lambda e, xg=xg, yg=yg, g=g: e.tensor_tensor(v(yg), v(xg), bc(d_skip[:, g * RPG:(g + 1) * RPG], HD), MUL),
                                   after=[s] + ya_free)
                        s = dve.do(lambda e, yg=yg, bank=bank: e.tensor_tensor(yg, yg, bank[:, 0:256], ADD))
                        if t == 1:
                            dve.do(lambda e, xg=xg, bank=bank, g=g: e.tensor_tensor(v(xg), v(bank[:, 256:512]),
                                   bc(from_start[:, g * RPG:(g + 1) * RPG], HD), MUL))
                            s = dve.do(lambda e, xg=xg, yg=yg: e.tensor_tensor(yg, yg, xg, ADD))
                        work.done(i, [dve.last])
                    yield
                ss, r8, tmp8 = stat(8), stat(8), stat(8)
                dve.do(lambda e: e.tensor_tensor(R[0][:, :], R[0][:, :], R[2][:, :], MUL))
                s = act.do(lambda e: e.activation(R[3][:, :], R[0][:, :], ACT.Square), after=[dve.last])
                dve.do(lambda e: e.tensor_reduce(ss, R[3][:, :].rearrange("p (g c) -> p g c", g=8), AX, ADD), after=[s])
                rsqrt(r8, ss, 1.0 / 256, tmp8)
                dve.do(lambda e: e.tensor_tensor(R[0][:, :].rearrange("p (g c) -> p g c", g=8), R[0][:, :].rearrange("p (g c) -> p g c", g=8),
                       bc(r8, 256), MUL))
                yield
                yaT = R[5][:, :].rearrange("p (k s) -> p k s", k=KD)
                yT_ready["a"] = transpose_scaled(y, yaT, KD, [dve.last], free, col["ssm_norm"])
                yield

            yT_ready = {}
            kvb = tok(R[7][:, 0:D])
            qb, zb = tok(R[6][:, :]), tok(R[8][:, :])
            together(seq(silu(ZA, D, za, free), plain(QB, D, qb, 0, free, HD ** -0.5), plain(KV, CH, kvb, 0, free), silu(ZB, D, zb, free)), mamba(), 3.5)

            def window():
                q_rot = tok(R[9][:, :])
                k_dup = R[7][:, D:2 * D].rearrange("p (t g u c) -> p t g u c", t=T, g=KVH, u=2)
                base_w = now()
                for t in range(T):
                    tmp = R[10][:, 0:D].rearrange("p (h c) -> p h c", h=HEADS)
                    rope(q_rot[:, t, :].rearrange("p (h c) -> p h c", h=HEADS), qb[:, t, :].rearrange("p (h c) -> p h c", h=HEADS),
                         cosT[:, t, :], sinT[:, t, :], HEADS, tmp, free=base_w)
                    rope(k_dup[:, t, :, 0, :], kvb[:, t, 0:256].rearrange("p (g c) -> p g c", g=KVH), cosT[:, t, :], sinT[:, t, :],
                         KVH, R[10][:, 0:256].rearrange("p (h c) -> p h c", h=KVH))
                    dve.do(lambda e, t=t: e.tensor_copy(k_dup[:, t, :, 1, :], k_dup[:, t, :, 0, :]))
                    yield
                qT = R[6][:, :].rearrange("p (k s) -> p k s", k=KD)
                ready = transpose_scaled(q_rot, qT, KD, [dve.last], [dve.last])
                yield
                kT = R[10][:, 0:D].rearrange("p (g s) -> p g s", g=KVH)
                k_flat = R[7][:, D:2 * D].rearrange("p (t c) -> p t c", t=T)
                ready = transpose_scaled(k_flat, kT, KVH, [dve.last], [dve.last])
                yield
                y_free = [pe.last]

                def scores(h, t, dst, after):
                    keys = (t + 1) * P
                    par = HD * (h % 2)
                    pe.do(lambda e: e.matmul(dst, qT[par:par + HD, h // 2, t * P:(t + 1) * P], kT[par:par + HD, h // KVH, 0:keys],
                          start=True, stop=False), after=after)
                    mask = causal_mask if t == 0 else window_mask
                    return pe.do(lambda e: e.matmul(dst, idbf[:, :], mask, start=False, stop=True), after=[maskbf_made])
                units = [(t, h, 2, 2, scores, (t + 1) * P) for t in range(T) for q in range(0, HEADS, 4) for h in (q, q + 1)]
                yb = tok(R[9][:, :])
                yield from attention(units, HEADS, HD, yb, y_free, lambda h, b: kvb[:, b, 256 + (h // 4) * HD:256 + (h // 4 + 1) * HD],
                                     ready, [R[4][:, 0:CH], R[4][:, CH:2 * CH]], [R[4][:, 2 * CH:3 * CH], R[4][:, 3 * CH:4 * CH]],
                                     sink=sinks, zsilu3=zb)
                ybT = R[8][:, :].rearrange("p (k s) -> p k s", k=KD)
                yT_ready["b"] = transpose_scaled(yb, ybT, KD, [dve.last], [dve.last])
                yield

            free_a = now()
            cq, ck, cv, zc = (tok(R[i][:, :]) for i in range(4))
            together(seq(plain(CF, 16, fr_, 0, []), plain(CQ, D, cq, 0, free_a, HD ** -0.5), plain(CK, D, ck, 0, free_a), plain(CV, D, cv, 0, free_a),
                         silu(CZ, D, zc, free_a)), window(), 2.6)

            def forget():
                free_b = now()
                qT = R[6][:, :].rearrange("p (k s) -> p k s", k=KD)
                kT = R[7][:, :].rearrange("p (k s) -> p k s", k=KD)
                transpose_scaled(cq, qT, KD, [act.last], free_b)
                yield
                ready = transpose_scaled(ck, kT, KD, [act.last], free_b)
                yield
                lf, z, q = (stat(32).rearrange("p (t h) -> p t h", t=T) for _ in range(3))
                dve.do(lambda e: e.tensor_tensor(fr_, fr_, f_bias.unsqueeze(1).to_broadcast([P, T, 16]), ADD), after=[act.last])
                log1p_exp_neg_abs(lf, fr_, z, q)
                dve.do(lambda e: e.scalar_tensor_tensor(lf, fr_, 0.0, lf, MIN, SUB))
                lf_ready = dve.last
                bias_ring = Ring([R[10][:, 3 * i * P:3 * (i + 1) * P] for i in range(4)])
                bias_ring.readers = [free_b for _ in range(4)]

                def scores(h, t, dst, after):
                    keys = (t + 1) * P
                    par = HD * (h % 2)
                    i, bm, readers = bias_ring.take()
                    s = dve.do(lambda e: e.tensor_scalar(bm[:, 0:P], above, lf[:, 0, h:h + 1], None, MUL), after=readers)
                    if t == 1:
                        s = dve.do(lambda e: e.tensor_scalar(bm[:, P:3 * P], ones_gt, lf[:, 1, h:h + 1], None, MUL), after=readers)
                    pe.do(lambda e: e.matmul(dst, qT[par:par + HD, h // 2, t * P:(t + 1) * P], kT[par:par + HD, h // 2, 0:keys],
                          start=True, stop=False), after=after)
                    if t == 0:
                        pe.do(lambda e: e.matmul(dst, upto, bm[:, 0:P], start=False, stop=False), after=[s])
                        last = pe.do(lambda e: e.matmul(dst, idbf[:, :], causal_mask, start=False, stop=True), after=[maskbf_made])
                    else:
                        pe.do(lambda e: e.matmul(dst, upto, bm[:, P:3 * P], start=False, stop=False), after=[s])
                        pe.do(lambda e: e.matmul(dst[:, 0:P], ones, bm[:, 0:P], start=False, stop=False))
                        last = pe.do(lambda e: e.matmul(dst[:, P:2 * P], idbf[:, :], causal_mask, start=False, stop=True), after=[maskbf_made])
                    bias_ring.done(i, [last])
                    return last
                units = [(t, h, 2, 2, scores, (t + 1) * P) for t in range(T) for q in range(0, HEADS, 4) for h in (q, q + 1)]
                y_c = tok(R[9][:, :])
                yield from attention(units, HEADS, HD, y_c, free_b, lambda h, b: cv[:, b, h * HD:(h + 1) * HD],
                                     ready, [R[4][:, 0:CH], R[4][:, CH:2 * CH]], [R[4][:, 2 * CH:3 * CH], R[4][:, 3 * CH:4 * CH]], zsilu3=zc)
                ycT = R[0][:, :].rearrange("p (k s) -> p k s", k=KD)
                yT_ready["c"] = transpose_scaled(y_c, ycT, KD, [dve.last], [dve.last, pe.last])
                yield

            yaT, ybT, ycT = (R[i][:, :].rearrange("p (k s) -> p k s", k=KD) for i in (5, 8, 0))
            gb = d["rows"]
            g0 = ROWS1[l] + 80

            def mix(i, yT, key):
                return gated_add(yT, KD, w_in[:, GATES + i * D:GATES + (i + 1) * D], w_proj[i],
                                 gb[:, g0 + i * D:g0 + (i + 1) * D], i == 0, yT_ready[key])
            together(seq(mix(0, yaT, "a"), mix(1, ybT, "b")), forget(), 2.7)
            for _ in mix(2, ycT, "c"):
                pass
            mT = R[1][:, :].rearrange("p (k s) -> p k s", k=KD)
            out_projection(w_out, mT, now())
            hT_readers[:] = [pe.last]

        COLS1, COLS2 = d["cols_at"][0:2], d["cols_at"][2]
        ROWS1, ROWS2 = d["rows_at"][0:2], d["rows_at"][2]
        for l in range(LAYERS):
            layer(l)

        def second():
            cursor[0] = 0
            col = COLS2
            w_in = d["w_in_2"]
            start = now()
            r0 = ROWS2["small"]
            n_small = 64 * 2 + 128 * 2 + NGRP + EXP
            row_in = sp.load("rows2", [(rows2[:, :], d["rows"][:, r0:r0 + n_small].to_broadcast([P, n_small]))])
            g_q, g_k, g_qm, g_km = rows2[:, 0:64], rows2[:, 64:128], rows2[:, 128:256], rows2[:, 256:384]
            b_grp, b_exp = rows2[:, 384:388], rows2[:, 388:420]
            fw = R[0][:, 0:D]
            fw_in = sp.load("r0", [(fw, d["rows"][:, ROWS2["final"]:ROWS2["final"] + D].to_broadcast([P, D]))], after=start)
            mem3 = tok(R[2][:, :])
            mem_in = sp.load("r2", [(mem3[:, t, :], d["mem"][t * P:(t + 1) * P, :]) for t in range(T)], after=start)
            pos_i, pos_f = R[10][:, 0:T + S].bitcast(I32), rows[:, 0:T + S]
            pos_in = sp.load("pos", [(pos_i[:, 0:T], d["pos_col"]),
                                     (pos_i[:, T:T + S], d["pos"].to_broadcast([P, S]))], after=start)

            r, s = rms_factor(x3, [dve.last])
            for t in range(T):
                dve.do(lambda e, t=t: e.scalar_tensor_tensor(x3[:, t, :], x3[:, t, :], r[:, t:t + 1], fw, MUL, MUL), after=[fw_in])
            x_ready = dve.last

            def plain(c0, n, dst3, dcol, fr, ready, w=None, scale=None):
                src = w_in if w is None else w
                lhs = hT if w is None else mhT
                for o in range(0, n, CH):
                    m = min(CH, n - o)
                    project(lhs, src[:, c0 + o:c0 + o + m], D, m, plain_to(dst3, dcol + o, m, fr, scale), after=ready)
                    yield

            mhT = R[3][:, :].rearrange("p (k s) -> p k s", k=KD)
            normed = tok(R[1][:, :])
            to_hT(mem3, normed, col["g_mem"], after=[mem_in], dst=mhT, dst_free=start)
            mem_ready = [dve.last]
            kmv = tok(R[4][:, :])
            for _ in plain(0, 2 * CH, kmv, 0, start, mem_ready, w=d["w_mem_kv"]):
                pass
            kmv_ready = act.last
            to_hT(x3, normed, col["g_mix"], after=[x_ready, pe.last])
            h_ready = [dve.last]

            def sin_cos(sn, cs, x, n, tmp):
                dve.do(lambda e: e.tensor_scalar(n, x, TURNS, ROUND, MUL, ADD))
                dve.do(lambda e: e.tensor_scalar(n, n, ROUND, None, SUB))
                for part in TWO_PI:
                    dve.do(lambda e, part=part: e.scalar_tensor_tensor(x, n, -part, x, MUL, ADD))
                dve.do(lambda e: e.tensor_scalar(x, x, PI, -PI, MIN, MAX))
                s = act.do(lambda e: e.activation(sn, x, ACT.Sin), after=[dve.last])
                dve.do(lambda e: e.scalar_tensor_tensor(tmp, x, -1.0, x, MUL, MAX))
                dve.do(lambda e: e.tensor_scalar(tmp, tmp, -1.0, HALF_PI, MUL, ADD))
                return act.do(lambda e: e.activation(cs, tmp, ACT.Sin), after=[dve.last])

            dve.do(lambda e: e.tensor_copy(pos_f, pos_i), after=[pos_in])
            ang, sn2, cs2, tmp2, n2 = (stat(64) for _ in range(5))
            inv = consts[:, 1024:1056]
            for t in range(T):
                dve.do(lambda e, t=t: e.tensor_scalar(ang[:, 32 * t:32 * t + 32], inv, pos_f[:, t:t + 1], None, MUL))
            rope_ready = sin_cos(sn2, cs2, ang, n2, tmp2)
            sn3, cs3 = sn2.rearrange("p (t f) -> p t f", t=T), cs2.rearrange("p (t f) -> p t f", t=T)

            lre, lim, ldt = (small_cols[:, col[n]:col[n] + ST] for n in ("lam_re", "lam_im", "log_dt"))
            dt5, rad, th, thn, tht, c5, s5, nr, ni, fr5, fi5, den = (stat(ST) for _ in range(12))
            a = act.do(lambda e: e.activation(dt5, ldt, ACT.Exp), after=[const_in])
            dve.do(lambda e: e.tensor_tensor(rad, lre, dt5, MUL), after=[a])
            dve.do(lambda e: e.tensor_tensor(th, lim, dt5, MUL))
            act.do(lambda e: e.activation(rad, rad, ACT.Exp), after=[dve.last])
            sin_cos(s5, c5, th, thn, tht)
            dve.do(lambda e: e.tensor_tensor(nr, rad, c5, MUL), after=[act.last])
            dve.do(lambda e: e.tensor_scalar(nr, nr, -1.0, None, ADD))
            dve.do(lambda e: e.tensor_tensor(ni, rad, s5, MUL))
            dve.do(lambda e: e.tensor_tensor(den, lre, lre, MUL))
            dve.do(lambda e: e.tensor_tensor(tht, lim, lim, MUL))
            dve.do(lambda e: e.tensor_tensor(den, den, tht, ADD))
            dve.do(lambda e: e.reciprocal(den, den))
            for dst, a1, a2, op in ((fr5, nr, ni, ADD), (fi5, ni, nr, SUB)):
                dve.do(lambda e, dst=dst, a1=a1: e.tensor_tensor(dst, a1, lre, MUL))
                dve.do(lambda e, a2=a2: e.tensor_tensor(tht, a2, lim, MUL))
                dve.do(lambda e, dst=dst, op=op: e.tensor_tensor(dst, dst, tht, op))
                dve.do(lambda e, dst=dst: e.tensor_tensor(dst, dst, den, MUL))
            wc, ws = [c5], [s5]
            for j in range(7):
                c_, s_, q_ = stat(ST), stat(ST), tht
                pc, ps_ = wc[-1], ws[-1]
                dve.do(lambda e, c_=c_, pc=pc: e.tensor_tensor(c_, pc, pc, MUL))
                dve.do(lambda e, ps_=ps_: e.tensor_tensor(q_, ps_, ps_, MUL))
                dve.do(lambda e, c_=c_: e.tensor_tensor(c_, c_, q_, SUB))
                dve.do(lambda e, s_=s_, pc=pc, ps_=ps_: e.scalar_tensor_tensor(s_, pc, 2.0, ps_, MUL, MUL))
                wc.append(c_)
                ws.append(s_)

            u3, q3 = tok(R[5][:, 0:D]), tok(R[5][:, D:2 * D])
            kvi, qm3 = tok(R[6][:, 0:D]), tok(R[6][:, D:2 * D])
            for _ in plain(Q2, CH, q3, 0, start, h_ready):
                pass
            for _ in plain(KVI2, QM2 - KVI2, kvi, 0, start, h_ready):
                pass

            def head_norm(x_4, heads, c, gain, junk, after=()):
                ss, r, tmp = stat(heads), stat(heads), stat(heads)
                dve.do(lambda e: e.tensor_tensor(junk, x_4, x_4, MUL), after=after)
                dve.do(lambda e: e.tensor_reduce(ss, junk, AX, ADD))
                rsqrt(r, ss, 1.0 / c, tmp)
                dve.do(lambda e: e.tensor_tensor(x_4, x_4, bc(r, c), MUL))
                return dve.do(lambda e: e.tensor_tensor(x_4, x_4, gain.unsqueeze(1).to_broadcast([P, heads, c]), MUL))

            def sparse():
                dve.do(lambda e: e.tensor_scalar(g_q, g_q, HD ** -0.5, None, MUL), after=[row_in, act.last])
                rot = tok(R[7][:, :])
                tmp = R[8][:, 0:CH].rearrange("p (h c) -> p h c", h=8)

                def hv(a, h):
                    return a.rearrange("p (h c) -> p h c", h=h)
                for t in range(T):
                    qh, kh = hv(q3[:, t, :], 8), hv(kvi[:, t, 0:64], 1)
                    head_norm(qh, 8, HD, g_q, tmp, after=start)
                    head_norm(kh, 1, HD, g_k, tmp[:, 0:1, :])
                    cs, sn = cs3[:, t, :], sn3[:, t, :]
                    rope(hv(rot[:, t, 0:512], 8), qh, cs, sn, 8, tmp, free=[rope_ready])
                    rope(hv(rot[:, t, 512:576], 1), kh, cs, sn, 1, tmp[:, 0:1, :])
                    dve.do(lambda e, t=t: e.tensor_copy(rot[:, t, 576:640], rot[:, t, 512:576]))
                    rope(hv(rot[:, t, 640:896], 4), hv(kvi[:, t, 128:384], 4), cs, sn, 4, tmp[:, 0:4, :])
                    rope(hv(rot[:, t, 896:960], 1), hv(kvi[:, t, 384:448], 1), cs, sn, 1, tmp[:, 0:1, :])
                    dve.do(lambda e, t=t: e.tensor_copy(rot[:, t, 960:1024], rot[:, t, 896:960]))
                    yield
                aT = R[8][:, :].rearrange("p (k s) -> p k s", k=KD)
                ready = transpose_scaled(rot, aT, KD, [dve.last], [dve.last])
                yield
                def select(t):
                    pq = pos_f[:, t:t + 1]
                    isc, valid, tmp_i = R[7][:, 0:S], R[7][:, S:2 * S], R[7][:, 2 * S:3 * S]
                    wi = stat(4)
                    top = stat(8)
                    dve.do(lambda e, t=t: e.tensor_scalar(wi, kvi[:, t, 448:452], 4 ** -0.5 * HD ** -0.5, None, MUL), after=[pe.last])
                    n = 0
                    for par in range(2):
                        i, bank, readers = work.take()
                        for j in range(2):
                            s = pe.do(lambda e, par=par, j=j, bank=bank, t=t: e.matmul(bank[:, j * S:(j + 1) * S],
                                      aT[64 * par:64 * par + 64, 5 + j, t * P:(t + 1) * P], aT[64 * par:64 * par + 64, 7, :],
                                      start=True, stop=True), after=ready + readers)
                        for j in range(2):
                            h = 2 * j + par
                            dst = isc if n == 0 else tmp_i
                            dve.do(lambda e, dst=dst, j=j, h=h, bank=bank, wi=wi: e.tensor_scalar(dst, bank[:, j * S:(j + 1) * S], 0.0,
                                   wi[:, h:h + 1], MAX, MUL), after=[s])
                            if n:
                                dve.do(lambda e: e.tensor_tensor(isc, isc, tmp_i, ADD))
                            n += 1
                        work.done(i, [dve.last])
                    dve.do(lambda e, pq=pq: e.tensor_scalar(valid, pos_f[:, T:T + S], pq, None, ALU.is_le))
                    dve.do(lambda e: e.tensor_scalar(tmp_i, valid, -1.0, LATER, ADD, MUL))
                    dve.do(lambda e: e.tensor_tensor(isc, isc, valid, MUL))
                    dve.do(lambda e: e.tensor_tensor(isc, isc, tmp_i, ADD))
                    for _ in range(TOPK // 8):
                        dve.do(lambda e, top=top: e.max(top, isc))
                        dve.do(lambda e, top=top: e.match_replace(isc, top, isc, STRUCK))
                    dve.do(lambda e: e.tensor_scalar(isc, isc, STRUCK, None, ALU.is_equal))
                    dve.do(lambda e: e.tensor_tensor(isc, isc, valid, MUL))
                    dve.do(lambda e, t=t: e.tensor_scalar(selmask[:, t * S:(t + 1) * S], isc, -1.0, -NEG, ADD, MUL))
                    yield
                for t in range(T):
                    yield from select(t)
                sel_ready = dve.last

                def scores(h, t, dst, after):
                    par = 64 * (h % 2)
                    pe.do(lambda e: e.matmul(dst, aT[par:par + 64, h // 2, t * P:(t + 1) * P], aT[par:par + 64, 4, :], start=True, stop=False), after=after)
                    return pe.do(lambda e: e.matmul(dst, idbf[:, :], selmask[:, t * S:(t + 1) * S], start=False, stop=True), after=[sel_ready])
                units = [(t, h, 2, 2, scores, S) for t in range(T) for q in range(0, 8, 4) for h in (q, q + 1)]
                yield from attention(units, 8, HD, y_dsa, [], lambda h, b: kvi[:, b, 64:128], ready + [sel_ready],
                                     [R[9][:, 0:CH], R[9][:, CH:2 * CH]], [R[9][:, 2 * CH:3 * CH], R[9][:, 3 * CH:4 * CH]])
                yT_ready2["dsa"] = transpose_scaled(y_dsa, ydT, 4, [dve.last], start)
                yield

            yT_ready2 = {}
            y_dsa, ydT = tok(R[10][:, 0:D]), R[10][:, D:2 * D].rearrange("p (k s) -> p k s", k=4)
            together(itertools.chain(plain(U2, CH, u3, 0, start, h_ready), plain(QM2, CH, qm3, 0, start, h_ready)), sparse(), 1.0)

            def memory():
                y_m, ymT = tok(R[7][:, 0:D]), R[7][:, D:2 * D].rearrange("p (k s) -> p k s", k=4)
                free = now()
                dve.do(lambda e: e.tensor_scalar(g_qm, g_qm, 128 ** -0.5, None, MUL), after=[act.last, kmv_ready])
                for t in range(T):
                    jv = R[8][:, 0:CH].rearrange("p (h c) -> p h c", h=4)
                    head_norm(qm3[:, t, :].rearrange("p (h c) -> p h c", h=4), 4, 128, g_qm, jv, after=free)
                    head_norm(kmv[:, t, 0:CH].rearrange("p (h c) -> p h c", h=4), 4, 128, g_km, jv)
                    yield
                qT = R[8][:, 0:D].rearrange("p (h s) -> p h s", h=4)
                kT = R[8][:, D:2 * D].rearrange("p (h s) -> p h s", h=4)
                transpose_scaled(qm3, qT, 4, [dve.last], [dve.last])
                ready = transpose_scaled(kmv[:, :, 0:CH], kT, 4, [dve.last], [])
                yield

                def scores(h, t, dst, after):
                    return pe.do(lambda e: e.matmul(dst, qT[:, h, t * P:(t + 1) * P], kT[:, h, :], start=True, stop=True), after=after)
                units = [(t, h, 2, 1, scores, S) for t in range(T) for h in range(0, 4, 2)]
                yield from attention(units, 4, 128, y_m, [], lambda h, b: kmv[:, b, CH + h * 128:CH + (h + 1) * 128], ready,
                                     [R[9][:, 0:CH], R[9][:, CH:2 * CH]], [R[9][:, 2 * CH:3 * CH], R[9][:, 3 * CH:4 * CH]])
                yT_ready2["mem"] = transpose_scaled(y_m, ymT, 4, [dve.last], [])
                yield

            def ssm():
                free = now()
                uT = R[4][:, 0:D].rearrange("p (k s) -> p k s", k=4)
                ysT = R[4][:, D:2 * D].rearrange("p (k s) -> p k s", k=4)
                u_ready = transpose_scaled(u3, uT, 4, [act.last], free)
                yield
                for half in range(2):
                    ec = R[half][:, :].rearrange("p (i s) -> p i s", i=8)
                    es = R[2 + half][:, :].rearrange("p (i s) -> p i s", i=8)
                    tm = R[9][:, 0:D].rearrange("p (i s) -> p i s", i=8)
                    dve.do(lambda e, ec=ec: e.memset(ec[:, :, 0:1], 1.0), after=free)
                    dve.do(lambda e, es=es: e.memset(es[:, :, 0:1], 0.0))
                    for j in range(8):
                        m = 1 << j
                        c_, s_ = (bc(w[j][:, 8 * half:8 * half + 8], m) for w in (wc, ws))
                        a_c, a_s, o_c, o_s, tt = ec[:, :, 0:m], es[:, :, 0:m], ec[:, :, m:2 * m], es[:, :, m:2 * m], tm[:, :, 0:m]
                        for o, x1, x2, y1, y2, op in ((o_c, a_c, c_, a_s, s_, SUB), (o_s, a_c, s_, a_s, c_, ADD)):
                            dve.do(lambda e, o=o, x1=x1, x2=x2: e.tensor_tensor(o, x1, x2, MUL))
                            dve.do(lambda e, tt=tt, y1=y1, y2=y2: e.tensor_tensor(tt, y1, y2, MUL))
                            dve.do(lambda e, o=o, tt=tt, op=op: e.tensor_tensor(o, o, tt, op))
                        if j % 4 == 3:
                            yield
                def quarter(k):
                    bcol, ccol = R[9][:, 0:2 * CH], R[9][:, 2 * CH:4 * CH]
                    bcm = [bcol[:, j * CH:(j + 1) * CH].rearrange("p (i c) -> p i c", i=4) for j in range(2)]
                    ccm = [ccol[:, j * CH:(j + 1) * CH].rearrange("p (i c) -> p i c", i=4) for j in range(2)]
                    loaded = sp.load("r9", [(v, d[n][:, 4 * k:4 * k + 4, :]) for v, n in zip(bcm + ccm, ("b_re", "b_im", "c_re", "c_im"))], after=now())
                    half, i0 = k // 2, 4 * (k % 2)
                    ec = R[half][:, :].rearrange("p (i s) -> p i s", i=8)[:, i0:i0 + 4, :]
                    es = R[2 + half][:, :].rearrange("p (i s) -> p i s", i=8)[:, i0:i0 + 4, :]
                    q4 = [R[5][:, 0:D], R[5][:, D:2 * D], R[6][:, 0:D], R[6][:, D:2 * D]]
                    vre, vim, gre, gim = (a.rearrange("p (i s) -> p i s", i=4) for a in q4)
                    tmp = R[8][:, 0:D].rearrange("p (i s) -> p i s", i=4)
                    tmc = R[8][:, D:2 * D].rearrange("p (a i c) -> p a i c", a=2, i=4)
                    free_q = now()
                    for j2 in range(2):
                        got = []
                        for w in range(2):
                            i, bank, readers = work.take()
                            for j in range(2):
                                s = pe.do(lambda e, w=w, j=j, j2=j2, bank=bank, k=k: e.matmul(bank[:, j * S:(j + 1) * S], bcm[w][:, 2 * j2 + j, :], uT[:, k, :],
                                          start=True, stop=True), after=[loaded] + u_ready + readers)
                            got.append((i, bank, s))
                        bre, bim = (g[1][:, :].rearrange("p (i s) -> p i s", i=2) for g in got)
                        sl = slice(2 * j2, 2 * j2 + 2)
                        for o, x1, y1, op in ((vre, bre, bim, ADD), (vim, bim, bre, SUB)):
                            dve.do(lambda e, o=o, x1=x1, sl=sl: e.tensor_tensor(o[:, sl, :], x1, ec[:, sl, :], MUL), after=[got[0][2], got[1][2]] + free_q)
                            dve.do(lambda e, y1=y1, sl=sl: e.tensor_tensor(tmp[:, sl, :], y1, es[:, sl, :], MUL))
                            dve.do(lambda e, o=o, sl=sl, op=op: e.tensor_tensor(o[:, sl, :], o[:, sl, :], tmp[:, sl, :], op))
                        for i, _, _ in got:
                            work.done(i, [dve.last])
                    yield
                    for v, g in ((vre, gre), (vim, gim)):
                        for i in range(4):
                            dve.do(lambda e, v=v, g=g, i=i: e.tensor_tensor_scan(g[:, i, :], rad[:, 4 * k + i:4 * k + i + 1].to_broadcast([P, S]),
                                   v[:, i, :], 0.0, MUL, ADD))
                    for o, x1, y1, op in ((vre, gre, gim, SUB), (vim, gim, gre, ADD)):
                        dve.do(lambda e, o=o, x1=x1: e.tensor_tensor(o, x1, ec, MUL))
                        dve.do(lambda e, y1=y1: e.tensor_tensor(tmp, y1, es, MUL))
                        dve.do(lambda e, o=o, op=op: e.tensor_tensor(o, o, tmp, op))
                    f_r, f_i = (bc(a[:, 4 * k:4 * k + 4], P) for a in (fr5, fi5))
                    dve.do(lambda e: e.tensor_tensor(tmc[:, 0, :, :], ccm[0], f_i, MUL), after=[loaded])
                    dve.do(lambda e: e.tensor_tensor(tmc[:, 1, :, :], ccm[1], f_i, MUL))
                    dve.do(lambda e: e.tensor_tensor(ccm[0], ccm[0], f_r, MUL))
                    dve.do(lambda e: e.tensor_tensor(ccm[1], ccm[1], f_r, MUL))
                    dve.do(lambda e: e.tensor_tensor(ccm[0], ccm[0], tmc[:, 1, :, :], SUB))
                    dve.do(lambda e: e.scalar_tensor_tensor(ccm[1], ccm[1], -1.0, tmc[:, 0, :, :], MUL, SUB))
                    i, bank, readers = work.take()
                    for j in range(4):
                        for w, h in enumerate((vre, vim)):
                            s = pe.do(lambda e, j=j, w=w, h=h, bank=bank: e.matmul(bank[:, 0:S], ccm[w][:, j, :], h[:, j, :],
                                      start=(j == 0 and w == 0), stop=(j == 3 and w == 1)), after=[dve.last] + readers)
                    dcol = small_cols[:, col["d_skip"] + k:col["d_skip"] + k + 1]
                    s = dve.do(lambda e, k=k, bank=bank, dcol=dcol: e.scalar_tensor_tensor(ysT[:, k, :], uT[:, k, :], dcol, bank[:, 0:S], MUL, ADD), after=[s])
                    work.done(i, [s])
                    yield
                for k in range(4):
                    yield from quarter(k)
                yf, g1 = R[4][:, D:2 * D], R[8][:, 0:D]
                dve.do(lambda e: e.tensor_tensor(g1, yf, yf, MUL))
                dve.do(lambda e: e.tensor_scalar(g1, g1, 0.044715, 1.0, MUL, ADD))
                dve.do(lambda e: e.tensor_tensor(g1, g1, yf, MUL))
                a = act.do(lambda e: e.activation(g1, g1, ACT.Exp, scale=-2.0 * (2.0 / np.pi) ** 0.5), after=[dve.last])
                recip_1p(g1, after=[a])
                dve.do(lambda e: e.tensor_tensor(yf, yf, g1, MUL))
                y_ok = dve.last
                si, slot, w, loaded = chunk_load(d["w_glu"], CH, CH)
                for k in range(0, 4, 2):
                    i, bank, readers = work.take()
                    for j in range(2):
                        for kk in range(4):
                            s = pe.do(lambda e, j=j, k=k, kk=kk, bank=bank: e.matmul(bank[:, j * S:(j + 1) * S], w[:, kk, (k + j) * P:(k + j + 1) * P], ysT[:, kk, :],
                                      start=(kk == 0), stop=(kk == 3)), after=[y_ok, loaded] + readers)
                    a = act.do(lambda e, k=k, bank=bank: e.activation(g1[:, k * S:(k + 2) * S], bank[:, :], ACT.Exp, scale=-1.0), after=[s])
                    work.done(i, [a])
                wring.done(si, [s])
                recip_1p(g1, after=[a])
                yT_ready2["ssm"] = [dve.do(lambda e: e.tensor_tensor(yf, yf, g1, MUL), after=[s])]
                yield

            ymT = R[7][:, D:2 * D].rearrange("p (k s) -> p k s", k=4)
            ysT = R[4][:, D:2 * D].rearrange("p (k s) -> p k s", k=4)

            def mix(i, yT, key, w):
                return gated_add(yT, 4, w_in[:, GATES2 + i * D:GATES2 + (i + 1) * D], d[w], None, i == 1, yT_ready2[key])

            def later(*makers):
                for m in makers:
                    yield from m()
            merged_readers[:] = [pe.last]
            together(mix(1, ydT, "dsa", "w_up_dsa"), memory(), 3.0)
            together(mix(2, ymT, "mem", "w_up_mem"), ssm(), 4.0)
            for _ in mix(0, ysT, "ssm", "w_up_ssm"):
                pass
            mT = R[1][:, :].rearrange("p (k s) -> p k s", k=KD)
            out_projection(d["w_out_2"], mT, now())
            hT_readers[:] = [pe.last]

            to_hT(x3, tok(R[0][:, :]), col["g_ffn"], after=[dve.last])
            h_ready = [dve.last]
            i, slot, readers = wring.take()
            n_r = NGRP + EXP
            wr = slot[:, 0:KD * n_r].rearrange("p (k n) -> p k n", k=KD)
            loaded = sp.load(f"w{i}", [(wr[:, :, 0:NGRP], d["w_group"].rearrange("(k p) n -> p k n", p=P)),
                                       (wr[:, :, NGRP:n_r], d["w_expert"].rearrange("(k p) n -> p k n", p=P))], after=readers)
            lg, le = stat(T * NGRP), stat(T * EXP)
            lg3, le3 = lg.rearrange("p (t g) -> p t g", t=T), le.rearrange("p (t g) -> p t g", t=T)
            b_i, bank, readers = work.take()
            for t in range(T):
                for k in range(KD):
                    s = pe.do(lambda e, t=t, k=k: e.matmul(bank[:, t * n_r:(t + 1) * n_r], hT[:, k, t * P:(t + 1) * P], wr[:, k, :],
                              start=(k == 0), stop=(k == KD - 1)), after=[loaded] + h_ready + readers)
            wring.done(i, [s])
            lv = bank[:, 0:T * n_r].rearrange("p (t n) -> p t n", t=T)
            dve.do(lambda e: e.tensor_tensor(lg3, lv[:, :, 0:NGRP], b_grp.unsqueeze(1).to_broadcast([P, T, NGRP]), ADD), after=[s])
            s = dve.do(lambda e: e.tensor_tensor(le3, lv[:, :, NGRP:n_r], b_exp.unsqueeze(1).to_broadcast([P, T, EXP]), ADD))
            work.done(b_i, [s])

            def softmax(x, n, m):
                v = x.rearrange("p (a b) -> p a b", b=m)
                red = stat(n)
                dve.do(lambda e: e.tensor_reduce(red, v, AX, MAX))
                dve.do(lambda e: e.tensor_tensor(v, v, bc(red, m), SUB))
                a = act.do(lambda e: e.activation(x, x, ACT.Exp), after=[dve.last])
                dve.do(lambda e: e.tensor_reduce(red, v, AX, ADD), after=[a])
                dve.do(lambda e: e.reciprocal(red, red))
                dve.do(lambda e: e.tensor_tensor(v, v, bc(red, m), MUL))
            softmax(lg, T, NGRP)
            softmax(le, T * NGRP, EPG)

            def first_of_highest(x3_, m, top, hot):
                order = consts[:, 1056:1056 + m].unsqueeze(1).to_broadcast([P, T, m])
                key = stat(T)
                dve.do(lambda e: e.tensor_reduce(top, x3_, AX, MAX))
                dve.do(lambda e: e.tensor_tensor(hot, x3_, bc(top, m), ALU.is_equal))
                dve.do(lambda e: e.tensor_tensor(hot, hot, order, MUL))
                dve.do(lambda e: e.tensor_reduce(key, hot, AX, MAX))
                dve.do(lambda e: e.tensor_tensor(hot, hot, bc(key, m), ALU.is_equal))
            g_gate, g_hot = stat(T), stat(T * NGRP)
            g_hot3 = g_hot.rearrange("p (t g) -> p t g", t=T)
            first_of_highest(lg3, NGRP, g_gate, g_hot3)
            pr, ep = stat(T * EXP), stat(T * EPG)
            le4 = le.rearrange("p (a b) -> p a b", b=EPG)
            dve.do(lambda e: e.tensor_tensor(pr.rearrange("p (a b) -> p a b", b=EPG), le4, bc(g_hot, EPG), MUL))
            ep3 = ep.rearrange("p (t b) -> p t b", t=T)
            pr4 = pr.rearrange("p (t g b) -> p t g b", t=T, g=NGRP)
            dve.do(lambda e: e.tensor_tensor(ep3, pr4[:, :, 0, :], pr4[:, :, 1, :], ADD))
            for g in (2, 3):
                dve.do(lambda e, g=g: e.tensor_tensor(ep3, ep3, pr4[:, :, g, :], ADD))
            top1, top2, hot1, hot2, tot = stat(T), stat(T), stat(T * EPG), stat(T * EPG), stat(T)
            h1, h2 = (a.rearrange("p (t b) -> p t b", t=T) for a in (hot1, hot2))
            first_of_highest(ep3, EPG, top1, h1)
            dve.do(lambda e: e.scalar_tensor_tensor(ep, hot1, -2.0, ep, MUL, ADD))
            first_of_highest(ep3, EPG, top2, h2)
            dve.do(lambda e: e.tensor_tensor(tot, top1, top2, ADD))
            dve.do(lambda e: e.reciprocal(tot, tot))
            dve.do(lambda e: e.tensor_tensor(tot, tot, g_gate, MUL))
            dve.do(lambda e: e.tensor_tensor(top1, top1, tot, MUL))
            dve.do(lambda e: e.tensor_tensor(top2, top2, tot, MUL))
            dve.do(lambda e: e.tensor_tensor(h1, h1, bc(top1, EPG), MUL))
            dve.do(lambda e: e.tensor_tensor(h2, h2, bc(top2, EPG), MUL))
            dve.do(lambda e: e.tensor_tensor(h1, h1, h2, ADD))
            comb = pr
            comb4 = pr4
            for t in range(T):
                for g in range(NGRP):
                    dve.do(lambda e, t=t, g=g: e.tensor_scalar(comb4[:, t, g, :], h1[:, t, :], g_hot3[:, t, g:g + 1], None, MUL))
            comb3 = comb.rearrange("p (t e) -> p t e", t=T)

            free = now()
            hid_ring = Ring([R[2][:, 0:D], R[2][:, D:2 * D]])
            hid_ring.readers = [free, free]

            def up(x):
                hi, hid, hreaders = hid_ring.take()
                hid3 = hid.rearrange("p (j s) -> p j s", j=4)
                for w_name in ("w_gate", "w_up"):
                    i, slot, w, loaded = chunk_load(d[w_name][x], D, FF)
                    for jj in range(2):
                        b, bank, readers = bulk.take()
                        for j in range(2):
                            for k in range(KD):
                                s = pe.do(lambda e, j=j, jj=jj, k=k, bank=bank, w=w: e.matmul(bank[:, j * S:(j + 1) * S],
                                          w[:, k, (2 * jj + j) * P:(2 * jj + j + 1) * P], hT[:, k, :], start=(k == 0), stop=(k == KD - 1)),
                                          after=[loaded] + readers + h_ready)
                        part = hid[:, jj * CH:(jj + 1) * CH]
                        if w_name == "w_gate":
                            a = act.do(lambda e, part=part, bank=bank: e.activation(part, bank[:, :], ACT.Silu), after=[s] + hreaders)
                        else:
                            a = dve.do(lambda e, part=part, bank=bank: e.tensor_tensor(part, part, bank[:, :], MUL), after=[s, act.last])
                        bulk.done(b, [a])
                    wring.done(i, [s])
                return hi, hid3, a

            def down(x, hi, hid3, ready):
                i, slot, readers = wring.take()
                w = slot[:, 0:4 * D].rearrange("p (j n) -> p j n", j=4)
                loaded = sp.load(f"w{i}", [(w, d["w_down"][x].rearrange("(j p) n -> p j n", p=P))], after=readers)
                for t in range(T):
                    for n0 in range(0, D, CH):
                        b, bank, readers = work.take()
                        for j in range(4):
                            s = pe.do(lambda e, t=t, j=j, n0=n0, bank=bank: e.matmul(bank[:, :], hid3[:, j, t * P:(t + 1) * P], w[:, j, n0:n0 + CH],
                                      start=(j == 0), stop=(j == 3)), after=[loaded, ready] + readers)
                        dst, cw = m3[:, t, n0:n0 + CH], comb3[:, t, x:x + 1]
                        if x == 0:
                            a = dve.do(lambda e, dst=dst, cw=cw, bank=bank: e.tensor_scalar(dst, bank[:, :], cw, None, MUL), after=[s] + free)
                        else:
                            a = dve.do(lambda e, dst=dst, cw=cw, bank=bank: e.scalar_tensor_tensor(dst, bank[:, :], cw, dst, MUL, ADD), after=[s])
                        work.done(b, [a])
                wring.done(i, [s])
                hid_ring.done(hi, [s])
            pending = None
            for x in range(EXP):
                got = up(x)
                if pending is not None:
                    down(x - 1, *pending)
                pending = got
            down(EXP - 1, *pending)
            stores = []
            for t in range(T):
                s = dve.do(lambda e, t=t: e.tensor_tensor(x3[:, t, :], x3[:, t, :], m3[:, t, :], ADD))
                stores.append((out[t * P:(t + 1) * P, :], x3[:, t, :]))
            return sp.load("out", stores, after=[s])

        if STAGE >= 2:
            rows2 = sb("rows2", 64 * 2 + 128 * 2 + NGRP + EXP)
            selmask = sb("selected_mask", T * S, BF16)
            final = second()
        else:
            final = sp.load("out", [(out[t * P:(t + 1) * P, :], x3[:, t, :]) for t in range(T)], after=now())
        for lane in (pe, dve, act, pool):
            lane.count()
        block = ctx.enter_context(nc.Block())

        @block.sync
        def _(e):
            sp.emit(e)
            e.wait_ge(final.sem, final.value)

        @block.tensor
        def _(e):
            pe.emit(e)

        @block.vector
        def _(e):
            dve.emit(e)

        @block.scalar
        def _(e):
            act.emit(e)

        @block.gpsimd
        def _(e):
            pool.emit(e)


STAGE = 2


def shape_constants():
    i = np.arange(P)
    c = np.zeros((P, 1408), np.float32)
    c[:, 0:128] = np.eye(P)
    c[:, 128:256] = i[:, None] <= i[None, :]
    c[:, 256:384] = 1.0
    c[:, 384:512] = i[:, None] > i[None, :]
    c[:, 512:640] = np.where(i[:, None] >= i[None, :], 0.0, NEG)
    c[:, 640:768] = np.where(i[None, :] > i[:, None], 0.0, NEG)
    c[:, 768:896] = np.where(i[:, None] >= i[None, :], 0.0, NEG)
    pos = np.arange(S, dtype=np.float32)
    inv = (np.float32(10000.0) ** (-np.arange(0, HD, 2, dtype=np.float32) / np.float32(HD))).astype(np.float32)
    ang = pos[:, None] * inv[None, :]
    for t in range(T):
        c[:, 896 + 32 * t:928 + 32 * t] = np.cos(ang[t * P:(t + 1) * P])
        c[:, 960 + 32 * t:992 + 32 * t] = np.sin(ang[t * P:(t + 1) * P])
    c[:, 1024:1056] = 1.0 / (np.float32(10000.0) ** (np.arange(0, HD, 2, dtype=np.float32) / np.float32(HD)))
    c[:, 1056:1064] = np.arange(8, 0, -1)
    return c


def kernel(**inputs):
    import concourse.bacc as bacc
    from concourse.bass_utils import run_bass_kernel_spmd as run

    nc = bacc.Bacc("TRN2", target_bir_lowering=False, num_devices=1)
    a = {k: np.asarray(v) for k, v in inputs.items()}
    cols, at = [], []

    def add(v):
        c0 = sum(x.shape[1] for x in cols)
        cols.append(v.reshape(-1, P).T)
        return c0
    for l in range(LAYERS):
        e = {"norm": add(a["norm_w"][l])}
        e["conv"] = [add(a["conv_w"][l][w]) for w in range(CONV_W)][0]
        e["conv_b"], e["ssm_norm"] = add(a["conv_b"][l]), add(a["ssm_norm_w"][l])
        at.append(e)
    e = {n: add(a[n + "_2"][0]) for n in ("g_mem", "g_mix", "g_ffn", "lam_re", "lam_im", "d_skip")}
    e["log_dt"] = add(np.repeat(a["log_dt_2"][0], SN))
    at.append(e)
    rows, rat = [], []

    def addr(v):
        r0 = sum(len(x) for x in rows)
        rows.append(v.reshape(-1))
        return r0
    for l in range(LAYERS):
        rat.append(addr(a["dt_bias"][l]))
        for n in ("a_log", "d_skip", "sinks", "f_bias", "gate_bias"):
            addr(a[n][l])
    e = {"final": addr(a["final_norm_w"]), "small": addr(a["g_q_2"][0])}
    for n in ("g_k_2", "g_qm_2", "g_km_2", "b_group_2", "b_expert_2"):
        addr(a[n][0])
    rat.append(e)
    b_pad, c_pad = {}, {}
    for part in ("re", "im"):
        b, c = a["b_" + part + "_2"][0], a["c_" + part + "_2"][0]
        bp, cp = np.zeros((P, ST, P), np.float32), np.zeros((P, ST, P), np.float32)
        for g in range(SG):
            i, g2 = divmod(g, 2)
            ch, st = 32 * (i % 4) + SH * g2, SN * g2
            bp[ch:ch + SH, i, st:st + SN] = b[g].T
            cp[st:st + SN, i, ch:ch + SH] = c[g].T
        b_pad[part], c_pad[part] = bp, cp
    arrays = {"x": a["x"][0], "w_in": a["w_in"], "w_proj": a["w_proj"], "w_out": a["w_out"],
              "consts": shape_constants(), "cols": np.concatenate(cols, 1), "rows": np.concatenate(rows)[None, :],
              "b_re": b_pad["re"], "b_im": b_pad["im"], "c_re": c_pad["re"], "c_im": c_pad["im"],
              "mem": a["mem_2"][0], "pos": a["positions_2"],
              "pos_col": a["positions_2"].reshape(T, P).T}
    for n in ("w_in", "w_out"):
        arrays[n + "_2"] = a[n + "_2"][0]
    for n in ("w_mem_kv", "w_glu", "w_up_ssm", "w_up_dsa", "w_up_mem", "w_group", "w_expert", "w_gate", "w_up", "w_down"):
        arrays[n] = a[n + "_2"][0]
    feed, d = {}, {}
    for n, v in arrays.items():
        v = np.ascontiguousarray(v)
        feed["in_" + n] = v
        d[n] = nc.dram_tensor("in_" + n, v.shape, mybir.dt.from_np(v.dtype), kind="ExternalInput").ap()
    d["cols_at"], d["rows_at"] = at, rat
    out = nc.dram_tensor("out_x", (S, D), F32, kind="ExternalOutput").ap()
    build(nc, d, out)
    r = run(nc, [feed], core_ids=[0])
    return r.results[0]["out_x"].reshape(1, S, D)
```

```python
from contextlib import ExitStack

import itertools

import numpy as np

import concourse.bass as bass
from concourse import mybir

F32 = mybir.dt.float32
F32R = mybir.dt.float32r
BF16 = mybir.dt.bfloat16
I32 = mybir.dt.int32
ALU = mybir.AluOpType
ACT = mybir.ActivationFunctionType
AX = mybir.AxisListType.X
ADD, SUB, MUL, MAX, MIN = ALU.add, ALU.subtract, ALU.mult, ALU.max, ALU.min

P = 128
D = 1024
S = 256
T = S // P
KD = D // P
TURNS = 0.15915494309189535
ROUND = 12582912.0
PI, HALF_PI = 3.1415925, 1.5707963267948966
TWO_PI = (6.28125, 0.0019350051879882812, 3.019916050561733e-07)
LATER, STRUCK = 1e37, -1e38
LAYERS = 2
AHEAD = 3
PK = 2
CH = 512
EPS = 1e-6
NEG = -1e30

XBC, ZA, DT, KV, ZB = 0, 2048, 3072, 4112, 4624
QB, CQ, CK, CV, CF, CZ, GATES = 3088, 5648, 6672, 7696, 8720, 8736, 9760
N_IN = GATES + 3 * D
HEADS, HD = 16, 64
KVH = 4
GROUPS, RPG = 4, 4
CONV_W = 4

U2, Q2, KVI2, QM2, GATES2 = 0, 512, 1024, 1476, 1988
N_IN2 = GATES2 + 3 * D
SG, SH, SN = 32, 16, 64
ST = SG * SN // P
TOPK = min(256, S // 4)
EXP, FF = 32, 512
NGRP, EPG = 4, 8


class Step:

    def __init__(self, sem, value=None):
        self.sem, self.value, self.needed = sem, value, False


class Lane:

    def __init__(self, sem, chained):
        self.sem, self.chained, self.queue, self.last = sem, chained, [], None

    def do(self, emit, after=()):
        after = [s for s in after if s is not None]
        if self.chained and self.last is not None:
            after.append(self.last)
        step = Step(self.sem)
        for s in after:
            s.needed = True
        self.queue.append((emit, after, step))
        self.last = step
        return step

    def count(self):
        n = 0
        for _, _, step in self.queue:
            if step.needed and step.value is None:
                n += 1
                step.value = n

    def emit(self, engine):
        seen = {}
        for emit, after, step in self.queue:
            for s in after:
                if seen.get(s.sem.name, 0) < s.value:
                    engine.wait_ge(s.sem, s.value)
                    seen[s.sem.name] = s.value
            made = emit(engine)
            if step.needed and step.sem is self.sem:
                made.then_inc(self.sem, 1)


class Loads:

    def __init__(self, new_sem):
        self.new_sem, self.queue, self.sems = new_sem, [], {}

    def load(self, name, pairs, after=()):
        if name not in self.sems:
            self.sems[name] = [self.new_sem("dma_" + name), 0]
        entry = self.sems[name]
        after = [s for s in after if s is not None]
        for s in after:
            s.needed = True
        for out, src in pairs:
            entry[1] += 16
            self.queue.append((out, src, after, entry[0]))
        return Step(entry[0], entry[1])

    def emit(self, engine):
        seen = {}
        for out, src, after, sem in self.queue:
            for s in after:
                if seen.get(s.sem.name, 0) < s.value:
                    engine.wait_ge(s.sem, s.value)
                    seen[s.sem.name] = s.value
            engine.dma_start(out, src).then_inc(sem, 16)


class Ring:

    def __init__(self, slots):
        self.slots, self.readers, self.at = slots, [[] for _ in slots], 0
        self.open = [False] * len(slots)

    def take(self):
        i = self.at % len(self.slots)
        self.at += 1
        if self.open[i]:
            raise ValueError("a slot is taken again before its last use was noted")
        self.open[i] = True
        return i, self.slots[i], self.readers[i]

    def done(self, i, steps):
        self.readers[i] = list(steps)
        self.open[i] = False


def bc(ap, n):
    return ap.unsqueeze(2).to_broadcast([ap.shape[0], ap.shape[1], n])


def build(nc, d, out):
    ctx = ExitStack()
    with ctx:
        def sb(name, cols, dt=F32):
            return ctx.enter_context(nc.sbuf_tensor(name, [P, cols], dt))

        def sem(name):
            return ctx.enter_context(nc.semaphore(name))

        pe, dve, act, pool = Lane(sem("pe"), False), Lane(sem("dve"), True), Lane(sem("act"), True), Lane(sem("pool"), True)
        sp = Loads(sem)

        consts = sb("consts", 1408)
        small_cols = sb("small_cols", d["cols"].shape[1])
        x_t = sb("x", T * D)
        h_hi, h_lo = sb("h_hi", KD * S, F32R), sb("h_lo", KD * S, F32R)
        y_hi, y_lo = sb("y_hi", KD * S, F32R), sb("y_lo", KD * S, F32R)
        merged = sb("merged", T * D)
        R = [sb(f"r{i}", T * D) for i in range(11)]
        wslots = [sb(f"w{i}", PK * CH) for i in range(6)]
        wsplit = [(sb(f"w_hi{i}", PK * CH, F32R), sb(f"w_lo{i}", PK * CH, F32R)) for i in range(4)]
        bias_slots = [sb(f"bias{i}", CH) for i in range(2)]
        small = sb("small", 1600)
        rows = sb("rows", 320)
        scratch = [sb(f"scratch{i}", CH) for i in range(3)]
        idbf = sb("ident_bf16", P, BF16)
        maskbf = sb("masks_bf16", 3 * P, BF16)
        banks = [ctx.enter_context(nc.psum_tensor(f"bank{i}", [P, CH], F32)) for i in range(8)]

        ident, upto, ones_gt = consts[:, 0:128], consts[:, 128:256], consts[:, 256:512]
        ones, above = consts[:, 256:384], consts[:, 384:512]
        causal01 = consts[:, 128:256]
        cosT = consts[:, 896:960].rearrange("p (t f) -> p t f", t=T)
        sinT = consts[:, 960:1024].rearrange("p (t f) -> p t f", t=T)
        x3 = x_t[:, :].rearrange("p (t c) -> p t c", t=T)
        m3 = merged[:, :].rearrange("p (t c) -> p t c", t=T)
        hT = tuple(a[:, :].rearrange("p (k s) -> p k s", k=KD) for a in (h_hi, h_lo))
        yT = tuple(a[:, :].rearrange("p (k s) -> p k s", k=KD) for a in (y_hi, y_lo))

        wring, sring, bring = Ring(wslots), Ring(wsplit), Ring(bias_slots)
        bulk = Ring(banks[0:4])
        work = Ring(banks[4:7])
        mixed = Ring(banks[7:8])
        scr = Ring(scratch)

        cursor = [0]

        def stat(n):
            if cursor[0] + n > 1600:
                raise ValueError("statistics area is full")
            a = small[:, cursor[0]:cursor[0] + n]
            cursor[0] += n
            return a

        def now():
            return [l.last for l in (pe, dve, act, pool) if l.last is not None]

        def tok(ap):
            return ap.rearrange("p (t c) -> p t c", t=T)

        walk = [0]
        const_in = sp.load("consts", [(consts[:, 0:1408], d["consts"]), (small_cols[:, :], d["cols"])])
        x_in = sp.load("x", [(x_t[:, t * D:(t + 1) * D], d["x"][t * P:(t + 1) * P, :]) for t in range(T)])
        maskbf_made = dve.do(lambda v: v.tensor_copy(maskbf[:, 0:3 * P], consts[:, 512:896]), after=[const_in])
        dve.do(lambda v: v.tensor_copy(idbf[:, :], ident))
        causal_mask, window_mask = maskbf[:, 0:P], maskbf[:, P:3 * P]

        def rsqrt(r, v, scale, tmp):
            dve.do(lambda e: e.tensor_scalar(v, v, scale, EPS, MUL, ADD))
            s = act.do(lambda e: e.activation(r, v, ACT.Ln), after=[dve.last])
            s = act.do(lambda e: e.activation(r, r, ACT.Exp, scale=-0.5))
            for _ in range(2):
                dve.do(lambda e: e.tensor_tensor(tmp, r, r, MUL), after=[s])
                dve.do(lambda e: e.tensor_tensor(tmp, tmp, v, MUL))
                dve.do(lambda e: e.tensor_scalar(tmp, tmp, -0.5, 1.5, MUL, ADD))
                s = dve.do(lambda e: e.tensor_tensor(r, r, tmp, MUL))
            return s

        def sigmoid(dst, src, scale=1.0, after=()):
            a = act.do(lambda e: e.activation(dst, src, ACT.Tanh, scale=0.5 * scale), after=after)
            return dve.do(lambda e: e.tensor_scalar(dst, dst, 0.5, 0.5, MUL, ADD), after=[a])

        def log1p_exp_neg_abs(r, x, z, q, after=()):
            dve.do(lambda e: e.scalar_tensor_tensor(r, x, -1.0, x, MUL, MAX), after=after)
            s = act.do(lambda e: e.activation(r, r, ACT.Exp, scale=-1.0), after=[dve.last])
            dve.do(lambda e: e.tensor_scalar(z, r, 2.0, None, ADD), after=[s])
            dve.do(lambda e: e.reciprocal(z, z))
            dve.do(lambda e: e.tensor_tensor(r, r, z, MUL))
            dve.do(lambda e: e.tensor_tensor(z, r, r, MUL))
            dve.do(lambda e: e.tensor_scalar(q, z, 1.0 / 17, None, MUL))
            for n in (15, 13, 11, 9, 7, 5, 3):
                dve.do(lambda e, n=n: e.scalar_tensor_tensor(q, q, 1.0 / n, z, ADD, MUL))
            dve.do(lambda e: e.scalar_tensor_tensor(q, q, 1.0, r, ADD, MUL))
            return dve.do(lambda e: e.tensor_scalar(r, q, 2.0, None, MUL))

        def transposes(blocks, emit_out, after=(), width=4):
            for b0 in range(0, len(blocks), width):
                part = blocks[b0:b0 + width]
                i, bank, readers = work.take()
                for j, blk in enumerate(part):
                    c = blk.shape[1]
                    s = pe.do(lambda e, j=j, blk=blk, c=c, bank=bank: e.transpose(
                        bank[0:c, j * P:(j + 1) * P], blk, ident), after=list(after) + readers)
                work.done(i, emit_out(b0, len(part), bank, s))

        def rms_factor(src3, after=()):
            parts, ss, r, tmp = stat(2 * T), stat(T), stat(T), stat(T)
            i, squares, readers = scr.take()
            for t in range(T):
                for h in range(2):
                    s = act.do(lambda e, t=t, h=h: e.activation(squares[:, :], src3[:, t, h * CH:(h + 1) * CH], ACT.Square,
                               accum_out=parts[:, 2 * t + h:2 * t + h + 1]), after=list(after) + readers)
            scr.done(i, [s])
            dve.do(lambda e: e.tensor_reduce(ss, parts.rearrange("p (t h) -> p t h", h=2), AX, ADD), after=[s])
            return r, rsqrt(r, ss, 1.0 / D, tmp)

        def split(pair, src, after=()):
            hi, lo = pair
            a = act.do(lambda e: e.copy(hi, src), after=after)
            return [a, dve.do(lambda e: e.tensor_tensor(lo, src, hi.bitcast(F32), SUB), after=[a] + list(after))]

        def transpose_split(y3, pair, n_k, ready, free, col0=None):
            blocks = [y3[:, t, k * P:(k + 1) * P] for t in range(T) for k in range(n_k)]
            width = min(4, n_k)

            def copy_out(b0, n, bank, step):
                t, k = divmod(b0, n_k)
                dst = tuple(p[:, k:k + n, t * P:(t + 1) * P] for p in pair)
                src = bank[:, 0:n * P].rearrange("p (k s) -> p k s", k=n)
                if col0 is None:
                    return split(dst, src, after=[step] + free)
                i, tmp, readers = scr.take()
                tmp3 = tmp[:, 0:n * P].rearrange("p (k s) -> p k s", k=n)
                s = dve.do(lambda e: e.tensor_tensor(tmp3, src, bc(small_cols[:, col0 + k:col0 + k + n], P), MUL),
                           after=[step, const_in] + readers)
                done = split(dst, tmp3, after=[s] + free)
                scr.done(i, done)
                return [s]
            transposes(blocks, copy_out, after=ready, width=width)
            return [act.last, dve.last]

        def to_hT(src3, normed3, col0, after=(), dst=None, dst_free=None):
            r, s = rms_factor(src3, after)
            for t in range(T):
                s = dve.do(lambda e, t=t: e.tensor_scalar(normed3[:, t, :], src3[:, t, :], r[:, t:t + 1], None, MUL))
            return transpose_split(normed3, hT if dst is None else dst, KD, [s], hT_readers if dst is None else dst_free, col0)

        hT_readers, yT_readers = [], []

        order, fetched, made = [], [], [0]

        def piece(src, n):
            if walk[0] == 0:
                order.append((src, n))
                return fetch(src, n)
            while made[0] < len(order) and len(fetched) <= AHEAD:
                fetched.append(fetch(*order[made[0]]))
                made[0] += 1
            return fetched.pop(0)

        def fetch(src, n):
            i, slot, readers = wring.take()
            raw = slot[:, 0:PK * n].rearrange("p (k n) -> p k n", k=PK)
            loaded = sp.load(f"w{i}", [(raw, src.rearrange("(k p) n -> p k n", p=P))], after=readers)
            j, (hi, lo), sreaders = sring.take()
            hi, lo = (a[:, 0:PK * n].rearrange("p (k n) -> p k n", k=PK) for a in (hi, lo))
            a = act.do(lambda e: e.copy(hi, raw), after=[loaded] + sreaders)
            done = [a, pool.do(lambda e: e.tensor_tensor(lo, raw, hi.bitcast(F32), SUB), after=[a])]
            wring.done(i, done)
            return j, hi, lo, done

        def product(out, stat_pair, mov_pair, first, last, after, shared=False):
            (sh, sl), (mh, ml) = stat_pair, mov_pair
            pe.do(lambda e: e.matmul(out, sh, mh, start=first, stop=False, skip_group_check=shared), after=after)
            pe.do(lambda e: e.matmul(out, sh, ml, start=False, stop=False, skip_group_check=shared))
            return pe.do(lambda e: e.matmul(out, sl, mh, start=False, stop=last, skip_group_check=shared))

        def project(lhsT, src, rows_n, n, copy_out, after=(), bias=None, banks=None):
            k_n = rows_n // P
            banks = bulk if banks is None else banks
            out = [banks.take() for t in range(T)]
            if bias is not None:
                bi, brow, breaders = bring.take()
                b_in = sp.load(f"bias{bi}", [(brow[0:1, 0:n], bias)], after=breaders)
                for i, bank, readers in out:
                    s = pe.do(lambda e, bank=bank: e.matmul(bank[:, 0:n], ones[0:1, :], brow[0:1, 0:n],
                              start=True, stop=False), after=[b_in, const_in] + readers)
                bring.done(bi, [s])
            for k0 in range(0, k_n, PK):
                j, hi, lo, ready = piece(src[k0 * P:(k0 + PK) * P, :], n)
                for t, (i, bank, readers) in enumerate(out):
                    for k in range(PK):
                        kk = k0 + k
                        s = product(bank[:, 0:n], tuple(a[:, kk, t * P:(t + 1) * P] for a in lhsT), (hi[:, k, :], lo[:, k, :]),
                                    kk == 0 and bias is None, kk == k_n - 1, ready + readers + list(after))
                    if k0 + PK == k_n:
                        banks.done(i, copy_out(t, bank, s))
                sring.done(j, [s])
                yield

        def copy_to(dst3, c0, n):
            def f(t, bank, step):
                return [act.do(lambda e: e.copy(dst3[:, t, c0:c0 + n], bank[:, 0:n]), after=[step] + wait_for)]
            wait_for = []
            f.wait_for = wait_for
            return f

        def silu_to(dst3, c0, n, free):
            def f(t, bank, step):
                i, e_t, readers = scr.take()
                s = sigmoid(e_t[:, 0:n], bank[:, 0:n], after=[step, const_in] + readers)
                s = dve.do(lambda e: e.tensor_tensor(dst3[:, t, c0:c0 + n], bank[:, 0:n], e_t[:, 0:n], MUL), after=[s] + free)
                scr.done(i, [s])
                return [s]
            return f

        def plain_to(dst3, c0, n, free, scale=None):
            def f(t, bank, step):
                if scale is None:
                    return [act.do(lambda e: e.copy(dst3[:, t, c0:c0 + n], bank[:, 0:n]), after=[step] + free)]
                return [act.do(lambda e: e.mul(dst3[:, t, c0:c0 + n], bank[:, 0:n], scale), after=[step] + free)]
            return f

        def gated_add(y3, ky, wg, wp, bias_row, first, y_ready, col0=None):
            yk = tuple(a[:, 0:ky, :] for a in yT)
            if y3 is not None:
                y_ready = transpose_split(y3, yk, ky, y_ready, list(yT_readers), col0)
            for n0 in range(0, D, CH):
                sig = {}

                def gate_out(t, bank, step):
                    i, e_t, readers = scr.take()
                    s = sigmoid(e_t[:, :], bank[:, :], after=[step] + readers)
                    sig[t] = (i, e_t, s)
                    return [s]

                def branch_out(t, bank, step):
                    i, e_t, sg = sig[t]
                    dst = m3[:, t, n0:n0 + CH]
                    if first:
                        s = dve.do(lambda e: e.tensor_tensor(dst, bank[:, :], e_t[:, :], MUL), after=[step, sg] + merged_readers)
                        scr.done(i, [s])
                        return [s]
                    s0 = dve.do(lambda e: e.tensor_tensor(e_t[:, :], bank[:, :], e_t[:, :], MUL), after=[step, sg])
                    s = dve.do(lambda e: e.tensor_tensor(dst, dst, e_t[:, :], ADD))
                    scr.done(i, [s])
                    return [s0]
                yield from project(hT, wg[:, n0:n0 + CH], D, CH, gate_out,
                                   bias=None if bias_row is None else bias_row[:, n0:n0 + CH])
                yield from project(yk, wp[:, n0:n0 + CH], ky * P, CH, branch_out, after=y_ready)
                yT_readers[:] = [pe.last]

        merged_readers = []

        def out_projection(w):
            ready = transpose_split(m3, yT, KD, [dve.last], list(yT_readers))
            merged_readers[:] = [pe.last]
            for n0 in range(0, D, CH):
                def add(t, bank, step):
                    dst = x3[:, t, n0:n0 + CH]
                    return [dve.do(lambda e: e.tensor_tensor(dst, dst, bank[:, :], ADD), after=[step])]
                for _ in project(yT, w[:, n0:n0 + CH], D, CH, add, after=ready):
                    pass
            yT_readers[:] = [pe.last]

        def transpose_scaled(y3, yT, n_k, ready, free, col0=None):
            blocks = [y3[:, t, k * P:(k + 1) * P] for t in range(T) for k in range(n_k)]
            width = min(4, n_k)

            def copy_out(b0, n, bank, step):
                t, k = divmod(b0, n_k)
                dst = yT[:, k:k + n, t * P:(t + 1) * P]
                src = bank[:, 0:n * P].rearrange("p (k s) -> p k s", k=n)
                if col0 is None:
                    return [act.do(lambda e: e.copy(dst, src), after=[step] + free)]
                return [dve.do(lambda e: e.tensor_tensor(dst, src, bc(small_cols[:, col0 + k:col0 + k + n], P), MUL),
                               after=[step] + free)]
            transposes(blocks, copy_out, after=ready, width=width)
            return [act.last if col0 is None else dve.last]

        def attention(units, n_heads, dv, y3, v_of, ready, p_buf, pT_buf, sink=None, gated=False):
            mx_all, sum_all = stat(T * n_heads), stat(T * n_heads)
            pring, ptring = Ring(p_buf), Ring(pT_buf)
            outs, filled = {}, {}
            per_bank = CH // dv
            state = []

            def stage_scores(u):
                t, h0, hn, hs, scores, keys = u
                i, bank, readers = work.take()
                for j in range(hn):
                    s = scores(h0 + j * hs, t, bank[:, j * keys:(j + 1) * keys], list(ready) + readers)
                c = t * n_heads + h0
                mx = mx_all[:, c:c + hs * (hn - 1) + 1:hs]
                s = dve.do(lambda e: e.tensor_reduce(mx, bank[:, 0:hn * keys].rearrange("p (h k) -> p h k", h=hn), AX, MAX), after=[s])
                if sink is not None:
                    dve.do(lambda e: e.tensor_tensor(mx, mx, sink[:, h0:h0 + hs * (hn - 1) + 1:hs], MAX))
                s = dve.do(lambda e: e.tensor_scalar(mx, mx, -1.0, None, MUL))
                pi, p, preaders = pring.take()
                for j in range(hn):
                    a = act.do(lambda e, j=j: e.activation(p[:, j * keys:(j + 1) * keys], bank[:, j * keys:(j + 1) * keys], ACT.Exp,
                               bias=mx[:, j:j + 1], accum_out=sum_all[:, c + j * hs:c + j * hs + 1]), after=[s] + preaders)
                work.done(i, [a])
                return pi, p, a

            def stage_transpose(u, pi, p, a):
                t, h0, hn, hs, scores, keys = u
                kb = keys // P
                n = hn * kb
                i, bank, readers = work.take()
                for j in range(n):
                    s = pe.do(lambda e, j=j: e.transpose(bank[:, j * P:(j + 1) * P], p[:, j * P:(j + 1) * P], ident), after=[a] + readers)
                pring.done(pi, [s])
                ti, pT, treaders = ptring.take()
                s = act.do(lambda e: e.copy(pT[:, 0:n * P], bank[:, 0:n * P]), after=[s] + treaders)
                work.done(i, [s])
                return ti, pT, s

            def stage_pv(u, ti, pT, ready_pT):
                t, h0, hn, hs, scores, keys = u
                kb = keys // P
                for j in range(hn):
                    h = h0 + j * hs
                    key = (t, h // per_bank)
                    if key not in outs:
                        outs[key] = mixed.take()
                        filled[key] = 0
                    i, bank, readers = outs[key]
                    c = (h % per_bank) * dv
                    for b in range(kb):
                        s = pe.do(lambda e, j=j, b=b, bank=bank, c=c, h=h: e.matmul(
                            bank[:, c:c + dv], pT[:, (j * kb + b) * P:(j * kb + b + 1) * P], v_of(h, b),
                            start=(b == 0), stop=(b == kb - 1)), after=[ready_pT] + readers)
                    filled[key] += 1
                    if filled[key] == min(per_bank, n_heads):
                        first = h // per_bank * per_bank
                        finish(t, first, first + filled[key], i, bank, s)
                ptring.done(ti, [s])

            def finish(t, h0, h1, i, bank, s):
                c = t * n_heads
                sm, mx = sum_all[:, c + h0:c + h1], mx_all[:, c + h0:c + h1]
                n = h1 - h0
                if sink is not None:
                    es = stat(n)
                    dve.do(lambda e: e.tensor_tensor(es, sink[:, h0:h1], mx, ADD))
                    a = act.do(lambda e: e.activation(es, es, ACT.Exp), after=[dve.last])
                    dve.do(lambda e: e.tensor_tensor(sm, sm, es, ADD), after=[a])
                dve.do(lambda e: e.reciprocal(sm, sm), after=[act.last])
                dst = y3[:, t, h0 * dv:h1 * dv]
                dst3 = dst.rearrange("p (h c) -> p h c", h=n)
                if gated:
                    dve.do(lambda e: e.tensor_tensor(dst3, dst3, bc(sm, dv), MUL))
                    s = dve.do(lambda e: e.tensor_tensor(dst, dst, bank[:, 0:n * dv], MUL), after=[s])
                else:
                    s = dve.do(lambda e: e.tensor_tensor(dst3, bank[:, 0:n * dv].rearrange("p (h c) -> p h c", h=n),
                               bc(sm, dv), MUL), after=[s])
                mixed.done(i, [s])

            a1, a2 = {}, {}
            n = len(units)
            for i in range(n + 2):
                if i < n:
                    a1[i] = stage_scores(units[i])
                if 1 <= i <= n:
                    a2[i - 1] = stage_transpose(units[i - 1], *a1.pop(i - 1))
                if i >= 2:
                    stage_pv(units[i - 2], *a2.pop(i - 2))
                yield

        def rope(dst, src, cos, sin, heads, tmp, half=HD // 2, free=()):
            def b(a):
                return a.unsqueeze(1).to_broadcast([P, heads, half])
            x1, x2 = src[:, :, 0:half], src[:, :, half:2 * half]
            t1, t2 = tmp[:, :, 0:half], tmp[:, :, half:2 * half]
            d1, d2 = dst[:, :, 0:half], dst[:, :, half:2 * half]
            dve.do(lambda e: e.tensor_tensor(t1, x2, b(sin), MUL), after=free)
            dve.do(lambda e: e.tensor_tensor(t2, x1, b(sin), MUL))
            dve.do(lambda e: e.tensor_tensor(d1, x1, b(cos), MUL))
            dve.do(lambda e: e.tensor_tensor(d2, x2, b(cos), MUL))
            dve.do(lambda e: e.tensor_tensor(d1, d1, t1, SUB))
            return dve.do(lambda e: e.tensor_tensor(d2, d2, t2, ADD))

        steps_of = []

        def together(main, side):
            if walk[0] == 0:
                steps_of.append([sum(1 for _ in main), sum(1 for _ in side)])
                return
            n_main, n_side = steps_of.pop(0)
            given = 0
            for i in range(n_main):
                next(main)
                while given * n_main < (i + 1) * n_side:
                    next(side)
                    given += 1
            for _ in itertools.chain(main, side):
                pass

        def layer(l):
            cursor[0] = 0
            w_in, w_proj, w_out = d["w_in"][l], d["w_proj"][l], d["w_out"][l]
            col = COLS1[l]
            base = now()
            rowp = d["rows"]
            r0 = ROWS1[l]
            row_in = sp.load("rows", [(rows[:, 0:5 * 16], rowp[:, r0:r0 + 5 * 16].to_broadcast([P, 5 * 16]))], after=base)
            dt_bias, a_log, d_skip, sinks, f_bias = (rows[:, 16 * i:16 * i + 16] for i in range(5))
            normed = tok(R[9][:, :])
            h_ready = to_hT(x3, normed, col["norm"], after=[x_in, dve.last])
            free = now()

            def seq(*sections):
                for f in sections:
                    yield from f

            def plain(c0, n, dst3, dcol, fr, scale=None):
                for o in range(0, n, CH):
                    m = min(CH, n - o)
                    yield from project(hT, w_in[:, c0 + o:c0 + o + m], D, m, plain_to(dst3, dcol + o, m, fr, scale), after=h_ready)

            def silu(c0, n, dst3, fr):
                for o in range(0, n, CH):
                    yield from project(hT, w_in[:, c0 + o:c0 + o + CH], D, CH, silu_to(dst3, o, CH, fr), after=h_ready)

            xbc = [tok(R[0][:, :]), tok(R[1][:, :])]
            za = tok(R[2][:, :])
            dtr = stat(2 * 16).rearrange("p (t h) -> p t h", t=T)
            fr_ = stat(2 * 16).rearrange("p (t h) -> p t h", t=T)
            for _ in seq(plain(DT, 16, dtr, 0, free), plain(XBC, D, xbc[0], 0, free),
                         plain(XBC + D, D, xbc[1], 0, free)):
                pass

            y_ready = {}
            y_a, y_b, y_c = (tok(R[i][:, :]) for i in (5, 8, 3))

            def mamba():
                raw = [R[3][:, :].rearrange("p (k s) -> p k s", k=KD), R[4][:, :].rearrange("p (k s) -> p k s", k=KD)]
                conv = [R[0][:, :].rearrange("p (k s) -> p k s", k=KD), R[1][:, :].rearrange("p (k s) -> p k s", k=KD)]
                for half in range(2):
                    transpose_scaled(xbc[half], raw[half], KD, [act.last], free)
                    yield
                last_t = [pe.last]
                for half in range(2):
                    for k in range(KD):
                        c = half * KD + k
                        u, o = raw[half][:, k, :], conv[half][:, k, :]
                        wc = [small_cols[:, col["conv"] + w * 16 + c:col["conv"] + w * 16 + c + 1] for w in range(CONV_W)]
                        bcol = small_cols[:, col["conv_b"] + c:col["conv_b"] + c + 1]
                        dve.do(lambda e, u=u, o=o, wc=wc, bcol=bcol: e.tensor_scalar(o, u, wc[3], bcol, MUL, ADD), after=[act.last] + last_t)
                        for w in range(3):
                            sh = 3 - w
                            dve.do(lambda e, u=u, o=o, wc=wc, w=w, sh=sh: e.scalar_tensor_tensor(
                                o[:, sh:S], u[:, 0:S - sh], wc[w], o[:, sh:S], MUL, ADD))
                    src, e_t = R[half], R[3 + half]
                    a = sigmoid(e_t[:, :], src[:, :], after=[dve.last])
                    dve.do(lambda e, src=src, e_t=e_t: e.tensor_tensor(src[:, :], src[:, :], e_t[:, :], MUL), after=[a])
                    yield
                conv_ready = [dve.last]
                xT, bcT = conv
                x_tok, xdt = tok(R[3][:, :]), tok(R[4][:, :])
                blocks = [xT[:, k, t * P:(t + 1) * P] for t in range(T) for k in range(KD)]

                def x_out(b0, n, bank, step):
                    t, k = divmod(b0, KD)
                    return [act.do(lambda e: e.copy(x_tok[:, t, k * P:(k + n) * P], bank[:, 0:n * P]), after=[step, conv_ready[0]])]
                transposes(blocks, x_out, after=conv_ready)
                b_tok = R[9][:, 0:GROUPS * P].rearrange("p (g n) -> p g n", g=GROUPS)
                blocks = [bcT[:, g, 0:P] for g in range(GROUPS)]
                transposes(blocks, lambda b0, n, bank, step: [act.do(
                    lambda e: e.copy(b_tok[:, b0:b0 + n, :], bank[:, 0:n * P].rearrange("p (g n) -> p g n", g=n)), after=[step] + free)],
                    after=conv_ready)
                x_ready = act.last
                yield
                dt, adt, z, q = (stat(32).rearrange("p (t h) -> p t h", t=T) for _ in range(4))
                na = stat(16)
                dve.do(lambda e: e.tensor_tensor(dtr, dtr, dt_bias.unsqueeze(1).to_broadcast([P, T, 16]), ADD), after=[row_in, act.last])
                s = act.do(lambda e: e.activation(na, a_log, ACT.Exp), after=[row_in])
                log1p_exp_neg_abs(dt, dtr, z, q)
                dve.do(lambda e: e.scalar_tensor_tensor(dt, dtr, 0.0, dt, MAX, ADD))
                dve.do(lambda e: e.scalar_tensor_tensor(adt, dt, -1.0, na.unsqueeze(1).to_broadcast([P, T, 16]), MUL, MUL), after=[s])
                adt_ready = dve.last
                for t in range(T):
                    dve.do(lambda e, t=t: e.tensor_tensor(xdt[:, t, :].rearrange("p (h c) -> p h c", h=HEADS),
                           x_tok[:, t, :].rearrange("p (h c) -> p h c", h=HEADS), bc(dt[:, t, :], HD), MUL), after=[x_ready])
                xdt_ready = dve.last
                i, bank, readers = work.take()
                pe.do(lambda e: e.matmul(bank[:, 0:16], above, adt[:, 0, :], start=True, stop=True), after=[adt_ready] + readers)
                s = pe.do(lambda e: e.matmul(bank[:, 16:32], upto, adt[:, 1, :], start=True, stop=True))
                decs = stat(32)
                s = act.do(lambda e: e.activation(decs, bank[:, 0:32], ACT.Exp), after=[s])
                work.done(i, [s])
                to_end, from_start = decs[:, 0:16], decs[:, 16:32]
                xds = R[9][:, CH:CH + D]
                dve.do(lambda e: e.tensor_tensor(xds.rearrange("p (h c) -> p h c", h=HEADS), xdt[:, 0, :].rearrange("p (h c) -> p h c", h=HEADS),
                       bc(to_end, HD), MUL), after=[s] + free)
                state = R[10][:, 0:D]
                for g in range(0, GROUPS, 2):
                    i, bank, readers = work.take()
                    for j in range(2):
                        s = pe.do(lambda e, g=g, j=j, bank=bank: e.matmul(bank[:, j * 256:(j + 1) * 256], b_tok[:, g + j, :],
                                  xds[:, (g + j) * 256:(g + j + 1) * 256], start=True, stop=True), after=[dve.last, x_ready] + readers)
                    s = act.do(lambda e, g=g, bank=bank: e.copy(state[:, g * 256:(g + 2) * 256], bank[:, :]), after=[s] + free)
                    work.done(i, [s])
                state_ready = act.last
                yield
                cb = R[10][:, D:2 * D].rearrange("p (t g l) -> p t g l", t=T, g=GROUPS)
                for t in range(T):
                    i, bank, readers = work.take()
                    for g in range(GROUPS):
                        s = pe.do(lambda e, t=t, g=g, bank=bank: e.matmul(bank[:, g * P:(g + 1) * P], bcT[:, g, t * P:(t + 1) * P],
                                  bcT[:, GROUPS + g, t * P:(t + 1) * P], start=True, stop=True), after=conv_ready + readers)
                    s = dve.do(lambda e, t=t, bank=bank: e.tensor_tensor(cb[:, t, :, :], bank[:, :].rearrange("p (g l) -> p g l", g=GROUPS),
                               causal01.unsqueeze(1).to_broadcast([P, GROUPS, P]), MUL), after=[s] + free)
                    work.done(i, [s])
                yield
                y = y_a
                ya_free = free
                lhs_ring, m_ring = Ring([R[9][:, 0:CH], R[9][:, CH:2 * CH]]), Ring([R[9][:, 2 * CH:3 * CH], R[9][:, 3 * CH:4 * CH]])
                lhs_ring.readers = [[pe.last], [pe.last]]
                todo, pend = [(t, g) for t in range(T) for g in range(GROUPS)], []
                for n in range(len(todo) + 1):
                    if n < len(todo):
                        t, g = todo[n]
                        li, lhs, lr = lhs_ring.take()
                        lhs3 = lhs.rearrange("p (r k) -> p r k", r=RPG)
                        s = dve.do(lambda e, t=t, g=g, lhs3=lhs3: e.tensor_tensor(lhs3, above.unsqueeze(1).to_broadcast([P, RPG, P]),
                                   bc(adt[:, t, g * RPG:(g + 1) * RPG], P), MUL), after=lr)
                        i, bank, readers = work.take()
                        for r in range(RPG):
                            s2 = pe.do(lambda e, r=r, lhs3=lhs3, bank=bank: e.matmul(bank[:, r * P:(r + 1) * P], lhs3[:, r, :], upto,
                                       start=True, stop=True), after=[s] + readers)
                        lhs_ring.done(li, [s2])
                        mi, m, mr = m_ring.take()
                        s3 = act.do(lambda e, m=m, bank=bank: e.activation(m, bank[:, :], ACT.Exp), after=[s2] + mr)
                        work.done(i, [s3])
                        s4 = dve.do(lambda e, m=m, t=t, g=g: e.tensor_tensor(m.rearrange("p (r l) -> p r l", r=RPG), m.rearrange("p (r l) -> p r l", r=RPG),
                                    cb[:, t, g, :].unsqueeze(1).to_broadcast([P, RPG, P]), MUL), after=[s3])
                        pend.append((t, g, mi, m, s4))
                    if n >= 1:
                        t, g, mi, m, s4 = pend.pop(0)
                        i, bank, readers = work.take()
                        for r in range(RPG):
                            h = g * RPG + r
                            s = pe.do(lambda e, r=r, h=h, t=t, m=m, bank=bank: e.matmul(bank[:, r * HD:(r + 1) * HD], m[:, r * P:(r + 1) * P],
                                      xdt[:, t, h * HD:(h + 1) * HD], start=True, stop=True), after=[s4, xdt_ready] + readers)
                        m_ring.done(mi, [s])
                        if t == 1:
                            s = pe.do(lambda e, g=g, bank=bank: e.matmul(bank[:, 256:512], bcT[:, GROUPS + g, P:2 * P],
                                      state[:, g * 256:(g + 1) * 256], start=True, stop=True), after=[state_ready])
                        yg = y[:, t, g * 256:(g + 1) * 256]
                        xg = x_tok[:, t, g * 256:(g + 1) * 256]

                        def v(a):
                            return a.rearrange("p (r c) -> p r c", r=RPG)
                        s = dve.do(lambda e, xg=xg, yg=yg, g=g: e.tensor_tensor(v(yg), v(xg), bc(d_skip[:, g * RPG:(g + 1) * RPG], HD), MUL),
                                   after=[s] + ya_free)
                        s = dve.do(lambda e, yg=yg, bank=bank: e.tensor_tensor(yg, yg, bank[:, 0:256], ADD))
                        if t == 1:
                            dve.do(lambda e, xg=xg, bank=bank, g=g: e.tensor_tensor(v(xg), v(bank[:, 256:512]),
                                   bc(from_start[:, g * RPG:(g + 1) * RPG], HD), MUL))
                            s = dve.do(lambda e, xg=xg, yg=yg: e.tensor_tensor(yg, yg, xg, ADD))
                        work.done(i, [dve.last])
                    yield
                ss, r8, tmp8 = stat(8), stat(8), stat(8)
                dve.do(lambda e: e.tensor_tensor(R[5][:, :], R[5][:, :], R[2][:, :], MUL))
                s = act.do(lambda e: e.activation(R[3][:, :], R[5][:, :], ACT.Square), after=[dve.last])
                dve.do(lambda e: e.tensor_reduce(ss, R[3][:, :].rearrange("p (g c) -> p g c", g=8), AX, ADD), after=[s])
                rsqrt(r8, ss, 1.0 / 256, tmp8)
                y8 = R[5][:, :].rearrange("p (g c) -> p g c", g=8)
                y_ready["a"] = [dve.do(lambda e: e.tensor_tensor(y8, y8, bc(r8, 256), MUL))]
                yield

            kvb = tok(R[7][:, 0:D])
            qb, zb = tok(R[6][:, :]), tok(R[8][:, :])
            together(seq(silu(ZA, D, za, free), plain(QB, D, qb, 0, free, HD ** -0.5), plain(KV, CH, kvb, 0, free), silu(ZB, D, zb, free)), mamba())

            def window():
                q_rot = tok(R[9][:, :])
                k_dup = R[7][:, D:2 * D].rearrange("p (t g u c) -> p t g u c", t=T, g=KVH, u=2)
                base_w = now()
                for t in range(T):
                    tmp = R[10][:, 0:D].rearrange("p (h c) -> p h c", h=HEADS)
                    rope(q_rot[:, t, :].rearrange("p (h c) -> p h c", h=HEADS), qb[:, t, :].rearrange("p (h c) -> p h c", h=HEADS),
                         cosT[:, t, :], sinT[:, t, :], HEADS, tmp, free=base_w)
                    rope(k_dup[:, t, :, 0, :], kvb[:, t, 0:256].rearrange("p (g c) -> p g c", g=KVH), cosT[:, t, :], sinT[:, t, :],
                         KVH, R[10][:, 0:256].rearrange("p (h c) -> p h c", h=KVH))
                    dve.do(lambda e, t=t: e.tensor_copy(k_dup[:, t, :, 1, :], k_dup[:, t, :, 0, :]))
                    yield
                qT = R[6][:, :].rearrange("p (k s) -> p k s", k=KD)
                ready = transpose_scaled(q_rot, qT, KD, [dve.last], [dve.last])
                yield
                kT = R[10][:, 0:D].rearrange("p (g s) -> p g s", g=KVH)
                k_flat = R[7][:, D:2 * D].rearrange("p (t c) -> p t c", t=T)
                ready = transpose_scaled(k_flat, kT, KVH, [dve.last], [dve.last])
                yield
                def scores(h, t, dst, after):
                    keys = (t + 1) * P
                    par = HD * (h % 2)
                    pe.do(lambda e: e.matmul(dst, qT[par:par + HD, h // 2, t * P:(t + 1) * P], kT[par:par + HD, h // KVH, 0:keys],
                          start=True, stop=False), after=after)
                    mask = causal_mask if t == 0 else window_mask
                    return pe.do(lambda e: e.matmul(dst, idbf[:, :], mask, start=False, stop=True), after=[maskbf_made])
                units = [(t, h, 2, 2, scores, (t + 1) * P) for t in range(T) for q in range(0, HEADS, 4) for h in (q, q + 1)]
                yield from attention(units, HEADS, HD, y_b, lambda h, b: kvb[:, b, 256 + (h // 4) * HD:256 + (h // 4 + 1) * HD],
                                     ready, [R[4][:, 0:CH], R[4][:, CH:2 * CH]], [R[4][:, 2 * CH:3 * CH], R[4][:, 3 * CH:4 * CH]],
                                     sink=sinks, gated=True)
                y_ready["b"] = [dve.last]
                yield

            free_a = now()
            cq, ck, cv, zc = (tok(R[i][:, :]) for i in range(4))
            together(seq(plain(CF, 16, fr_, 0, []), plain(CQ, D, cq, 0, free_a, HD ** -0.5), plain(CK, D, ck, 0, free_a), plain(CV, D, cv, 0, free_a),
                         silu(CZ, D, zc, free_a)), window())

            def forget():
                free_b = now()
                qT = R[6][:, :].rearrange("p (k s) -> p k s", k=KD)
                kT = R[7][:, :].rearrange("p (k s) -> p k s", k=KD)
                transpose_scaled(cq, qT, KD, [act.last], free_b)
                yield
                ready = transpose_scaled(ck, kT, KD, [act.last], free_b)
                yield
                lf, z, q = (stat(32).rearrange("p (t h) -> p t h", t=T) for _ in range(3))
                dve.do(lambda e: e.tensor_tensor(fr_, fr_, f_bias.unsqueeze(1).to_broadcast([P, T, 16]), ADD), after=[act.last])
                log1p_exp_neg_abs(lf, fr_, z, q)
                dve.do(lambda e: e.scalar_tensor_tensor(lf, fr_, 0.0, lf, MIN, SUB))
                lf_ready = dve.last
                bias_ring = Ring([R[10][:, 3 * i * P:3 * (i + 1) * P] for i in range(4)])
                bias_ring.readers = [free_b for _ in range(4)]

                def scores(h, t, dst, after):
                    keys = (t + 1) * P
                    par = HD * (h % 2)
                    i, bm, readers = bias_ring.take()
                    s = dve.do(lambda e: e.tensor_scalar(bm[:, 0:P], above, lf[:, 0, h:h + 1], None, MUL), after=readers)
                    if t == 1:
                        s = dve.do(lambda e: e.tensor_scalar(bm[:, P:3 * P], ones_gt, lf[:, 1, h:h + 1], None, MUL), after=readers)
                    pe.do(lambda e: e.matmul(dst, qT[par:par + HD, h // 2, t * P:(t + 1) * P], kT[par:par + HD, h // 2, 0:keys],
                          start=True, stop=False), after=after)
                    if t == 0:
                        pe.do(lambda e: e.matmul(dst, upto, bm[:, 0:P], start=False, stop=False), after=[s])
                        last = pe.do(lambda e: e.matmul(dst, idbf[:, :], causal_mask, start=False, stop=True), after=[maskbf_made])
                    else:
                        pe.do(lambda e: e.matmul(dst, upto, bm[:, P:3 * P], start=False, stop=False), after=[s])
                        pe.do(lambda e: e.matmul(dst[:, 0:P], ones, bm[:, 0:P], start=False, stop=False))
                        last = pe.do(lambda e: e.matmul(dst[:, P:2 * P], idbf[:, :], causal_mask, start=False, stop=True), after=[maskbf_made])
                    bias_ring.done(i, [last])
                    return last
                units = [(t, h, 2, 2, scores, (t + 1) * P) for t in range(T) for q in range(0, HEADS, 4) for h in (q, q + 1)]
                yield from attention(units, HEADS, HD, y_c, lambda h, b: cv[:, b, h * HD:(h + 1) * HD],
                                     ready, [R[4][:, 0:CH], R[4][:, CH:2 * CH]], [R[4][:, 2 * CH:3 * CH], R[4][:, 3 * CH:4 * CH]], gated=True)
                y_ready["c"] = [dve.last]
                yield

            gb = d["rows"]
            g0 = ROWS1[l] + 80

            def mix(i, y, key, col0=None):
                return gated_add(y, KD, w_in[:, GATES + i * D:GATES + (i + 1) * D], w_proj[i],
                                 gb[:, g0 + i * D:g0 + (i + 1) * D], i == 0, y_ready[key], col0)
            together(seq(mix(0, y_a, "a", col["ssm_norm"]), mix(1, y_b, "b")), forget())
            for _ in mix(2, y_c, "c"):
                pass
            out_projection(w_out)
            hT_readers[:] = [pe.last]

        COLS1, COLS2 = d["cols_at"][0:2], d["cols_at"][2]
        ROWS1, ROWS2 = d["rows_at"][0:2], d["rows_at"][2]
        def second():
            cursor[0] = 0
            col = COLS2
            w_in = d["w_in_2"]
            start = now()
            r0 = ROWS2["small"]
            n_small = 64 * 2 + 128 * 2 + NGRP + EXP
            row_in = sp.load("rows2", [(rows2[:, :], d["rows"][:, r0:r0 + n_small].to_broadcast([P, n_small]))])
            g_q, g_k, g_qm, g_km = rows2[:, 0:64], rows2[:, 64:128], rows2[:, 128:256], rows2[:, 256:384]
            b_grp, b_exp = rows2[:, 384:388], rows2[:, 388:420]
            fw = R[0][:, 0:D]
            fw_in = sp.load("r0", [(fw, d["rows"][:, ROWS2["final"]:ROWS2["final"] + D].to_broadcast([P, D]))], after=start)
            mem3 = tok(R[2][:, :])
            mem_in = sp.load("r2", [(mem3[:, t, :], d["mem"][t * P:(t + 1) * P, :]) for t in range(T)], after=start)
            pos_i, pos_f = R[10][:, 0:T + S].bitcast(I32), rows[:, 0:T + S]
            pos_in = sp.load("pos", [(pos_i[:, 0:T], d["pos_col"]),
                                     (pos_i[:, T:T + S], d["pos"].to_broadcast([P, S]))], after=start)

            r, s = rms_factor(x3, [dve.last])
            for t in range(T):
                dve.do(lambda e, t=t: e.scalar_tensor_tensor(x3[:, t, :], x3[:, t, :], r[:, t:t + 1], fw, MUL, MUL), after=[fw_in])
            x_ready = dve.last

            def plain(c0, n, dst3, dcol, fr, ready, w=None, scale=None):
                src = w_in if w is None else w
                lhs = hT if w is None else mhT
                for o in range(0, n, CH):
                    m = min(CH, n - o)
                    yield from project(lhs, src[:, c0 + o:c0 + o + m], D, m, plain_to(dst3, dcol + o, m, fr, scale), after=ready)

            mhT = yT
            normed = tok(R[1][:, :])
            mem_ready = to_hT(mem3, normed, col["g_mem"], after=[mem_in], dst=mhT, dst_free=start)
            kmv = tok(R[4][:, :])
            for _ in plain(0, 2 * CH, kmv, 0, start, mem_ready, w=d["w_mem_kv"]):
                pass
            kmv_ready = act.last
            yT_readers[:] = [pe.last]
            h_ready = to_hT(x3, normed, col["g_mix"], after=[x_ready, pe.last])

            def sin_cos(sn, cs, x, n, tmp):
                dve.do(lambda e: e.tensor_scalar(n, x, TURNS, ROUND, MUL, ADD))
                dve.do(lambda e: e.tensor_scalar(n, n, ROUND, None, SUB))
                for part in TWO_PI:
                    dve.do(lambda e, part=part: e.scalar_tensor_tensor(x, n, -part, x, MUL, ADD))
                dve.do(lambda e: e.tensor_scalar(x, x, PI, -PI, MIN, MAX))
                s = act.do(lambda e: e.activation(sn, x, ACT.Sin), after=[dve.last])
                dve.do(lambda e: e.scalar_tensor_tensor(tmp, x, -1.0, x, MUL, MAX))
                dve.do(lambda e: e.tensor_scalar(tmp, tmp, -1.0, HALF_PI, MUL, ADD))
                return act.do(lambda e: e.activation(cs, tmp, ACT.Sin), after=[dve.last])

            dve.do(lambda e: e.tensor_copy(pos_f, pos_i), after=[pos_in])
            ang, sn2, cs2, tmp2, n2 = (stat(64) for _ in range(5))
            inv = consts[:, 1024:1056]
            for t in range(T):
                dve.do(lambda e, t=t: e.tensor_scalar(ang[:, 32 * t:32 * t + 32], inv, pos_f[:, t:t + 1], None, MUL))
            rope_ready = sin_cos(sn2, cs2, ang, n2, tmp2)
            sn3, cs3 = sn2.rearrange("p (t f) -> p t f", t=T), cs2.rearrange("p (t f) -> p t f", t=T)

            lre, lim, ldt = (small_cols[:, col[n]:col[n] + ST] for n in ("lam_re", "lam_im", "log_dt"))
            dt5, rad, th, thn, tht, c5, s5, nr, ni, fr5, fi5, den = (stat(ST) for _ in range(12))
            a = act.do(lambda e: e.activation(dt5, ldt, ACT.Exp), after=[const_in])
            dve.do(lambda e: e.tensor_tensor(rad, lre, dt5, MUL), after=[a])
            dve.do(lambda e: e.tensor_tensor(th, lim, dt5, MUL))
            act.do(lambda e: e.activation(rad, rad, ACT.Exp), after=[dve.last])
            sin_cos(s5, c5, th, thn, tht)
            dve.do(lambda e: e.tensor_tensor(nr, rad, c5, MUL), after=[act.last])
            dve.do(lambda e: e.tensor_scalar(nr, nr, -1.0, None, ADD))
            dve.do(lambda e: e.tensor_tensor(ni, rad, s5, MUL))
            dve.do(lambda e: e.tensor_tensor(den, lre, lre, MUL))
            dve.do(lambda e: e.tensor_tensor(tht, lim, lim, MUL))
            dve.do(lambda e: e.tensor_tensor(den, den, tht, ADD))
            dve.do(lambda e: e.reciprocal(den, den))
            for dst, a1, a2, op in ((fr5, nr, ni, ADD), (fi5, ni, nr, SUB)):
                dve.do(lambda e, dst=dst, a1=a1: e.tensor_tensor(dst, a1, lre, MUL))
                dve.do(lambda e, a2=a2: e.tensor_tensor(tht, a2, lim, MUL))
                dve.do(lambda e, dst=dst, op=op: e.tensor_tensor(dst, dst, tht, op))
                dve.do(lambda e, dst=dst: e.tensor_tensor(dst, dst, den, MUL))
            wc, ws = [c5], [s5]
            for j in range(7):
                c_, s_, q_ = stat(ST), stat(ST), tht
                pc, ps_ = wc[-1], ws[-1]
                dve.do(lambda e, c_=c_, pc=pc: e.tensor_tensor(c_, pc, pc, MUL))
                dve.do(lambda e, ps_=ps_: e.tensor_tensor(q_, ps_, ps_, MUL))
                dve.do(lambda e, c_=c_: e.tensor_tensor(c_, c_, q_, SUB))
                dve.do(lambda e, s_=s_, pc=pc, ps_=ps_: e.scalar_tensor_tensor(s_, pc, 2.0, ps_, MUL, MUL))
                wc.append(c_)
                ws.append(s_)

            u3, q3 = tok(R[5][:, 0:D]), tok(R[5][:, D:2 * D])
            kvi, qm3 = tok(R[6][:, 0:D]), tok(R[6][:, D:2 * D])
            for _ in plain(Q2, CH, q3, 0, start, h_ready):
                pass
            for _ in plain(KVI2, QM2 - KVI2, kvi, 0, start, h_ready):
                pass

            def head_norm(x_4, heads, c, gain, junk, after=()):
                ss, r, tmp = stat(heads), stat(heads), stat(heads)
                dve.do(lambda e: e.tensor_tensor(junk, x_4, x_4, MUL), after=after)
                dve.do(lambda e: e.tensor_reduce(ss, junk, AX, ADD))
                rsqrt(r, ss, 1.0 / c, tmp)
                dve.do(lambda e: e.tensor_tensor(x_4, x_4, bc(r, c), MUL))
                return dve.do(lambda e: e.tensor_tensor(x_4, x_4, gain.unsqueeze(1).to_broadcast([P, heads, c]), MUL))

            def sparse():
                dve.do(lambda e: e.tensor_scalar(g_q, g_q, HD ** -0.5, None, MUL), after=[row_in, act.last])
                rot = tok(R[7][:, :])
                tmp = R[8][:, 0:CH].rearrange("p (h c) -> p h c", h=8)

                def hv(a, h):
                    return a.rearrange("p (h c) -> p h c", h=h)
                for t in range(T):
                    qh, kh = hv(q3[:, t, :], 8), hv(kvi[:, t, 0:64], 1)
                    head_norm(qh, 8, HD, g_q, tmp, after=start)
                    head_norm(kh, 1, HD, g_k, tmp[:, 0:1, :])
                    cs, sn = cs3[:, t, :], sn3[:, t, :]
                    rope(hv(rot[:, t, 0:512], 8), qh, cs, sn, 8, tmp, free=[rope_ready])
                    rope(hv(rot[:, t, 512:576], 1), kh, cs, sn, 1, tmp[:, 0:1, :])
                    dve.do(lambda e, t=t: e.tensor_copy(rot[:, t, 576:640], rot[:, t, 512:576]))
                    rope(hv(rot[:, t, 640:896], 4), hv(kvi[:, t, 128:384], 4), cs, sn, 4, tmp[:, 0:4, :])
                    rope(hv(rot[:, t, 896:960], 1), hv(kvi[:, t, 384:448], 1), cs, sn, 1, tmp[:, 0:1, :])
                    dve.do(lambda e, t=t: e.tensor_copy(rot[:, t, 960:1024], rot[:, t, 896:960]))
                    yield
                aT = R[8][:, :].rearrange("p (k s) -> p k s", k=KD)
                ready = transpose_scaled(rot, aT, KD, [dve.last], [dve.last])
                yield
                def select(t):
                    pq = pos_f[:, t:t + 1]
                    isc, valid, tmp_i = R[7][:, 0:S], R[7][:, S:2 * S], R[7][:, 2 * S:3 * S]
                    wi = stat(4)
                    top = stat(8)
                    dve.do(lambda e, t=t: e.tensor_scalar(wi, kvi[:, t, 448:452], 4 ** -0.5 * HD ** -0.5, None, MUL), after=[pe.last])
                    n = 0
                    for par in range(2):
                        i, bank, readers = work.take()
                        for j in range(2):
                            s = pe.do(lambda e, par=par, j=j, bank=bank, t=t: e.matmul(bank[:, j * S:(j + 1) * S],
                                      aT[64 * par:64 * par + 64, 5 + j, t * P:(t + 1) * P], aT[64 * par:64 * par + 64, 7, :],
                                      start=True, stop=True), after=ready + readers)
                        for j in range(2):
                            h = 2 * j + par
                            dst = isc if n == 0 else tmp_i
                            dve.do(lambda e, dst=dst, j=j, h=h, bank=bank, wi=wi: e.tensor_scalar(dst, bank[:, j * S:(j + 1) * S], 0.0,
                                   wi[:, h:h + 1], MAX, MUL), after=[s])
                            if n:
                                dve.do(lambda e: e.tensor_tensor(isc, isc, tmp_i, ADD))
                            n += 1
                        work.done(i, [dve.last])
                    dve.do(lambda e, pq=pq: e.tensor_scalar(valid, pos_f[:, T:T + S], pq, None, ALU.is_le))
                    dve.do(lambda e: e.tensor_scalar(tmp_i, valid, -1.0, LATER, ADD, MUL))
                    dve.do(lambda e: e.tensor_tensor(isc, isc, valid, MUL))
                    dve.do(lambda e: e.tensor_tensor(isc, isc, tmp_i, ADD))
                    for _ in range(TOPK // 8):
                        dve.do(lambda e, top=top: e.max(top, isc))
                        dve.do(lambda e, top=top: e.match_replace(isc, top, isc, STRUCK))
                    dve.do(lambda e: e.tensor_scalar(isc, isc, STRUCK, None, ALU.is_equal))
                    dve.do(lambda e: e.tensor_tensor(isc, isc, valid, MUL))
                    dve.do(lambda e, t=t: e.tensor_scalar(selmask[:, t * S:(t + 1) * S], isc, -1.0, -NEG, ADD, MUL))
                    yield
                for t in range(T):
                    yield from select(t)
                sel_ready = dve.last

                def scores(h, t, dst, after):
                    par = 64 * (h % 2)
                    pe.do(lambda e: e.matmul(dst, aT[par:par + 64, h // 2, t * P:(t + 1) * P], aT[par:par + 64, 4, :], start=True, stop=False), after=after)
                    return pe.do(lambda e: e.matmul(dst, idbf[:, :], selmask[:, t * S:(t + 1) * S], start=False, stop=True), after=[sel_ready])
                units = [(t, h, 2, 2, scores, S) for t in range(T) for q in range(0, 8, 4) for h in (q, q + 1)]
                yield from attention(units, 8, HD, y_dsa, lambda h, b: kvi[:, b, 64:128], ready + [sel_ready],
                                     [R[9][:, 0:CH], R[9][:, CH:2 * CH]], [R[9][:, 2 * CH:3 * CH], R[9][:, 3 * CH:4 * CH]])
                ready2["dsa"] = [dve.last]
                yield

            ready2 = {}
            y_dsa, y_m = tok(R[10][:, 0:D]), tok(R[10][:, D:2 * D])
            together(itertools.chain(plain(U2, CH, u3, 0, start, h_ready), plain(QM2, CH, qm3, 0, start, h_ready)), sparse())

            def memory():
                free = now()
                dve.do(lambda e: e.tensor_scalar(g_qm, g_qm, 128 ** -0.5, None, MUL), after=[act.last, kmv_ready])
                for t in range(T):
                    jv = R[8][:, 0:CH].rearrange("p (h c) -> p h c", h=4)
                    head_norm(qm3[:, t, :].rearrange("p (h c) -> p h c", h=4), 4, 128, g_qm, jv, after=free)
                    head_norm(kmv[:, t, 0:CH].rearrange("p (h c) -> p h c", h=4), 4, 128, g_km, jv)
                    yield
                qT = R[8][:, 0:D].rearrange("p (h s) -> p h s", h=4)
                kT = R[8][:, D:2 * D].rearrange("p (h s) -> p h s", h=4)
                transpose_scaled(qm3, qT, 4, [dve.last], [dve.last])
                ready = transpose_scaled(kmv[:, :, 0:CH], kT, 4, [dve.last], [])
                yield

                def scores(h, t, dst, after):
                    return pe.do(lambda e: e.matmul(dst, qT[:, h, t * P:(t + 1) * P], kT[:, h, :], start=True, stop=True), after=after)
                units = [(t, h, 2, 1, scores, S) for t in range(T) for h in range(0, 4, 2)]
                yield from attention(units, 4, 128, y_m, lambda h, b: kmv[:, b, CH + h * 128:CH + (h + 1) * 128], ready,
                                     [R[9][:, 0:CH], R[9][:, CH:2 * CH]], [R[9][:, 2 * CH:3 * CH], R[9][:, 3 * CH:4 * CH]])
                ready2["mem"] = [dve.last]
                yield

            def ssm():
                free = now()
                uT = R[4][:, 0:D].rearrange("p (k s) -> p k s", k=4)
                ysT = R[4][:, D:2 * D].rearrange("p (k s) -> p k s", k=4)
                u_ready = transpose_scaled(u3, uT, 4, [act.last], free)
                yield
                for half in range(2):
                    ec = R[half][:, :].rearrange("p (i s) -> p i s", i=8)
                    es = R[2 + half][:, :].rearrange("p (i s) -> p i s", i=8)
                    tm = R[9][:, 0:D].rearrange("p (i s) -> p i s", i=8)
                    dve.do(lambda e, ec=ec: e.memset(ec[:, :, 0:1], 1.0), after=free)
                    dve.do(lambda e, es=es: e.memset(es[:, :, 0:1], 0.0))
                    for j in range(8):
                        m = 1 << j
                        c_, s_ = (bc(w[j][:, 8 * half:8 * half + 8], m) for w in (wc, ws))
                        a_c, a_s, o_c, o_s, tt = ec[:, :, 0:m], es[:, :, 0:m], ec[:, :, m:2 * m], es[:, :, m:2 * m], tm[:, :, 0:m]
                        for o, x1, x2, y1, y2, op in ((o_c, a_c, c_, a_s, s_, SUB), (o_s, a_c, s_, a_s, c_, ADD)):
                            dve.do(lambda e, o=o, x1=x1, x2=x2: e.tensor_tensor(o, x1, x2, MUL))
                            dve.do(lambda e, tt=tt, y1=y1, y2=y2: e.tensor_tensor(tt, y1, y2, MUL))
                            dve.do(lambda e, o=o, tt=tt, op=op: e.tensor_tensor(o, o, tt, op))
                        if j % 4 == 3:
                            yield
                def quarter(k):
                    bcol, ccol = R[9][:, 0:2 * CH], R[9][:, 2 * CH:4 * CH]
                    bcm = [bcol[:, j * CH:(j + 1) * CH].rearrange("p (i c) -> p i c", i=4) for j in range(2)]
                    ccm = [ccol[:, j * CH:(j + 1) * CH].rearrange("p (i c) -> p i c", i=4) for j in range(2)]
                    loaded = sp.load("r9", [(v, d[n][:, 4 * k:4 * k + 4, :]) for v, n in zip(bcm + ccm, ("b_re", "b_im", "c_re", "c_im"))], after=now())
                    half, i0 = k // 2, 4 * (k % 2)
                    ec = R[half][:, :].rearrange("p (i s) -> p i s", i=8)[:, i0:i0 + 4, :]
                    es = R[2 + half][:, :].rearrange("p (i s) -> p i s", i=8)[:, i0:i0 + 4, :]
                    q4 = [R[5][:, 0:D], R[5][:, D:2 * D], R[6][:, 0:D], R[6][:, D:2 * D]]
                    vre, vim, gre, gim = (a.rearrange("p (i s) -> p i s", i=4) for a in q4)
                    tmp = R[8][:, 0:D].rearrange("p (i s) -> p i s", i=4)
                    tmc = R[8][:, D:2 * D].rearrange("p (a i c) -> p a i c", a=2, i=4)
                    free_q = now()
                    for j2 in range(2):
                        got = []
                        for w in range(2):
                            i, bank, readers = work.take()
                            for j in range(2):
                                s = pe.do(lambda e, w=w, j=j, j2=j2, bank=bank, k=k: e.matmul(bank[:, j * S:(j + 1) * S], bcm[w][:, 2 * j2 + j, :], uT[:, k, :],
                                          start=True, stop=True), after=[loaded] + u_ready + readers)
                            got.append((i, bank, s))
                        bre, bim = (g[1][:, :].rearrange("p (i s) -> p i s", i=2) for g in got)
                        sl = slice(2 * j2, 2 * j2 + 2)
                        for o, x1, y1, op in ((vre, bre, bim, ADD), (vim, bim, bre, SUB)):
                            dve.do(lambda e, o=o, x1=x1, sl=sl: e.tensor_tensor(o[:, sl, :], x1, ec[:, sl, :], MUL), after=[got[0][2], got[1][2]] + free_q)
                            dve.do(lambda e, y1=y1, sl=sl: e.tensor_tensor(tmp[:, sl, :], y1, es[:, sl, :], MUL))
                            dve.do(lambda e, o=o, sl=sl, op=op: e.tensor_tensor(o[:, sl, :], o[:, sl, :], tmp[:, sl, :], op))
                        for i, _, _ in got:
                            work.done(i, [dve.last])
                    yield
                    for v, g in ((vre, gre), (vim, gim)):
                        for i in range(4):
                            dve.do(lambda e, v=v, g=g, i=i: e.tensor_tensor_scan(g[:, i, :], rad[:, 4 * k + i:4 * k + i + 1].to_broadcast([P, S]),
                                   v[:, i, :], 0.0, MUL, ADD))
                    for o, x1, y1, op in ((vre, gre, gim, SUB), (vim, gim, gre, ADD)):
                        dve.do(lambda e, o=o, x1=x1: e.tensor_tensor(o, x1, ec, MUL))
                        dve.do(lambda e, y1=y1: e.tensor_tensor(tmp, y1, es, MUL))
                        dve.do(lambda e, o=o, op=op: e.tensor_tensor(o, o, tmp, op))
                    f_r, f_i = (bc(a[:, 4 * k:4 * k + 4], P) for a in (fr5, fi5))
                    dve.do(lambda e: e.tensor_tensor(tmc[:, 0, :, :], ccm[0], f_i, MUL), after=[loaded])
                    dve.do(lambda e: e.tensor_tensor(tmc[:, 1, :, :], ccm[1], f_i, MUL))
                    dve.do(lambda e: e.tensor_tensor(ccm[0], ccm[0], f_r, MUL))
                    dve.do(lambda e: e.tensor_tensor(ccm[1], ccm[1], f_r, MUL))
                    dve.do(lambda e: e.tensor_tensor(ccm[0], ccm[0], tmc[:, 1, :, :], SUB))
                    dve.do(lambda e: e.scalar_tensor_tensor(ccm[1], ccm[1], -1.0, tmc[:, 0, :, :], MUL, SUB))
                    i, bank, readers = work.take()
                    for j in range(4):
                        for w, h in enumerate((vre, vim)):
                            s = pe.do(lambda e, j=j, w=w, h=h, bank=bank: e.matmul(bank[:, 0:S], ccm[w][:, j, :], h[:, j, :],
                                      start=(j == 0 and w == 0), stop=(j == 3 and w == 1)), after=[dve.last] + readers)
                    dcol = small_cols[:, col["d_skip"] + k:col["d_skip"] + k + 1]
                    s = dve.do(lambda e, k=k, bank=bank, dcol=dcol: e.scalar_tensor_tensor(ysT[:, k, :], uT[:, k, :], dcol, bank[:, 0:S], MUL, ADD), after=[s])
                    work.done(i, [s])
                    yield
                for k in range(4):
                    yield from quarter(k)
                yf, g1 = R[4][:, D:2 * D], R[8][:, 0:D]
                dve.do(lambda e: e.tensor_tensor(g1, yf, yf, MUL))
                dve.do(lambda e: e.tensor_scalar(g1, g1, 0.044715, 1.0, MUL, ADD))
                dve.do(lambda e: e.tensor_tensor(g1, g1, yf, MUL))
                a = sigmoid(g1, g1, 2.0 * (2.0 / np.pi) ** 0.5, after=[dve.last])
                dve.do(lambda e: e.tensor_tensor(yf, yf, g1, MUL), after=[a])
                y_ok = dve.last
                w = R[0][:, :].rearrange("p (k n) -> p k n", k=4)
                loaded = sp.load("r0", [(w, d["w_glu"].rearrange("(k p) n -> p k n", p=P))], after=now())
                for k in range(0, 4, 2):
                    i, bank, readers = work.take()
                    for j in range(2):
                        for kk in range(4):
                            s = pe.do(lambda e, j=j, k=k, kk=kk, bank=bank: e.matmul(bank[:, j * S:(j + 1) * S], w[:, kk, (k + j) * P:(k + j + 1) * P], ysT[:, kk, :],
                                      start=(kk == 0), stop=(kk == 3)), after=[y_ok, loaded] + readers)
                    a = sigmoid(g1[:, k * S:(k + 2) * S], bank[:, :], after=[s])
                    work.done(i, [act.last])
                ready2["ssm"] = [dve.do(lambda e: e.tensor_tensor(yf, yf, g1, MUL), after=[s, a])]
                yield

            ysT = R[4][:, D:2 * D].rearrange("p (k s) -> p k s", k=4)

            def mix(i, y, key, w):
                return gated_add(y, 4, w_in[:, GATES2 + i * D:GATES2 + (i + 1) * D], d[w], None, i == 1, ready2[key])

            merged_readers[:] = [pe.last]
            together(mix(1, y_dsa, "dsa", "w_up_dsa"), memory())
            together(mix(2, y_m, "mem", "w_up_mem"), ssm())
            ready2["ssm"] = split(tuple(a[:, 0:4, :] for a in yT), ysT, after=ready2["ssm"] + yT_readers)
            for _ in mix(0, None, "ssm", "w_up_ssm"):
                pass
            out_projection(d["w_out_2"])
            hT_readers[:] = [pe.last]

            h_ready = to_hT(x3, tok(R[0][:, :]), col["g_ffn"], after=[dve.last])
            n_r = NGRP + EXP
            wr = R[1][:, 0:KD * n_r].rearrange("p (k n) -> p k n", k=KD)
            wr_hi, wr_lo = (a[:, 0:KD * n_r].rearrange("p (k n) -> p k n", k=KD) for a in (y_hi, y_lo))
            loaded = sp.load("r1", [(wr[:, :, 0:NGRP], d["w_group"].rearrange("(k p) n -> p k n", p=P)),
                                       (wr[:, :, NGRP:n_r], d["w_expert"].rearrange("(k p) n -> p k n", p=P))], after=now())
            wr_ready = split((wr_hi, wr_lo), wr, after=[loaded] + yT_readers)
            lg, le = stat(T * NGRP), stat(T * EXP)
            lg3, le3 = lg.rearrange("p (t g) -> p t g", t=T), le.rearrange("p (t g) -> p t g", t=T)
            b_i, bank, readers = work.take()
            for t in range(T):
                for k in range(KD):
                    s = product(bank[:, t * n_r:(t + 1) * n_r], tuple(a[:, k, t * P:(t + 1) * P] for a in hT), (wr_hi[:, k, :], wr_lo[:, k, :]),
                                k == 0, k == KD - 1, wr_ready + h_ready + readers)
            lv = bank[:, 0:T * n_r].rearrange("p (t n) -> p t n", t=T)
            dve.do(lambda e: e.tensor_tensor(lg3, lv[:, :, 0:NGRP], b_grp.unsqueeze(1).to_broadcast([P, T, NGRP]), ADD), after=[s])
            s = dve.do(lambda e: e.tensor_tensor(le3, lv[:, :, NGRP:n_r], b_exp.unsqueeze(1).to_broadcast([P, T, EXP]), ADD))
            work.done(b_i, [s])

            def softmax(x, n, m):
                v = x.rearrange("p (a b) -> p a b", b=m)
                red = stat(n)
                dve.do(lambda e: e.tensor_reduce(red, v, AX, MAX))
                dve.do(lambda e: e.tensor_tensor(v, v, bc(red, m), SUB))
                a = act.do(lambda e: e.activation(x, x, ACT.Exp), after=[dve.last])
                dve.do(lambda e: e.tensor_reduce(red, v, AX, ADD), after=[a])
                dve.do(lambda e: e.reciprocal(red, red))
                dve.do(lambda e: e.tensor_tensor(v, v, bc(red, m), MUL))
            softmax(lg, T, NGRP)
            softmax(le, T * NGRP, EPG)

            def first_of_highest(x3_, m, top, hot):
                order = consts[:, 1056:1056 + m].unsqueeze(1).to_broadcast([P, T, m])
                key = stat(T)
                dve.do(lambda e: e.tensor_reduce(top, x3_, AX, MAX))
                dve.do(lambda e: e.tensor_tensor(hot, x3_, bc(top, m), ALU.is_equal))
                dve.do(lambda e: e.tensor_tensor(hot, hot, order, MUL))
                dve.do(lambda e: e.tensor_reduce(key, hot, AX, MAX))
                dve.do(lambda e: e.tensor_tensor(hot, hot, bc(key, m), ALU.is_equal))
            g_gate, g_hot = stat(T), stat(T * NGRP)
            g_hot3 = g_hot.rearrange("p (t g) -> p t g", t=T)
            first_of_highest(lg3, NGRP, g_gate, g_hot3)
            pr, ep = stat(T * EXP), stat(T * EPG)
            le4 = le.rearrange("p (a b) -> p a b", b=EPG)
            dve.do(lambda e: e.tensor_tensor(pr.rearrange("p (a b) -> p a b", b=EPG), le4, bc(g_hot, EPG), MUL))
            ep3 = ep.rearrange("p (t b) -> p t b", t=T)
            pr4 = pr.rearrange("p (t g b) -> p t g b", t=T, g=NGRP)
            dve.do(lambda e: e.tensor_tensor(ep3, pr4[:, :, 0, :], pr4[:, :, 1, :], ADD))
            for g in (2, 3):
                dve.do(lambda e, g=g: e.tensor_tensor(ep3, ep3, pr4[:, :, g, :], ADD))
            top1, top2, hot1, hot2, tot = stat(T), stat(T), stat(T * EPG), stat(T * EPG), stat(T)
            h1, h2 = (a.rearrange("p (t b) -> p t b", t=T) for a in (hot1, hot2))
            first_of_highest(ep3, EPG, top1, h1)
            dve.do(lambda e: e.scalar_tensor_tensor(ep, hot1, -2.0, ep, MUL, ADD))
            first_of_highest(ep3, EPG, top2, h2)
            dve.do(lambda e: e.tensor_tensor(tot, top1, top2, ADD))
            dve.do(lambda e: e.reciprocal(tot, tot))
            dve.do(lambda e: e.tensor_tensor(tot, tot, g_gate, MUL))
            dve.do(lambda e: e.tensor_tensor(top1, top1, tot, MUL))
            dve.do(lambda e: e.tensor_tensor(top2, top2, tot, MUL))
            dve.do(lambda e: e.tensor_tensor(h1, h1, bc(top1, EPG), MUL))
            dve.do(lambda e: e.tensor_tensor(h2, h2, bc(top2, EPG), MUL))
            dve.do(lambda e: e.tensor_tensor(h1, h1, h2, ADD))
            comb = pr
            comb4 = pr4
            for t in range(T):
                for g in range(NGRP):
                    dve.do(lambda e, t=t, g=g: e.tensor_scalar(comb4[:, t, g, :], h1[:, t, :], g_hot3[:, t, g:g + 1], None, MUL))
            comb3 = comb.rearrange("p (t e) -> p t e", t=T)

            free = now()
            hid_ring = Ring([tuple(a[:, i * D:(i + 1) * D] for a in (y_hi, y_lo)) for i in range(2)])
            hid_ring.readers = [free, free]
            act_ring = Ring([R[2][:, 0:D], R[2][:, D:2 * D]])
            act_ring.readers = [free, free]

            def up(x):
                ai, hid, areaders = act_ring.take()
                hi_i, pair, hreaders = hid_ring.take()
                for w_name in ("w_gate", "w_up"):
                    out = [bulk.take() for _ in range(2)]
                    for k0 in range(0, KD, PK):
                        i, hi, lo, ready = piece(d[w_name][x][k0 * P:(k0 + PK) * P, :], FF)
                        for jj, (b, bank, readers) in enumerate(out):
                            for j in range(2):
                                cols = slice((2 * jj + j) * P, (2 * jj + j + 1) * P)
                                for k in range(PK):
                                    s = product(bank[:, j * S:(j + 1) * S], (hi[:, k, cols], lo[:, k, cols]), tuple(a[:, k0 + k, :] for a in hT),
                                                k0 + k == 0 and j == 0, k0 + k == KD - 1, ready + readers + h_ready, shared=True)
                            if k0 + PK == KD:
                                part = hid[:, jj * CH:(jj + 1) * CH]
                                if w_name == "w_gate":
                                    a = act.do(lambda e, part=part, bank=bank: e.activation(part, bank[:, :], ACT.Silu), after=[s] + areaders)
                                else:
                                    a = dve.do(lambda e, part=part, bank=bank: e.tensor_tensor(part, part, bank[:, :], MUL), after=[s, gated])
                                bulk.done(b, [a])
                        sring.done(i, [s])
                    gated = act.last
                done = split(pair, hid, after=[dve.last] + hreaders)
                act_ring.done(ai, done)
                return hi_i, tuple(a.rearrange("p (j s) -> p j s", j=4) for a in pair), done

            def down(x, hi_i, hid, ready):
                for n0 in range(0, D, CH):
                    def add(t, bank, step):
                        dst, cw = m3[:, t, n0:n0 + CH], comb3[:, t, x:x + 1]
                        if x == 0:
                            return [dve.do(lambda e: e.tensor_scalar(dst, bank[:, :], cw, None, MUL), after=[step] + free)]
                        return [dve.do(lambda e: e.scalar_tensor_tensor(dst, bank[:, :], cw, dst, MUL, ADD), after=[step])]
                    for _ in project(hid, d["w_down"][x][:, n0:n0 + CH], FF, CH, add, after=ready, banks=down_banks):
                        pass
                hid_ring.done(hi_i, [pe.last])
            down_banks = Ring(banks[4:8])
            down_banks.readers = [now() for _ in range(4)]
            pending = None
            for x in range(EXP):
                got = up(x)
                if pending is not None:
                    down(x - 1, *pending)
                pending = got
            down(EXP - 1, *pending)
            stores = []
            for t in range(T):
                s = dve.do(lambda e, t=t: e.tensor_tensor(x3[:, t, :], x3[:, t, :], m3[:, t, :], ADD))
                stores.append((out[t * P:(t + 1) * P, :], x3[:, t, :]))
            return sp.load("out", stores, after=[s])

        rows2 = sb("rows2", 64 * 2 + 128 * 2 + NGRP + EXP)
        selmask = sb("selected_mask", T * S, BF16)
        marks = [(lane, len(lane.queue), lane.last) for lane in (pe, dve, act, pool)]
        loads_mark, sem_marks = len(sp.queue), {n: e[1] for n, e in sp.sems.items()}
        for walk[0] in range(2):
            for lane, n, last in marks:
                del lane.queue[n:]
                lane.last = last
            del sp.queue[loads_mark:]
            for n, e in sp.sems.items():
                e[1] = sem_marks.get(n, 0)
            for ring in (wring, sring, bring, bulk, work, mixed, scr):
                ring.at, ring.readers = 0, [[] for _ in ring.slots]
            hT_readers[:], yT_readers[:], merged_readers[:] = [], [], []
            for l in range(LAYERS):
                layer(l)
            final = second()
        for lane in (pe, dve, act, pool):
            lane.count()
        block = ctx.enter_context(nc.Block())

        @block.sync
        def _(e):
            sp.emit(e)
            e.wait_ge(final.sem, final.value)

        @block.tensor
        def _(e):
            pe.emit(e)

        @block.vector
        def _(e):
            dve.emit(e)

        @block.scalar
        def _(e):
            act.emit(e)

        @block.gpsimd
        def _(e):
            pool.emit(e)




def shape_constants():
    i = np.arange(P)
    c = np.zeros((P, 1408), np.float32)
    c[:, 0:128] = np.eye(P)
    c[:, 128:256] = i[:, None] <= i[None, :]
    c[:, 256:384] = 1.0
    c[:, 384:512] = i[:, None] > i[None, :]
    c[:, 512:640] = np.where(i[:, None] >= i[None, :], 0.0, NEG)
    c[:, 640:768] = np.where(i[None, :] > i[:, None], 0.0, NEG)
    c[:, 768:896] = np.where(i[:, None] >= i[None, :], 0.0, NEG)
    pos = np.arange(S, dtype=np.float32)
    inv = (np.float32(10000.0) ** (-np.arange(0, HD, 2, dtype=np.float32) / np.float32(HD))).astype(np.float32)
    ang = pos[:, None] * inv[None, :]
    for t in range(T):
        c[:, 896 + 32 * t:928 + 32 * t] = np.cos(ang[t * P:(t + 1) * P])
        c[:, 960 + 32 * t:992 + 32 * t] = np.sin(ang[t * P:(t + 1) * P])
    c[:, 1024:1056] = 1.0 / (np.float32(10000.0) ** (np.arange(0, HD, 2, dtype=np.float32) / np.float32(HD)))
    c[:, 1056:1064] = np.arange(8, 0, -1)
    return c


def kernel(**inputs):
    import concourse.bacc as bacc
    from concourse.bass_utils import run_bass_kernel_spmd as run

    nc = bacc.Bacc("TRN2", target_bir_lowering=False, num_devices=1,
                   dynamic_dma_scratch_size=1024)
    a = {k: np.asarray(v) for k, v in inputs.items()}
    cols, at = [], []

    def add(v):
        c0 = sum(x.shape[1] for x in cols)
        cols.append(v.reshape(-1, P).T)
        return c0
    for l in range(LAYERS):
        e = {"norm": add(a["norm_w"][l])}
        e["conv"] = [add(a["conv_w"][l][w]) for w in range(CONV_W)][0]
        e["conv_b"], e["ssm_norm"] = add(a["conv_b"][l]), add(a["ssm_norm_w"][l])
        at.append(e)
    e = {n: add(a[n + "_2"][0]) for n in ("g_mem", "g_mix", "g_ffn", "lam_re", "lam_im", "d_skip")}
    e["log_dt"] = add(np.repeat(a["log_dt_2"][0], SN))
    at.append(e)
    rows, rat = [], []

    def addr(v):
        r0 = sum(len(x) for x in rows)
        rows.append(v.reshape(-1))
        return r0
    for l in range(LAYERS):
        rat.append(addr(a["dt_bias"][l]))
        for n in ("a_log", "d_skip", "sinks", "f_bias", "gate_bias"):
            addr(a[n][l])
    e = {"final": addr(a["final_norm_w"]), "small": addr(a["g_q_2"][0])}
    for n in ("g_k_2", "g_qm_2", "g_km_2", "b_group_2", "b_expert_2"):
        addr(a[n][0])
    rat.append(e)
    b_pad, c_pad = {}, {}
    for part in ("re", "im"):
        b, c = a["b_" + part + "_2"][0], a["c_" + part + "_2"][0]
        bp, cp = np.zeros((P, ST, P), np.float32), np.zeros((P, ST, P), np.float32)
        for g in range(SG):
            i, g2 = divmod(g, 2)
            ch, st = 32 * (i % 4) + SH * g2, SN * g2
            bp[ch:ch + SH, i, st:st + SN] = b[g].T
            cp[st:st + SN, i, ch:ch + SH] = c[g].T
        b_pad[part], c_pad[part] = bp, cp
    arrays = {"x": a["x"][0], "w_in": a["w_in"], "w_proj": a["w_proj"], "w_out": a["w_out"],
              "consts": shape_constants(), "cols": np.concatenate(cols, 1), "rows": np.concatenate(rows)[None, :],
              "b_re": b_pad["re"], "b_im": b_pad["im"], "c_re": c_pad["re"], "c_im": c_pad["im"],
              "mem": a["mem_2"][0], "pos": a["positions_2"],
              "pos_col": a["positions_2"].reshape(T, P).T}
    for n in ("w_in", "w_out"):
        arrays[n + "_2"] = a[n + "_2"][0]
    for n in ("w_mem_kv", "w_glu", "w_up_ssm", "w_up_dsa", "w_up_mem", "w_group", "w_expert", "w_gate", "w_up", "w_down"):
        arrays[n] = a[n + "_2"][0]
    feed, d = {}, {}
    for n, v in arrays.items():
        v = np.ascontiguousarray(v)
        feed["in_" + n] = v
        d[n] = nc.dram_tensor("in_" + n, v.shape, mybir.dt.from_np(v.dtype), kind="ExternalInput").ap()
    d["cols_at"], d["rows_at"] = at, rat
    out = nc.dram_tensor("out_x", (S, D), F32, kind="ExternalOutput").ap()
    build(nc, d, out)
    r = run(nc, [feed], core_ids=[0])
    return r.results[0]["out_x"].reshape(1, S, D)
```

```python
from contextlib import ExitStack

import itertools

import numpy as np

import concourse.bass as bass
from concourse import mybir

F32 = mybir.dt.float32
F32R = mybir.dt.float32r
BF16 = mybir.dt.bfloat16
I32 = mybir.dt.int32
ALU = mybir.AluOpType
ACT = mybir.ActivationFunctionType
AX = mybir.AxisListType.X
ADD, SUB, MUL, MAX, MIN = ALU.add, ALU.subtract, ALU.mult, ALU.max, ALU.min

P = 128
D = 1024
S = 256
T = S // P
KD = D // P
TURNS = 0.15915494309189535
ROUND = 12582912.0
PI, HALF_PI = 3.1415925, 1.5707963267948966
TWO_PI = (6.28125, 0.0019350051879882812, 3.019916050561733e-07)
LATER, STRUCK = 1e37, -1e38
LAYERS = 2
AHEAD = 3
PK = 2
CH = 512
EPS = 1e-6
NEG = -1e30

XBC, ZA, DT, KV, ZB = 0, 2048, 3072, 4112, 4624
QB, CQ, CK, CV, CF, CZ, GATES = 3088, 5648, 6672, 7696, 8720, 8736, 9760
N_IN = GATES + 3 * D
HEADS, HD = 16, 64
KVH = 4
GROUPS, RPG = 4, 4
CONV_W = 4

U2, Q2, KVI2, QM2, GATES2 = 0, 512, 1024, 1476, 1988
N_IN2 = GATES2 + 3 * D
SG, SH, SN = 32, 16, 64
ST = SG * SN // P
TOPK = min(256, S // 4)
EXP, FF = 32, 512
NGRP, EPG = 4, 8


class Step:

    def __init__(self, sem, value=None):
        self.sem, self.value, self.needed = sem, value, False


class Lane:

    def __init__(self, sem, chained):
        self.sem, self.chained, self.queue, self.last = sem, chained, [], None

    def do(self, emit, after=()):
        after = [s for s in after if s is not None]
        if self.chained and self.last is not None:
            after.append(self.last)
        step = Step(self.sem)
        for s in after:
            s.needed = True
        self.queue.append((emit, after, step))
        self.last = step
        return step

    def count(self):
        n = 0
        for _, _, step in self.queue:
            if step.needed and step.value is None:
                n += 1
                step.value = n

    def emit(self, engine):
        seen = {}
        for emit, after, step in self.queue:
            for s in after:
                if seen.get(s.sem.name, 0) < s.value:
                    engine.wait_ge(s.sem, s.value)
                    seen[s.sem.name] = s.value
            made = emit(engine)
            if step.needed and step.sem is self.sem:
                made.then_inc(self.sem, 1)


class Loads:

    def __init__(self, new_sem):
        self.new_sem, self.queue, self.sems = new_sem, [], {}

    def load(self, name, pairs, after=()):
        if name not in self.sems:
            self.sems[name] = [self.new_sem("dma_" + name), 0]
        entry = self.sems[name]
        after = [s for s in after if s is not None]
        for s in after:
            s.needed = True
        for out, src in pairs:
            entry[1] += 16
            self.queue.append((out, src, after, entry[0]))
        return Step(entry[0], entry[1])

    def emit(self, engine):
        seen = {}
        for out, src, after, sem in self.queue:
            for s in after:
                if seen.get(s.sem.name, 0) < s.value:
                    engine.wait_ge(s.sem, s.value)
                    seen[s.sem.name] = s.value
            engine.dma_start(out, src).then_inc(sem, 16)


class Ring:

    def __init__(self, slots):
        self.slots, self.readers, self.at = slots, [[] for _ in slots], 0
        self.open = [False] * len(slots)

    def take(self):
        i = self.at % len(self.slots)
        self.at += 1
        if self.open[i]:
            raise ValueError("a slot is taken again before its last use was noted")
        self.open[i] = True
        return i, self.slots[i], self.readers[i]

    def done(self, i, steps):
        self.readers[i] = list(steps)
        self.open[i] = False


def bc(ap, n):
    return ap.unsqueeze(2).to_broadcast([ap.shape[0], ap.shape[1], n])


def build(nc, d, out):
    ctx = ExitStack()
    with ctx:
        def sb(name, cols, dt=F32):
            return ctx.enter_context(nc.sbuf_tensor(name, [P, cols], dt))

        def sem(name):
            return ctx.enter_context(nc.semaphore(name))

        pe, dve, act, pool = Lane(sem("pe"), False), Lane(sem("dve"), True), Lane(sem("act"), True), Lane(sem("pool"), True)
        sp = Loads(sem)

        consts = sb("consts", 1408)
        small_cols = sb("small_cols", d["cols"].shape[1])
        x_t = sb("x", T * D)
        h_hi, h_lo = sb("h_hi", KD * S, F32R), sb("h_lo", KD * S, F32R)
        y_hi, y_lo = sb("y_hi", KD * S, F32R), sb("y_lo", KD * S, F32R)
        merged = sb("merged", T * D)
        R = [sb(f"r{i}", T * D) for i in range(11)]
        wslots = [sb(f"w{i}", PK * CH) for i in range(6)]
        wsplit = [(sb(f"w_hi{i}", PK * CH, F32R), sb(f"w_lo{i}", PK * CH, F32R)) for i in range(4)]
        bias_slots = [sb(f"bias{i}", CH) for i in range(2)]
        small = sb("small", 1600)
        rows = sb("rows", 320)
        scratch = [sb(f"scratch{i}", CH) for i in range(4)]
        idbf = sb("ident_bf16", P, BF16)
        maskbf = sb("masks_bf16", 3 * P, BF16)
        banks = [ctx.enter_context(nc.psum_tensor(f"bank{i}", [P, CH], F32)) for i in range(8)]

        ident, upto, ones_gt = consts[:, 0:128], consts[:, 128:256], consts[:, 256:512]
        ones, above = consts[:, 256:384], consts[:, 384:512]
        causal01 = consts[:, 128:256]
        cosT = consts[:, 896:960].rearrange("p (t f) -> p t f", t=T)
        sinT = consts[:, 960:1024].rearrange("p (t f) -> p t f", t=T)
        x3 = x_t[:, :].rearrange("p (t c) -> p t c", t=T)
        m3 = merged[:, :].rearrange("p (t c) -> p t c", t=T)
        hT = tuple(a[:, :].rearrange("p (k s) -> p k s", k=KD) for a in (h_hi, h_lo))
        yT = tuple(a[:, :].rearrange("p (k s) -> p k s", k=KD) for a in (y_hi, y_lo))

        wring, sring, bring = Ring(wslots), Ring(wsplit), Ring(bias_slots)
        bulk = Ring(banks[0:4])
        work = Ring(banks[4:7])
        mixed = Ring(banks[7:8])
        scr, gates = Ring(scratch[0:2]), Ring(scratch[2:4])

        cursor = [0]

        def stat(n):
            if cursor[0] + n > 1600:
                raise ValueError("statistics area is full")
            a = small[:, cursor[0]:cursor[0] + n]
            cursor[0] += n
            return a

        def now():
            return [l.last for l in (pe, dve, act, pool) if l.last is not None]

        def tok(ap):
            return ap.rearrange("p (t c) -> p t c", t=T)

        walk = [0]
        const_in = sp.load("consts", [(consts[:, 0:1408], d["consts"]), (small_cols[:, :], d["cols"])])
        x_in = sp.load("x", [(x_t[:, t * D:(t + 1) * D], d["x"][t * P:(t + 1) * P, :]) for t in range(T)])
        maskbf_made = dve.do(lambda v: v.tensor_copy(maskbf[:, 0:3 * P], consts[:, 512:896]), after=[const_in])
        dve.do(lambda v: v.tensor_copy(idbf[:, :], ident))
        causal_mask, window_mask = maskbf[:, 0:P], maskbf[:, P:3 * P]

        def rsqrt(r, v, scale, tmp):
            dve.do(lambda e: e.tensor_scalar(v, v, scale, EPS, MUL, ADD))
            s = act.do(lambda e: e.activation(r, v, ACT.Ln), after=[dve.last])
            s = act.do(lambda e: e.activation(r, r, ACT.Exp, scale=-0.5))
            for _ in range(2):
                dve.do(lambda e: e.tensor_tensor(tmp, r, r, MUL), after=[s])
                dve.do(lambda e: e.tensor_tensor(tmp, tmp, v, MUL))
                dve.do(lambda e: e.tensor_scalar(tmp, tmp, -0.5, 1.5, MUL, ADD))
                s = dve.do(lambda e: e.tensor_tensor(r, r, tmp, MUL))
            return s

        def sigmoid(dst, src, scale=1.0, after=()):
            a = act.do(lambda e: e.activation(dst, src, ACT.Tanh, scale=0.5 * scale), after=after)
            return dve.do(lambda e: e.tensor_scalar(dst, dst, 0.5, 0.5, MUL, ADD), after=[a])

        def log1p_exp_neg_abs(r, x, z, q, after=()):
            dve.do(lambda e: e.scalar_tensor_tensor(r, x, -1.0, x, MUL, MAX), after=after)
            s = act.do(lambda e: e.activation(r, r, ACT.Exp, scale=-1.0), after=[dve.last])
            dve.do(lambda e: e.tensor_scalar(z, r, 2.0, None, ADD), after=[s])
            dve.do(lambda e: e.reciprocal(z, z))
            dve.do(lambda e: e.tensor_tensor(r, r, z, MUL))
            dve.do(lambda e: e.tensor_tensor(z, r, r, MUL))
            dve.do(lambda e: e.tensor_scalar(q, z, 1.0 / 17, None, MUL))
            for n in (15, 13, 11, 9, 7, 5, 3):
                dve.do(lambda e, n=n: e.scalar_tensor_tensor(q, q, 1.0 / n, z, ADD, MUL))
            dve.do(lambda e: e.scalar_tensor_tensor(q, q, 1.0, r, ADD, MUL))
            return dve.do(lambda e: e.tensor_scalar(r, q, 2.0, None, MUL))

        def transposes(blocks, emit_out, after=(), width=4):
            for b0 in range(0, len(blocks), width):
                part = blocks[b0:b0 + width]
                i, bank, readers = work.take()
                for j, blk in enumerate(part):
                    c = blk.shape[1]
                    s = pe.do(lambda e, j=j, blk=blk, c=c, bank=bank: e.transpose(
                        bank[0:c, j * P:(j + 1) * P], blk, ident), after=list(after) + readers)
                work.done(i, emit_out(b0, len(part), bank, s))

        def rms_factor(src3, after=()):
            parts, ss, r, tmp = stat(2 * T), stat(T), stat(T), stat(T)
            i, squares, readers = scr.take()
            for t in range(T):
                for h in range(2):
                    s = act.do(lambda e, t=t, h=h: e.activation(squares[:, :], src3[:, t, h * CH:(h + 1) * CH], ACT.Square,
                               accum_out=parts[:, 2 * t + h:2 * t + h + 1]), after=list(after) + readers)
            scr.done(i, [s])
            dve.do(lambda e: e.tensor_reduce(ss, parts.rearrange("p (t h) -> p t h", h=2), AX, ADD), after=[s])
            return r, rsqrt(r, ss, 1.0 / D, tmp)

        def split(pair, src, after=()):
            hi, lo = pair
            a = act.do(lambda e: e.copy(hi, src), after=after)
            return [a, dve.do(lambda e: e.tensor_tensor(lo, src, hi.bitcast(F32), SUB), after=[a] + list(after))]

        def transpose_split(y3, pair, n_k, ready, free, col0=None):
            blocks = [y3[:, t, k * P:(k + 1) * P] for t in range(T) for k in range(n_k)]
            width = min(4, n_k)

            def copy_out(b0, n, bank, step):
                t, k = divmod(b0, n_k)
                dst = tuple(p[:, k:k + n, t * P:(t + 1) * P] for p in pair)
                src = bank[:, 0:n * P].rearrange("p (k s) -> p k s", k=n)
                if col0 is None:
                    return split(dst, src, after=[step] + free)
                i, tmp, readers = scr.take()
                tmp3 = tmp[:, 0:n * P].rearrange("p (k s) -> p k s", k=n)
                s = dve.do(lambda e: e.tensor_tensor(tmp3, src, bc(small_cols[:, col0 + k:col0 + k + n], P), MUL),
                           after=[step, const_in] + readers)
                done = split(dst, tmp3, after=[s] + free)
                scr.done(i, done)
                return [s]
            transposes(blocks, copy_out, after=ready, width=width)
            return [act.last, dve.last]

        def normalize(src3, normed3, after=(), free=()):
            r, s = rms_factor(src3, after)
            for t in range(T):
                s = dve.do(lambda e, t=t: e.tensor_scalar(normed3[:, t, :], src3[:, t, :], r[:, t:t + 1], None, MUL), after=free)
            return s

        def to_hT(src3, normed3, col0, after=()):
            s = normalize(src3, normed3, after)
            return transpose_split(normed3, hT, KD, [s], hT_readers, col0)

        hT_readers, yT_readers = [], []

        order, fetched, made = [], [], [0]

        def piece(src, n):
            if walk[0] == 0:
                order.append((src, n))
                return fetch(src, n)
            while made[0] < len(order) and len(fetched) <= AHEAD:
                fetched.append(fetch(*order[made[0]]))
                made[0] += 1
            return fetched.pop(0)

        def fetch(src, n):
            i, slot, readers = wring.take()
            raw = slot[:, 0:PK * n].rearrange("p (k n) -> p k n", k=PK)
            loaded = sp.load(f"w{i}", [(raw, src.rearrange("(k p) n -> p k n", p=P))], after=readers)
            j, (hi, lo), sreaders = sring.take()
            hi, lo = (a[:, 0:PK * n].rearrange("p (k n) -> p k n", k=PK) for a in (hi, lo))
            a = act.do(lambda e: e.copy(hi, raw), after=[loaded] + sreaders)
            done = [a, pool.do(lambda e: e.tensor_tensor(lo, raw, hi.bitcast(F32), SUB), after=[a])]
            wring.done(i, done)
            return j, hi, lo, done

        def product(out, stat_pair, mov_pair, first, last, after, shared=False):
            (sh, sl), (mh, ml) = stat_pair, mov_pair
            pe.do(lambda e: e.matmul(out, sh, mh, start=first, stop=False, skip_group_check=shared), after=after)
            pe.do(lambda e: e.matmul(out, sh, ml, start=False, stop=False, skip_group_check=shared))
            return pe.do(lambda e: e.matmul(out, sl, mh, start=False, stop=last, skip_group_check=shared))

        def project(lhsT, src, rows_n, n, copy_out, after=(), bias=None, banks=None):
            k_n = rows_n // P
            banks = bulk if banks is None else banks
            out = [banks.take() for t in range(T)]
            if bias is not None:
                bi, brow, breaders = bring.take()
                b_in = sp.load(f"bias{bi}", [(brow[0:1, 0:n], bias)], after=breaders)
                for i, bank, readers in out:
                    s = pe.do(lambda e, bank=bank: e.matmul(bank[:, 0:n], ones[0:1, :], brow[0:1, 0:n],
                              start=True, stop=False), after=[b_in, const_in] + readers)
                bring.done(bi, [s])
            for k0 in range(0, k_n, PK):
                j, hi, lo, ready = piece(src[k0 * P:(k0 + PK) * P, :], n)
                for t, (i, bank, readers) in enumerate(out):
                    for k in range(PK):
                        kk = k0 + k
                        s = product(bank[:, 0:n], tuple(a[:, kk, t * P:(t + 1) * P] for a in lhsT), (hi[:, k, :], lo[:, k, :]),
                                    kk == 0 and bias is None, kk == k_n - 1, ready + readers + list(after))
                    if k0 + PK == k_n:
                        banks.done(i, copy_out(t, bank, s))
                sring.done(j, [s])
                yield

        def silu_to(dst3, c0, n, free):
            def f(t, bank, step):
                i, e_t, readers = scr.take()
                s = sigmoid(e_t[:, 0:n], bank[:, 0:n], after=[step, const_in] + readers)
                s = dve.do(lambda e: e.tensor_tensor(dst3[:, t, c0:c0 + n], bank[:, 0:n], e_t[:, 0:n], MUL), after=[s] + free)
                scr.done(i, [s])
                return [s]
            return f

        def plain_to(dst3, c0, n, free, scale=None):
            def f(t, bank, step):
                if scale is None:
                    return [act.do(lambda e: e.copy(dst3[:, t, c0:c0 + n], bank[:, 0:n]), after=[step] + free)]
                return [act.do(lambda e: e.mul(dst3[:, t, c0:c0 + n], bank[:, 0:n], scale), after=[step] + free)]
            return f

        def gated_add(y3, ky, wg, wp, bias_row, first, y_ready, col0=None):
            yk = tuple(a[:, 0:ky, :] for a in yT)
            if y3 is not None:
                y_ready = transpose_split(y3, yk, ky, y_ready, list(yT_readers), col0)
            for n0 in range(0, D, CH):
                sig = {}

                def gate_out(t, bank, step):
                    i, e_t, readers = gates.take()
                    s = sigmoid(e_t[:, :], bank[:, :], after=[step] + readers)
                    sig[t] = (i, e_t, s)
                    return [s]

                def branch_out(t, bank, step):
                    i, e_t, sg = sig[t]
                    dst = m3[:, t, n0:n0 + CH]
                    if first:
                        s = dve.do(lambda e: e.tensor_tensor(dst, bank[:, :], e_t[:, :], MUL), after=[step, sg] + merged_readers)
                        gates.done(i, [s])
                        return [s]
                    s0 = dve.do(lambda e: e.tensor_tensor(e_t[:, :], bank[:, :], e_t[:, :], MUL), after=[step, sg])
                    s = dve.do(lambda e: e.tensor_tensor(dst, dst, e_t[:, :], ADD))
                    gates.done(i, [s])
                    return [s0]
                yield from project(hT, wg[:, n0:n0 + CH], D, CH, gate_out,
                                   bias=None if bias_row is None else bias_row[:, n0:n0 + CH])
                yield from project(yk, wp[:, n0:n0 + CH], ky * P, CH, branch_out, after=y_ready)
                yT_readers[:] = [pe.last]

        merged_readers = []

        def out_projection(w):
            ready = transpose_split(m3, yT, KD, [dve.last], list(yT_readers))
            merged_readers[:] = [pe.last]
            for n0 in range(0, D, CH):
                def add(t, bank, step):
                    dst = x3[:, t, n0:n0 + CH]
                    return [dve.do(lambda e: e.tensor_tensor(dst, dst, bank[:, :], ADD), after=[step])]
                yield from project(yT, w[:, n0:n0 + CH], D, CH, add, after=ready)
            yT_readers[:] = [pe.last]

        def transpose_scaled(y3, yT, n_k, ready, free, col0=None):
            blocks = [y3[:, t, k * P:(k + 1) * P] for t in range(T) for k in range(n_k)]
            width = min(4, n_k)

            def copy_out(b0, n, bank, step):
                t, k = divmod(b0, n_k)
                dst = yT[:, k:k + n, t * P:(t + 1) * P]
                src = bank[:, 0:n * P].rearrange("p (k s) -> p k s", k=n)
                if col0 is None:
                    return [act.do(lambda e: e.copy(dst, src), after=[step] + free)]
                return [dve.do(lambda e: e.tensor_tensor(dst, src, bc(small_cols[:, col0 + k:col0 + k + n], P), MUL),
                               after=[step] + free)]
            transposes(blocks, copy_out, after=ready, width=width)
            return [act.last if col0 is None else dve.last]

        def attention(units, n_heads, dv, y3, v_of, ready, p_buf, pT_buf, sink=None, gated=False):
            mx_all, sum_all = stat(T * n_heads), stat(T * n_heads)
            pring, ptring = Ring(p_buf), Ring(pT_buf)
            outs, filled = {}, {}
            per_bank = CH // dv
            state = []

            def stage_scores(u):
                t, h0, hn, hs, scores, keys = u
                i, bank, readers = work.take()
                for j in range(hn):
                    s = scores(h0 + j * hs, t, bank[:, j * keys:(j + 1) * keys], list(ready) + readers)
                c = t * n_heads + h0
                mx = mx_all[:, c:c + hs * (hn - 1) + 1:hs]
                s = dve.do(lambda e: e.tensor_reduce(mx, bank[:, 0:hn * keys].rearrange("p (h k) -> p h k", h=hn), AX, MAX), after=[s])
                if sink is not None:
                    dve.do(lambda e: e.tensor_tensor(mx, mx, sink[:, h0:h0 + hs * (hn - 1) + 1:hs], MAX))
                s = dve.do(lambda e: e.tensor_scalar(mx, mx, -1.0, None, MUL))
                pi, p, preaders = pring.take()
                for j in range(hn):
                    a = act.do(lambda e, j=j: e.activation(p[:, j * keys:(j + 1) * keys], bank[:, j * keys:(j + 1) * keys], ACT.Exp,
                               bias=mx[:, j:j + 1], accum_out=sum_all[:, c + j * hs:c + j * hs + 1]), after=[s] + preaders)
                work.done(i, [a])
                return pi, p, a

            def stage_transpose(u, pi, p, a):
                t, h0, hn, hs, scores, keys = u
                kb = keys // P
                n = hn * kb
                i, bank, readers = work.take()
                for j in range(n):
                    s = pe.do(lambda e, j=j: e.transpose(bank[:, j * P:(j + 1) * P], p[:, j * P:(j + 1) * P], ident), after=[a] + readers)
                pring.done(pi, [s])
                ti, pT, treaders = ptring.take()
                s = act.do(lambda e: e.copy(pT[:, 0:n * P], bank[:, 0:n * P]), after=[s] + treaders)
                work.done(i, [s])
                return ti, pT, s

            def stage_pv(u, ti, pT, ready_pT):
                t, h0, hn, hs, scores, keys = u
                kb = keys // P
                for j in range(hn):
                    h = h0 + j * hs
                    key = (t, h // per_bank)
                    if key not in outs:
                        outs[key] = mixed.take()
                        filled[key] = 0
                    i, bank, readers = outs[key]
                    c = (h % per_bank) * dv
                    for b in range(kb):
                        s = pe.do(lambda e, j=j, b=b, bank=bank, c=c, h=h: e.matmul(
                            bank[:, c:c + dv], pT[:, (j * kb + b) * P:(j * kb + b + 1) * P], v_of(h, b),
                            start=(b == 0), stop=(b == kb - 1)), after=[ready_pT] + readers)
                    filled[key] += 1
                    if filled[key] == min(per_bank, n_heads):
                        first = h // per_bank * per_bank
                        finish(t, first, first + filled[key], i, bank, s)
                ptring.done(ti, [s])

            def finish(t, h0, h1, i, bank, s):
                c = t * n_heads
                sm, mx = sum_all[:, c + h0:c + h1], mx_all[:, c + h0:c + h1]
                n = h1 - h0
                if sink is not None:
                    es = stat(n)
                    dve.do(lambda e: e.tensor_tensor(es, sink[:, h0:h1], mx, ADD))
                    a = act.do(lambda e: e.activation(es, es, ACT.Exp), after=[dve.last])
                    dve.do(lambda e: e.tensor_tensor(sm, sm, es, ADD), after=[a])
                dve.do(lambda e: e.reciprocal(sm, sm), after=[act.last])
                dst = y3[:, t, h0 * dv:h1 * dv]
                dst3 = dst.rearrange("p (h c) -> p h c", h=n)
                if gated:
                    dve.do(lambda e: e.tensor_tensor(dst3, dst3, bc(sm, dv), MUL))
                    s = dve.do(lambda e: e.tensor_tensor(dst, dst, bank[:, 0:n * dv], MUL), after=[s])
                else:
                    s = dve.do(lambda e: e.tensor_tensor(dst3, bank[:, 0:n * dv].rearrange("p (h c) -> p h c", h=n),
                               bc(sm, dv), MUL), after=[s])
                mixed.done(i, [s])

            a1, a2 = {}, {}
            n = len(units)
            for i in range(n + 2):
                if i < n:
                    a1[i] = stage_scores(units[i])
                if 1 <= i <= n:
                    a2[i - 1] = stage_transpose(units[i - 1], *a1.pop(i - 1))
                if i >= 2:
                    stage_pv(units[i - 2], *a2.pop(i - 2))
                yield 1

        def rope(dst, src, cos, sin, heads, tmp, half=HD // 2, free=()):
            def b(a):
                return a.unsqueeze(1).to_broadcast([P, heads, half])
            x1, x2 = src[:, :, 0:half], src[:, :, half:2 * half]
            t1, t2 = tmp[:, :, 0:half], tmp[:, :, half:2 * half]
            d1, d2 = dst[:, :, 0:half], dst[:, :, half:2 * half]
            dve.do(lambda e: e.tensor_tensor(t1, x2, b(sin), MUL), after=free)
            dve.do(lambda e: e.tensor_tensor(t2, x1, b(sin), MUL))
            dve.do(lambda e: e.tensor_tensor(d1, x1, b(cos), MUL))
            dve.do(lambda e: e.tensor_tensor(d2, x2, b(cos), MUL))
            dve.do(lambda e: e.tensor_tensor(d1, d1, t1, SUB))
            return dve.do(lambda e: e.tensor_tensor(d2, d2, t2, ADD))

        steps_of = []

        def together(main, side):
            if walk[0] == 0:
                steps_of.append([sum(1 for _ in main), sum(w for w in side)])
                return
            n_main, shares = steps_of.pop(0)
            next(main)
            given, due = 1, 0
            for share in side:
                due += share
                while given < n_main and given * shares < due * n_main:
                    next(main)
                    given += 1
            for _ in main:
                pass

        def prepare():
            cursor[0] = 0
            col = COLS2
            start = now()
            mem3 = tok(R[7][:, :])
            mem_in = sp.load("r7", [(mem3[:, t, :], d["mem"][t * P:(t + 1) * P, :]) for t in range(T)], after=start)
            memT = R[5][:, :].rearrange("p (k s) -> p k s", k=KD)

            def sin_cos(sn, cs, x, n, tmp):
                dve.do(lambda e: e.tensor_scalar(n, x, TURNS, ROUND, MUL, ADD))
                dve.do(lambda e: e.tensor_scalar(n, n, ROUND, None, SUB))
                for part in TWO_PI:
                    dve.do(lambda e, part=part: e.scalar_tensor_tensor(x, n, -part, x, MUL, ADD))
                dve.do(lambda e: e.tensor_scalar(x, x, PI, -PI, MIN, MAX))
                s = act.do(lambda e: e.activation(sn, x, ACT.Sin), after=[dve.last])
                dve.do(lambda e: e.scalar_tensor_tensor(tmp, x, -1.0, x, MUL, MAX))
                dve.do(lambda e: e.tensor_scalar(tmp, tmp, -1.0, HALF_PI, MUL, ADD))
                return act.do(lambda e: e.activation(cs, tmp, ACT.Sin), after=[dve.last])

            pos_i, pos_f = R[10][:, 0:T + S].bitcast(I32), pos_rows[:, :]
            pos_in = sp.load("pos", [(pos_i[:, 0:T], d["pos_col"]),
                                     (pos_i[:, T:T + S], d["pos"].to_broadcast([P, S]))], after=start)
            dve.do(lambda e: e.tensor_copy(pos_f, pos_i), after=[pos_in])
            ang, sn2, cs2, tmp2, n2 = (stat(64) for _ in range(5))
            inv = consts[:, 1024:1056]
            for t in range(T):
                dve.do(lambda e, t=t: e.tensor_scalar(ang[:, 32 * t:32 * t + 32], inv, pos_f[:, t:t + 1], None, MUL))
            rope_ready = sin_cos(sn2, cs2, ang, n2, tmp2)
            sn3, cs3 = sn2.rearrange("p (t f) -> p t f", t=T), cs2.rearrange("p (t f) -> p t f", t=T)

            yield 1
            normed = tok(R[9][:, :])
            s = normalize(mem3, normed, [mem_in], start)
            prepared["memT"] = transpose_scaled(normed, memT, KD, [s], start, col["g_mem"])[0]
            yield 4
            lre, lim, ldt = (small_cols[:, col[n]:col[n] + ST] for n in ("lam_re", "lam_im", "log_dt"))
            dt5, rad, th, thn, tht, c5, s5, nr, ni, fr5, fi5, den = (stat(ST) for _ in range(12))
            a = act.do(lambda e: e.activation(dt5, ldt, ACT.Exp), after=[const_in])
            dve.do(lambda e: e.tensor_tensor(rad, lre, dt5, MUL), after=[a])
            dve.do(lambda e: e.tensor_tensor(th, lim, dt5, MUL))
            act.do(lambda e: e.activation(rad, rad, ACT.Exp), after=[dve.last])
            sin_cos(s5, c5, th, thn, tht)
            dve.do(lambda e: e.tensor_tensor(nr, rad, c5, MUL), after=[act.last])
            dve.do(lambda e: e.tensor_scalar(nr, nr, -1.0, None, ADD))
            dve.do(lambda e: e.tensor_tensor(ni, rad, s5, MUL))
            dve.do(lambda e: e.tensor_tensor(den, lre, lre, MUL))
            dve.do(lambda e: e.tensor_tensor(tht, lim, lim, MUL))
            dve.do(lambda e: e.tensor_tensor(den, den, tht, ADD))
            dve.do(lambda e: e.reciprocal(den, den))
            for dst, a1, a2, op in ((fr5, nr, ni, ADD), (fi5, ni, nr, SUB)):
                dve.do(lambda e, dst=dst, a1=a1: e.tensor_tensor(dst, a1, lre, MUL))
                dve.do(lambda e, a2=a2: e.tensor_tensor(tht, a2, lim, MUL))
                dve.do(lambda e, dst=dst, op=op: e.tensor_tensor(dst, dst, tht, op))
                dve.do(lambda e, dst=dst: e.tensor_tensor(dst, dst, den, MUL))
            wc, ws = [c5], [s5]
            for j in range(7):
                c_, s_, q_ = stat(ST), stat(ST), tht
                pc, ps_ = wc[-1], ws[-1]
                dve.do(lambda e, c_=c_, pc=pc: e.tensor_tensor(c_, pc, pc, MUL))
                dve.do(lambda e, ps_=ps_: e.tensor_tensor(q_, ps_, ps_, MUL))
                dve.do(lambda e, c_=c_: e.tensor_tensor(c_, c_, q_, SUB))
                dve.do(lambda e, s_=s_, pc=pc, ps_=ps_: e.scalar_tensor_tensor(s_, pc, 2.0, ps_, MUL, MUL))
                wc.append(c_)
                ws.append(s_)

            yield 3
            angles_ready = dve.last
            for half in range(2):
                ec = R[half][:, :].rearrange("p (i s) -> p i s", i=8)
                es = R[2 + half][:, :].rearrange("p (i s) -> p i s", i=8)
                tm = R[6][:, 0:D].rearrange("p (i s) -> p i s", i=8)
                dve.do(lambda e, ec=ec: e.memset(ec[:, :, 0:1], 1.0), after=start + [angles_ready])
                dve.do(lambda e, es=es: e.memset(es[:, :, 0:1], 0.0))
                for j in range(8):
                    m = 1 << j
                    c_, s_ = (bc(w[j][:, 8 * half:8 * half + 8], m) for w in (wc, ws))
                    a_c, a_s, o_c, o_s, tt = ec[:, :, 0:m], es[:, :, 0:m], ec[:, :, m:2 * m], es[:, :, m:2 * m], tm[:, :, 0:m]
                    for o, x1, x2, y1, y2, op in ((o_c, a_c, c_, a_s, s_, SUB), (o_s, a_c, s_, a_s, c_, ADD)):
                        dve.do(lambda e, o=o, x1=x1, x2=x2: e.tensor_tensor(o, x1, x2, MUL))
                        dve.do(lambda e, tt=tt, y1=y1, y2=y2: e.tensor_tensor(tt, y1, y2, MUL))
                        dve.do(lambda e, o=o, tt=tt, op=op: e.tensor_tensor(o, o, tt, op))
                    yield 2 if j > 5 else 1
            prepared.update(tables=dve.last, pos=pos_f, rope=rope_ready, sn3=sn3, cs3=cs3,
                            rad=rad, fr5=fr5, fi5=fi5)
            yield 1

        prepared = {}

        def layer(l):
            cursor[0] = 0
            w_in, w_proj, w_out = d["w_in"][l], d["w_proj"][l], d["w_out"][l]
            col = COLS1[l]
            base = now()
            rowp = d["rows"]
            r0 = ROWS1[l]
            row_in = sp.load("rows", [(rows[:, 0:5 * 16], rowp[:, r0:r0 + 5 * 16].to_broadcast([P, 5 * 16]))], after=base)
            dt_bias, a_log, d_skip, sinks, f_bias = (rows[:, 16 * i:16 * i + 16] for i in range(5))
            normed = tok(R[9][:, :])
            h_ready = to_hT(x3, normed, col["norm"], after=[x_in, dve.last])
            free = now()

            def seq(*sections):
                for f in sections:
                    yield from f

            def plain(c0, n, dst3, dcol, fr, scale=None):
                for o in range(0, n, CH):
                    m = min(CH, n - o)
                    yield from project(hT, w_in[:, c0 + o:c0 + o + m], D, m, plain_to(dst3, dcol + o, m, fr, scale), after=h_ready)

            def silu(c0, n, dst3, fr):
                for o in range(0, n, CH):
                    yield from project(hT, w_in[:, c0 + o:c0 + o + CH], D, CH, silu_to(dst3, o, CH, fr), after=h_ready)

            xbc = [tok(R[0][:, :]), tok(R[1][:, :])]
            za = tok(R[2][:, :])
            dtr = stat(2 * 16).rearrange("p (t h) -> p t h", t=T)
            fr_ = stat(2 * 16).rearrange("p (t h) -> p t h", t=T)
            for _ in seq(plain(DT, 16, dtr, 0, free), plain(XBC, D, xbc[0], 0, free)):
                pass
            xbc_queued = [True, False]

            def second_half():
                yield from plain(XBC + D, D, xbc[1], 0, free)
                xbc_queued[1] = True

            y_ready = {}
            y_a, y_b, y_c = (tok(R[i][:, :]) for i in (5, 8, 3))

            def mamba():
                raw = [R[3][:, :].rearrange("p (k s) -> p k s", k=KD), R[4][:, :].rearrange("p (k s) -> p k s", k=KD)]
                conv = [R[0][:, :].rearrange("p (k s) -> p k s", k=KD), R[1][:, :].rearrange("p (k s) -> p k s", k=KD)]
                for half in range(2):
                    if walk[0] == 1 and not xbc_queued[half]:
                        raise ValueError("the projection has to be queued first")
                    transpose_scaled(xbc[half], raw[half], KD, [act.last], free)
                    last_t = [pe.last]
                    yield 1
                    for k in range(KD):
                        c = half * KD + k
                        u, o = raw[half][:, k, :], conv[half][:, k, :]
                        wc = [small_cols[:, col["conv"] + w * 16 + c:col["conv"] + w * 16 + c + 1] for w in range(CONV_W)]
                        bcol = small_cols[:, col["conv_b"] + c:col["conv_b"] + c + 1]
                        dve.do(lambda e, u=u, o=o, wc=wc, bcol=bcol: e.tensor_scalar(o, u, wc[3], bcol, MUL, ADD), after=[act.last] + last_t)
                        for w in range(3):
                            sh = 3 - w
                            dve.do(lambda e, u=u, o=o, wc=wc, w=w, sh=sh: e.scalar_tensor_tensor(
                                o[:, sh:S], u[:, 0:S - sh], wc[w], o[:, sh:S], MUL, ADD))
                    src, e_t = R[half], R[3 + half]
                    a = sigmoid(e_t[:, :], src[:, :], after=[dve.last])
                    dve.do(lambda e, src=src, e_t=e_t: e.tensor_tensor(src[:, :], src[:, :], e_t[:, :], MUL), after=[a])
                    yield 8
                conv_ready = [dve.last]
                xT, bcT = conv
                x_tok, xdt = tok(R[3][:, :]), tok(R[4][:, :])
                blocks = [xT[:, k, t * P:(t + 1) * P] for t in range(T) for k in range(KD)]

                def x_out(b0, n, bank, step):
                    t, k = divmod(b0, KD)
                    return [act.do(lambda e: e.copy(x_tok[:, t, k * P:(k + n) * P], bank[:, 0:n * P]), after=[step, conv_ready[0]])]
                transposes(blocks, x_out, after=conv_ready)
                b_tok = R[9][:, 0:GROUPS * P].rearrange("p (g n) -> p g n", g=GROUPS)
                blocks = [bcT[:, g, 0:P] for g in range(GROUPS)]
                transposes(blocks, lambda b0, n, bank, step: [act.do(
                    lambda e: e.copy(b_tok[:, b0:b0 + n, :], bank[:, 0:n * P].rearrange("p (g n) -> p g n", g=n)), after=[step] + free)],
                    after=conv_ready)
                x_ready = act.last
                yield 1
                dt, adt, z, q = (stat(32).rearrange("p (t h) -> p t h", t=T) for _ in range(4))
                na = stat(16)
                dve.do(lambda e: e.tensor_tensor(dtr, dtr, dt_bias.unsqueeze(1).to_broadcast([P, T, 16]), ADD), after=[row_in, act.last])
                s = act.do(lambda e: e.activation(na, a_log, ACT.Exp), after=[row_in])
                log1p_exp_neg_abs(dt, dtr, z, q)
                dve.do(lambda e: e.scalar_tensor_tensor(dt, dtr, 0.0, dt, MAX, ADD))
                dve.do(lambda e: e.scalar_tensor_tensor(adt, dt, -1.0, na.unsqueeze(1).to_broadcast([P, T, 16]), MUL, MUL), after=[s])
                adt_ready = dve.last
                for t in range(T):
                    dve.do(lambda e, t=t: e.tensor_tensor(xdt[:, t, :].rearrange("p (h c) -> p h c", h=HEADS),
                           x_tok[:, t, :].rearrange("p (h c) -> p h c", h=HEADS), bc(dt[:, t, :], HD), MUL), after=[x_ready])
                xdt_ready = dve.last
                yield 3
                i, bank, readers = work.take()
                pe.do(lambda e: e.matmul(bank[:, 0:16], above, adt[:, 0, :], start=True, stop=True), after=[adt_ready] + readers)
                s = pe.do(lambda e: e.matmul(bank[:, 16:32], upto, adt[:, 1, :], start=True, stop=True))
                decs = stat(32)
                s = act.do(lambda e: e.activation(decs, bank[:, 0:32], ACT.Exp), after=[s])
                work.done(i, [s])
                to_end, from_start = decs[:, 0:16], decs[:, 16:32]
                xds = R[9][:, CH:CH + D]
                dve.do(lambda e: e.tensor_tensor(xds.rearrange("p (h c) -> p h c", h=HEADS), xdt[:, 0, :].rearrange("p (h c) -> p h c", h=HEADS),
                       bc(to_end, HD), MUL), after=[s] + free)
                xds_ready = dve.last
                yield 1
                state = R[10][:, 0:D]
                for g in range(0, GROUPS, 2):
                    i, bank, readers = work.take()
                    for j in range(2):
                        s = pe.do(lambda e, g=g, j=j, bank=bank: e.matmul(bank[:, j * 256:(j + 1) * 256], b_tok[:, g + j, :],
                                  xds[:, (g + j) * 256:(g + j + 1) * 256], start=True, stop=True), after=[xds_ready, x_ready] + readers)
                    s = act.do(lambda e, g=g, bank=bank: e.copy(state[:, g * 256:(g + 2) * 256], bank[:, :]), after=[s] + free)
                    work.done(i, [s])
                state_ready = act.last
                yield 1
                cb = R[10][:, D:2 * D].rearrange("p (t g l) -> p t g l", t=T, g=GROUPS)
                for t in range(T):
                    i, bank, readers = work.take()
                    for g in range(GROUPS):
                        s = pe.do(lambda e, t=t, g=g, bank=bank: e.matmul(bank[:, g * P:(g + 1) * P], bcT[:, g, t * P:(t + 1) * P],
                                  bcT[:, GROUPS + g, t * P:(t + 1) * P], start=True, stop=True), after=conv_ready + readers)
                    s = dve.do(lambda e, t=t, bank=bank: e.tensor_tensor(cb[:, t, :, :], bank[:, :].rearrange("p (g l) -> p g l", g=GROUPS),
                               causal01.unsqueeze(1).to_broadcast([P, GROUPS, P]), MUL), after=[s] + free)
                    work.done(i, [s])
                yield 1
                y = y_a
                ya_free = free
                lhs_ring, m_ring = Ring([R[9][:, 0:CH], R[9][:, CH:2 * CH]]), Ring([R[9][:, 2 * CH:3 * CH], R[9][:, 3 * CH:4 * CH]])
                lhs_ring.readers = [[pe.last], [pe.last]]
                todo, pend = [(t, g) for t in range(T) for g in range(GROUPS)], []
                for n in range(len(todo) + 1):
                    if n < len(todo):
                        t, g = todo[n]
                        li, lhs, lr = lhs_ring.take()
                        lhs3 = lhs.rearrange("p (r k) -> p r k", r=RPG)
                        s = dve.do(lambda e, t=t, g=g, lhs3=lhs3: e.tensor_tensor(lhs3, above.unsqueeze(1).to_broadcast([P, RPG, P]),
                                   bc(adt[:, t, g * RPG:(g + 1) * RPG], P), MUL), after=lr)
                        i, bank, readers = work.take()
                        for r in range(RPG):
                            s2 = pe.do(lambda e, r=r, lhs3=lhs3, bank=bank: e.matmul(bank[:, r * P:(r + 1) * P], lhs3[:, r, :], upto,
                                       start=True, stop=True), after=[s] + readers)
                        lhs_ring.done(li, [s2])
                        mi, m, mr = m_ring.take()
                        s3 = act.do(lambda e, m=m, bank=bank: e.activation(m, bank[:, :], ACT.Exp), after=[s2] + mr)
                        work.done(i, [s3])
                        s4 = dve.do(lambda e, m=m, t=t, g=g: e.tensor_tensor(m.rearrange("p (r l) -> p r l", r=RPG), m.rearrange("p (r l) -> p r l", r=RPG),
                                    cb[:, t, g, :].unsqueeze(1).to_broadcast([P, RPG, P]), MUL), after=[s3])
                        pend.append((t, g, mi, m, s4))
                    if n >= 1:
                        t, g, mi, m, s4 = pend.pop(0)
                        i, bank, readers = work.take()
                        for r in range(RPG):
                            h = g * RPG + r
                            s = pe.do(lambda e, r=r, h=h, t=t, m=m, bank=bank: e.matmul(bank[:, r * HD:(r + 1) * HD], m[:, r * P:(r + 1) * P],
                                      xdt[:, t, h * HD:(h + 1) * HD], start=True, stop=True), after=[s4, xdt_ready] + readers)
                        m_ring.done(mi, [s])
                        if t == 1:
                            s = pe.do(lambda e, g=g, bank=bank: e.matmul(bank[:, 256:512], bcT[:, GROUPS + g, P:2 * P],
                                      state[:, g * 256:(g + 1) * 256], start=True, stop=True), after=[state_ready])
                        yg = y[:, t, g * 256:(g + 1) * 256]
                        xg = x_tok[:, t, g * 256:(g + 1) * 256]

                        def v(a):
                            return a.rearrange("p (r c) -> p r c", r=RPG)
                        s = dve.do(lambda e, xg=xg, yg=yg, g=g: e.tensor_tensor(v(yg), v(xg), bc(d_skip[:, g * RPG:(g + 1) * RPG], HD), MUL),
                                   after=[s] + ya_free)
                        s = dve.do(lambda e, yg=yg, bank=bank: e.tensor_tensor(yg, yg, bank[:, 0:256], ADD))
                        if t == 1:
                            dve.do(lambda e, xg=xg, bank=bank, g=g: e.tensor_tensor(v(xg), v(bank[:, 256:512]),
                                   bc(from_start[:, g * RPG:(g + 1) * RPG], HD), MUL))
                            s = dve.do(lambda e, xg=xg, yg=yg: e.tensor_tensor(yg, yg, xg, ADD))
                        work.done(i, [dve.last])
                    yield 1
                ss, r8, tmp8 = stat(8), stat(8), stat(8)
                dve.do(lambda e: e.tensor_tensor(R[5][:, :], R[5][:, :], R[2][:, :], MUL))
                s = act.do(lambda e: e.activation(R[3][:, :], R[5][:, :], ACT.Square), after=[dve.last])
                dve.do(lambda e: e.tensor_reduce(ss, R[3][:, :].rearrange("p (g c) -> p g c", g=8), AX, ADD), after=[s])
                rsqrt(r8, ss, 1.0 / 256, tmp8)
                y8 = R[5][:, :].rearrange("p (g c) -> p g c", g=8)
                y_ready["a"] = [dve.do(lambda e: e.tensor_tensor(y8, y8, bc(r8, 256), MUL))]
                yield 1

            kvb = tok(R[7][:, 0:D])
            qb, zb = tok(R[6][:, :]), tok(R[8][:, :])
            together(seq(second_half(), silu(ZA, D, za, free), plain(QB, D, qb, 0, free, HD ** -0.5), plain(KV, CH, kvb, 0, free), silu(ZB, D, zb, free)), mamba())

            def window():
                q_rot = tok(R[9][:, :])
                k_dup = R[7][:, D:2 * D].rearrange("p (t g u c) -> p t g u c", t=T, g=KVH, u=2)
                base_w = now()
                for t in range(T):
                    tmp = R[10][:, 0:D].rearrange("p (h c) -> p h c", h=HEADS)
                    rope(q_rot[:, t, :].rearrange("p (h c) -> p h c", h=HEADS), qb[:, t, :].rearrange("p (h c) -> p h c", h=HEADS),
                         cosT[:, t, :], sinT[:, t, :], HEADS, tmp, free=base_w)
                    rope(k_dup[:, t, :, 0, :], kvb[:, t, 0:256].rearrange("p (g c) -> p g c", g=KVH), cosT[:, t, :], sinT[:, t, :],
                         KVH, R[10][:, 0:256].rearrange("p (h c) -> p h c", h=KVH))
                    dve.do(lambda e, t=t: e.tensor_copy(k_dup[:, t, :, 1, :], k_dup[:, t, :, 0, :]))
                    yield 1
                qT = R[6][:, :].rearrange("p (k s) -> p k s", k=KD)
                ready = transpose_scaled(q_rot, qT, KD, [dve.last], [dve.last])
                yield 1
                kT = R[10][:, 0:D].rearrange("p (g s) -> p g s", g=KVH)
                k_flat = R[7][:, D:2 * D].rearrange("p (t c) -> p t c", t=T)
                ready = transpose_scaled(k_flat, kT, KVH, [dve.last], [dve.last])
                yield 1
                def scores(h, t, dst, after):
                    keys = (t + 1) * P
                    par = HD * (h % 2)
                    pe.do(lambda e: e.matmul(dst, qT[par:par + HD, h // 2, t * P:(t + 1) * P], kT[par:par + HD, h // KVH, 0:keys],
                          start=True, stop=False), after=after)
                    mask = causal_mask if t == 0 else window_mask
                    return pe.do(lambda e: e.matmul(dst, idbf[:, :], mask, start=False, stop=True), after=[maskbf_made])
                units = [(t, h, 2, 2, scores, (t + 1) * P) for t in range(T) for q in range(0, HEADS, 4) for h in (q, q + 1)]
                yield from attention(units, HEADS, HD, y_b, lambda h, b: kvb[:, b, 256 + (h // 4) * HD:256 + (h // 4 + 1) * HD],
                                     ready, [R[4][:, 0:CH], R[4][:, CH:2 * CH]], [R[4][:, 2 * CH:3 * CH], R[4][:, 3 * CH:4 * CH]],
                                     sink=sinks, gated=True)
                y_ready["b"] = [dve.last]
                yield 1

            free_a = now()
            cq, ck, cv, zc = (tok(R[i][:, :]) for i in range(4))
            together(seq(plain(CF, 16, fr_, 0, []), plain(CQ, D, cq, 0, free_a, HD ** -0.5), plain(CK, D, ck, 0, free_a), plain(CV, D, cv, 0, free_a),
                         silu(CZ, D, zc, free_a)), window())

            def forget():
                free_b = now()
                qT = R[6][:, :].rearrange("p (k s) -> p k s", k=KD)
                kT = R[7][:, :].rearrange("p (k s) -> p k s", k=KD)
                transpose_scaled(cq, qT, KD, [act.last], free_b)
                yield 1
                ready = transpose_scaled(ck, kT, KD, [act.last], free_b)
                yield 1
                lf, z, q = (stat(32).rearrange("p (t h) -> p t h", t=T) for _ in range(3))
                dve.do(lambda e: e.tensor_tensor(fr_, fr_, f_bias.unsqueeze(1).to_broadcast([P, T, 16]), ADD), after=[act.last])
                log1p_exp_neg_abs(lf, fr_, z, q)
                dve.do(lambda e: e.scalar_tensor_tensor(lf, fr_, 0.0, lf, MIN, SUB))
                lf_ready = dve.last
                bias_ring = Ring([R[10][:, 3 * i * P:3 * (i + 1) * P] for i in range(4)])
                bias_ring.readers = [free_b for _ in range(4)]

                def scores(h, t, dst, after):
                    keys = (t + 1) * P
                    par = HD * (h % 2)
                    i, bm, readers = bias_ring.take()
                    s = dve.do(lambda e: e.tensor_scalar(bm[:, 0:P], above, lf[:, 0, h:h + 1], None, MUL), after=readers)
                    if t == 1:
                        s = dve.do(lambda e: e.tensor_scalar(bm[:, P:3 * P], ones_gt, lf[:, 1, h:h + 1], None, MUL), after=readers)
                    pe.do(lambda e: e.matmul(dst, qT[par:par + HD, h // 2, t * P:(t + 1) * P], kT[par:par + HD, h // 2, 0:keys],
                          start=True, stop=False), after=after)
                    if t == 0:
                        pe.do(lambda e: e.matmul(dst, upto, bm[:, 0:P], start=False, stop=False), after=[s])
                        last = pe.do(lambda e: e.matmul(dst, idbf[:, :], causal_mask, start=False, stop=True), after=[maskbf_made])
                    else:
                        pe.do(lambda e: e.matmul(dst, upto, bm[:, P:3 * P], start=False, stop=False), after=[s])
                        pe.do(lambda e: e.matmul(dst[:, 0:P], ones, bm[:, 0:P], start=False, stop=False))
                        last = pe.do(lambda e: e.matmul(dst[:, P:2 * P], idbf[:, :], causal_mask, start=False, stop=True), after=[maskbf_made])
                    bias_ring.done(i, [last])
                    return last
                units = [(t, h, 2, 2, scores, (t + 1) * P) for t in range(T) for q in range(0, HEADS, 4) for h in (q, q + 1)]
                yield from attention(units, HEADS, HD, y_c, lambda h, b: cv[:, b, h * HD:(h + 1) * HD],
                                     ready, [R[4][:, 0:CH], R[4][:, CH:2 * CH]], [R[4][:, 2 * CH:3 * CH], R[4][:, 3 * CH:4 * CH]], gated=True)
                y_ready["c"] = [dve.last]
                yield 1

            gb = d["rows"]
            g0 = ROWS1[l] + 80

            def mix(i, y, key, col0=None):
                return gated_add(y, KD, w_in[:, GATES + i * D:GATES + (i + 1) * D], w_proj[i],
                                 gb[:, g0 + i * D:g0 + (i + 1) * D], i == 0, y_ready[key], col0)
            together(seq(mix(0, y_a, "a", col["ssm_norm"]), mix(1, y_b, "b")), forget())
            def last_mix():
                yield from mix(2, y_c, "c")
                hT_readers[:] = [pe.last]
                if l == LAYERS - 1:
                    prepared["mem_ready"] = split(hT, R[5][:, :].rearrange("p (k s) -> p k s", k=KD),
                                                  after=hT_readers + [prepared["memT"]])
                yield from out_projection(w_out)
            if l < LAYERS - 1:
                for _ in last_mix():
                    pass
            else:
                prepared["memT"] = None
                together(last_mix(), prepare())

        COLS1, COLS2 = d["cols_at"][0:2], d["cols_at"][2]
        ROWS1, ROWS2 = d["rows_at"][0:2], d["rows_at"][2]
        def second():
            pos_f, sn3, cs3, rad, fr5, fi5 = (prepared[n] for n in ("pos", "sn3", "cs3", "rad", "fr5", "fi5"))
            rope_ready = prepared["rope"]
            col = COLS2
            w_in = d["w_in_2"]
            start = now()
            r0 = ROWS2["small"]
            n_small = 64 * 2 + 128 * 2 + NGRP + EXP
            row_in = sp.load("rows2", [(rows2[:, :], d["rows"][:, r0:r0 + n_small].to_broadcast([P, n_small]))])
            g_q, g_k, g_qm, g_km = rows2[:, 0:64], rows2[:, 64:128], rows2[:, 128:256], rows2[:, 256:384]
            b_grp, b_exp = rows2[:, 384:388], rows2[:, 388:420]
            fw = R[9][:, 0:D]
            fw_in = sp.load("r9", [(fw, d["rows"][:, ROWS2["final"]:ROWS2["final"] + D].to_broadcast([P, D]))], after=start)

            def plain(c0, n, dst3, dcol, fr, ready, w=None, scale=None):
                src = w_in if w is None else w
                for o in range(0, n, CH):
                    m = min(CH, n - o)
                    yield from project(hT, src[:, c0 + o:c0 + o + m], D, m, plain_to(dst3, dcol + o, m, fr, scale), after=ready)

            r, s = rms_factor(x3, [dve.last])
            for t in range(T):
                dve.do(lambda e, t=t: e.scalar_tensor_tensor(x3[:, t, :], x3[:, t, :], r[:, t:t + 1], fw, MUL, MUL), after=[fw_in])
            normed = tok(R[10][:, :])
            s = normalize(x3, normed, [dve.last])

            kmv = tok(R[4][:, :])
            for _ in plain(0, 2 * CH, kmv, 0, start, prepared["mem_ready"], w=d["w_mem_kv"]):
                pass
            kmv_ready = act.last
            hT_readers[:] = [pe.last]
            h_ready = transpose_split(normed, hT, KD, [s], hT_readers, col["g_mix"])

            u3, q3 = tok(R[5][:, 0:D]), tok(R[5][:, D:2 * D])
            kvi, qm3 = tok(R[6][:, 0:D]), tok(R[6][:, D:2 * D])
            for _ in plain(Q2, CH, q3, 0, start, h_ready):
                pass
            for _ in plain(KVI2, QM2 - KVI2, kvi, 0, start, h_ready):
                pass

            def head_norm(x_4, heads, c, gain, junk, after=()):
                ss, r, tmp = stat(heads), stat(heads), stat(heads)
                dve.do(lambda e: e.tensor_tensor(junk, x_4, x_4, MUL), after=after)
                dve.do(lambda e: e.tensor_reduce(ss, junk, AX, ADD))
                rsqrt(r, ss, 1.0 / c, tmp)
                dve.do(lambda e: e.tensor_tensor(x_4, x_4, bc(r, c), MUL))
                return dve.do(lambda e: e.tensor_tensor(x_4, x_4, gain.unsqueeze(1).to_broadcast([P, heads, c]), MUL))

            def sparse():
                dve.do(lambda e: e.tensor_scalar(g_q, g_q, HD ** -0.5, None, MUL), after=[row_in, act.last])
                rot = tok(R[7][:, :])
                tmp = R[8][:, 0:CH].rearrange("p (h c) -> p h c", h=8)

                def hv(a, h):
                    return a.rearrange("p (h c) -> p h c", h=h)
                for t in range(T):
                    qh, kh = hv(q3[:, t, :], 8), hv(kvi[:, t, 0:64], 1)
                    head_norm(qh, 8, HD, g_q, tmp, after=start)
                    head_norm(kh, 1, HD, g_k, tmp[:, 0:1, :])
                    cs, sn = cs3[:, t, :], sn3[:, t, :]
                    rope(hv(rot[:, t, 0:512], 8), qh, cs, sn, 8, tmp, free=[rope_ready])
                    rope(hv(rot[:, t, 512:576], 1), kh, cs, sn, 1, tmp[:, 0:1, :])
                    dve.do(lambda e, t=t: e.tensor_copy(rot[:, t, 576:640], rot[:, t, 512:576]))
                    rope(hv(rot[:, t, 640:896], 4), hv(kvi[:, t, 128:384], 4), cs, sn, 4, tmp[:, 0:4, :])
                    rope(hv(rot[:, t, 896:960], 1), hv(kvi[:, t, 384:448], 1), cs, sn, 1, tmp[:, 0:1, :])
                    dve.do(lambda e, t=t: e.tensor_copy(rot[:, t, 960:1024], rot[:, t, 896:960]))
                    yield 1
                aT = R[8][:, :].rearrange("p (k s) -> p k s", k=KD)
                ready = transpose_scaled(rot, aT, KD, [dve.last], [dve.last])
                yield 1
                def select(t):
                    pq = pos_f[:, t:t + 1]
                    isc, valid, tmp_i = R[7][:, 0:S], R[7][:, S:2 * S], R[7][:, 2 * S:3 * S]
                    wi = stat(4)
                    top = stat(8)
                    dve.do(lambda e, t=t: e.tensor_scalar(wi, kvi[:, t, 448:452], 4 ** -0.5 * HD ** -0.5, None, MUL), after=[pe.last])
                    n = 0
                    for par in range(2):
                        i, bank, readers = work.take()
                        for j in range(2):
                            s = pe.do(lambda e, par=par, j=j, bank=bank, t=t: e.matmul(bank[:, j * S:(j + 1) * S],
                                      aT[64 * par:64 * par + 64, 5 + j, t * P:(t + 1) * P], aT[64 * par:64 * par + 64, 7, :],
                                      start=True, stop=True), after=ready + readers)
                        for j in range(2):
                            h = 2 * j + par
                            dst = isc if n == 0 else tmp_i
                            dve.do(lambda e, dst=dst, j=j, h=h, bank=bank, wi=wi: e.tensor_scalar(dst, bank[:, j * S:(j + 1) * S], 0.0,
                                   wi[:, h:h + 1], MAX, MUL), after=[s])
                            if n:
                                dve.do(lambda e: e.tensor_tensor(isc, isc, tmp_i, ADD))
                            n += 1
                        work.done(i, [dve.last])
                    dve.do(lambda e, pq=pq: e.tensor_scalar(valid, pos_f[:, T:T + S], pq, None, ALU.is_le))
                    dve.do(lambda e: e.tensor_scalar(tmp_i, valid, -1.0, LATER, ADD, MUL))
                    dve.do(lambda e: e.tensor_tensor(isc, isc, valid, MUL))
                    dve.do(lambda e: e.tensor_tensor(isc, isc, tmp_i, ADD))
                    for _ in range(TOPK // 8):
                        dve.do(lambda e, top=top: e.max(top, isc))
                        dve.do(lambda e, top=top: e.match_replace(isc, top, isc, STRUCK))
                    dve.do(lambda e: e.tensor_scalar(isc, isc, STRUCK, None, ALU.is_equal))
                    dve.do(lambda e: e.tensor_tensor(isc, isc, valid, MUL))
                    dve.do(lambda e, t=t: e.tensor_scalar(selmask[:, t * S:(t + 1) * S], isc, -1.0, -NEG, ADD, MUL))
                    yield 1
                for t in range(T):
                    yield from select(t)
                sel_ready = dve.last

                def scores(h, t, dst, after):
                    par = 64 * (h % 2)
                    pe.do(lambda e: e.matmul(dst, aT[par:par + 64, h // 2, t * P:(t + 1) * P], aT[par:par + 64, 4, :], start=True, stop=False), after=after)
                    return pe.do(lambda e: e.matmul(dst, idbf[:, :], selmask[:, t * S:(t + 1) * S], start=False, stop=True), after=[sel_ready])
                units = [(t, h, 2, 2, scores, S) for t in range(T) for q in range(0, 8, 4) for h in (q, q + 1)]
                yield from attention(units, 8, HD, y_dsa, lambda h, b: kvi[:, b, 64:128], ready + [sel_ready],
                                     [R[9][:, 0:CH], R[9][:, CH:2 * CH]], [R[9][:, 2 * CH:3 * CH], R[9][:, 3 * CH:4 * CH]])
                ready2["dsa"] = [dve.last]
                yield 1

            ready2 = {}
            y_dsa, y_m = tok(R[10][:, 0:D]), tok(R[10][:, D:2 * D])
            together(itertools.chain(plain(U2, CH, u3, 0, start, h_ready), plain(QM2, CH, qm3, 0, start, h_ready)), sparse())

            def memory():
                free = now()
                dve.do(lambda e: e.tensor_scalar(g_qm, g_qm, 128 ** -0.5, None, MUL), after=[act.last, kmv_ready])
                for t in range(T):
                    jv = R[8][:, 0:CH].rearrange("p (h c) -> p h c", h=4)
                    head_norm(qm3[:, t, :].rearrange("p (h c) -> p h c", h=4), 4, 128, g_qm, jv, after=free)
                    head_norm(kmv[:, t, 0:CH].rearrange("p (h c) -> p h c", h=4), 4, 128, g_km, jv)
                    yield 1
                qT = R[8][:, 0:D].rearrange("p (h s) -> p h s", h=4)
                kT = R[8][:, D:2 * D].rearrange("p (h s) -> p h s", h=4)
                transpose_scaled(qm3, qT, 4, [dve.last], [dve.last])
                ready = transpose_scaled(kmv[:, :, 0:CH], kT, 4, [dve.last], [])
                yield 1

                def scores(h, t, dst, after):
                    return pe.do(lambda e: e.matmul(dst, qT[:, h, t * P:(t + 1) * P], kT[:, h, :], start=True, stop=True), after=after)
                units = [(t, h, 2, 1, scores, S) for t in range(T) for h in range(0, 4, 2)]
                yield from attention(units, 4, 128, y_m, lambda h, b: kmv[:, b, CH + h * 128:CH + (h + 1) * 128], ready,
                                     [R[9][:, 0:CH], R[9][:, CH:2 * CH]], [R[9][:, 2 * CH:3 * CH], R[9][:, 3 * CH:4 * CH]])
                ready2["mem"] = [dve.last]
                yield 1

            def ssm():
                free = now()
                uT = R[4][:, 0:D].rearrange("p (k s) -> p k s", k=4)
                ysT = R[4][:, D:2 * D].rearrange("p (k s) -> p k s", k=4)
                u_ready = transpose_scaled(u3, uT, 4, [act.last], free)
                yield 1
                bc_at, v_at = [R[9], R[7]], [(R[5][:, 0:D], R[5][:, D:2 * D]), (R[10][:, 0:D], R[10][:, D:2 * D])]
                gre, gim = (R[6][:, j * D:(j + 1) * D].rearrange("p (i s) -> p i s", i=4) for j in range(2))
                tmp = R[8][:, 0:D].rearrange("p (i s) -> p i s", i=4)
                tmc = R[8][:, D:2 * D].rearrange("p (a i c) -> p a i c", a=2, i=4)
                ssm_banks = Ring(banks[4:8])
                ssm_banks.readers = [now() for _ in range(4)]
                bcm, ccm, bc_loaded, c_ready, states, grown = {}, {}, {}, {}, {}, {}

                def fetch_quarter(k):
                    at = bc_at[k % 2]
                    parts = [at[:, j * CH:(j + 1) * CH].rearrange("p (i c) -> p i c", i=4) for j in range(4)]
                    bcm[k], ccm[k] = parts[0:2], parts[2:4]
                    loaded = sp.load(f"r{9 - 2 * (k % 2)}", [(v, d[n][:, 4 * k:4 * k + 4, :]) for v, n in
                                     zip(parts, ("b_re", "b_im", "c_re", "c_im"))], after=now())
                    bc_loaded[k] = loaded
                    f_r, f_i = (bc(a[:, 4 * k:4 * k + 4], P) for a in (fr5, fi5))
                    c0, c1 = ccm[k]
                    pool.do(lambda e: e.tensor_tensor(tmc[:, 0, :, :], c0, f_i, MUL), after=[loaded] + free)
                    pool.do(lambda e: e.tensor_tensor(tmc[:, 1, :, :], c1, f_i, MUL))
                    pool.do(lambda e: e.tensor_tensor(c0, c0, f_r, MUL))
                    pool.do(lambda e: e.tensor_tensor(c1, c1, f_r, MUL))
                    pool.do(lambda e: e.tensor_tensor(c0, c0, tmc[:, 1, :, :], SUB))
                    pool.do(lambda e: e.tensor_tensor(c1, c1, tmc[:, 0, :, :], ADD))
                    c_ready[k] = pool.do(lambda e: e.tensor_scalar(c1, c1, -1.0, None, MUL))

                def angle(k):
                    half, i0 = k // 2, 4 * (k % 2)
                    return (R[half + o][:, :].rearrange("p (i s) -> p i s", i=8)[:, i0:i0 + 4, :] for o in (0, 2))

                def inputs(k, j2):
                    got = []
                    for w in range(2):
                        i, bank, readers = ssm_banks.take()
                        for j in range(2):
                            s = pe.do(lambda e, j=j, w=w, bank=bank: e.matmul(bank[:, j * S:(j + 1) * S], bcm[k][w][:, 2 * j2 + j, :], uT[:, k, :],
                                      start=True, stop=True), after=[bc_loaded[k]] + u_ready + readers)
                        got.append((i, bank, s))
                    return got

                def turned(k, j2, got, readers):
                    ec, es = angle(k)
                    vre, vim = (a.rearrange("p (i s) -> p i s", i=4) for a in v_at[k % 2])
                    bre, bim = (g[1][:, :].rearrange("p (i s) -> p i s", i=2) for g in got)
                    sl = slice(2 * j2, 2 * j2 + 2)
                    for o, x1, y1, op in ((vre, bre, bim, ADD), (vim, bim, bre, SUB)):
                        dve.do(lambda e, o=o, x1=x1: e.tensor_tensor(o[:, sl, :], x1, ec[:, sl, :], MUL),
                               after=[got[0][2], got[1][2], prepared["tables"]] + readers)
                        dve.do(lambda e, y1=y1: e.tensor_tensor(tmp[:, sl, :], y1, es[:, sl, :], MUL))
                        dve.do(lambda e, o=o, op=op: e.tensor_tensor(o[:, sl, :], o[:, sl, :], tmp[:, sl, :], op))
                    for i, _, _ in got:
                        ssm_banks.done(i, [dve.last])

                def grow(k):
                    ec, es = angle(k)
                    vre, vim = (a.rearrange("p (i s) -> p i s", i=4) for a in v_at[k % 2])
                    for v, g in ((vre, gre), (vim, gim)):
                        for i in range(4):
                            dve.do(lambda e, v=v, g=g, i=i: e.tensor_tensor_scan(g[:, i, :], rad[:, 4 * k + i:4 * k + i + 1].to_broadcast([P, S]),
                                   v[:, i, :], 0.0, MUL, ADD))
                    for o, x1, y1, op in ((vre, gre, gim, SUB), (vim, gim, gre, ADD)):
                        dve.do(lambda e, o=o, x1=x1: e.tensor_tensor(o, x1, ec, MUL))
                        dve.do(lambda e, y1=y1: e.tensor_tensor(tmp, y1, es, MUL))
                        dve.do(lambda e, o=o, op=op: e.tensor_tensor(o, o, tmp, op))
                    states[k], grown[k] = (vre, vim), dve.last

                def outputs(k):
                    i, bank, readers = ssm_banks.take()
                    for j in range(4):
                        for w, h in enumerate(states[k]):
                            s = pe.do(lambda e, j=j, w=w, h=h: e.matmul(bank[:, 0:S], ccm[k][w][:, j, :], h[:, j, :],
                                      start=(j == 0 and w == 0), stop=(j == 3 and w == 1)), after=[grown[k], c_ready[k]] + readers)
                    return i, bank, s

                def collect(k, i, bank, s):
                    dcol = small_cols[:, col["d_skip"] + k:col["d_skip"] + k + 1]
                    s = dve.do(lambda e: e.scalar_tensor_tensor(ysT[:, k, :], uT[:, k, :], dcol, bank[:, 0:S], MUL, ADD), after=[s])
                    ssm_banks.done(i, [s])

                fetch_quarter(0)
                fetch_quarter(1)
                v_free = [free, now()]
                out_k = None
                for k in range(5):
                    if k < 4:
                        got = inputs(k, 0)
                    if k:
                        out_k = outputs(k - 1)
                        after_c = [out_k[2]]
                    if k < 4:
                        turned(k, 0, got, v_free[k % 2])
                    if k:
                        collect(k - 1, *out_k)
                        v_free[(k - 1) % 2] = after_c
                        if k + 1 < 4:
                            fetch_quarter(k + 1)
                    if k < 4:
                        turned(k, 1, inputs(k, 1), v_free[k % 2])
                        yield 1
                        grow(k)
                        yield 2
                    if k == 1:
                        w = R[0][:, :].rearrange("p (k n) -> p k n", k=4)
                        loaded = sp.load("r0", [(w, d["w_glu"].rearrange("(k p) n -> p k n", p=P))], after=now())
                work.readers = [now() for _ in work.slots]
                mixed.readers = [now()]
                yield 1
                yf, g1 = R[4][:, D:2 * D], R[8][:, 0:D]
                dve.do(lambda e: e.tensor_tensor(g1, yf, yf, MUL))
                dve.do(lambda e: e.tensor_scalar(g1, g1, 0.044715, 1.0, MUL, ADD))
                dve.do(lambda e: e.tensor_tensor(g1, g1, yf, MUL))
                a = sigmoid(g1, g1, 2.0 * (2.0 / np.pi) ** 0.5, after=[dve.last])
                dve.do(lambda e: e.tensor_tensor(yf, yf, g1, MUL), after=[a])
                y_ok = dve.last
                for k in range(0, 4, 2):
                    i, bank, readers = work.take()
                    for j in range(2):
                        for kk in range(4):
                            s = pe.do(lambda e, j=j, k=k, kk=kk, bank=bank: e.matmul(bank[:, j * S:(j + 1) * S], w[:, kk, (k + j) * P:(k + j + 1) * P], ysT[:, kk, :],
                                      start=(kk == 0), stop=(kk == 3)), after=[y_ok, loaded] + readers)
                    a = sigmoid(g1[:, k * S:(k + 2) * S], bank[:, :], after=[s])
                    work.done(i, [act.last])
                ready2["ssm"] = [dve.do(lambda e: e.tensor_tensor(yf, yf, g1, MUL), after=[s, a])]
                yield 1

            ysT = R[4][:, D:2 * D].rearrange("p (k s) -> p k s", k=4)

            def mix(i, y, key, w):
                return gated_add(y, 4, w_in[:, GATES2 + i * D:GATES2 + (i + 1) * D], d[w], None, i == 1, ready2[key])

            merged_readers[:] = [pe.last]
            together(mix(1, y_dsa, "dsa", "w_up_dsa"), memory())
            together(mix(2, y_m, "mem", "w_up_mem"), ssm())
            ready2["ssm"] = split(tuple(a[:, 0:4, :] for a in yT), ysT, after=ready2["ssm"] + yT_readers)
            for _ in mix(0, None, "ssm", "w_up_ssm"):
                pass
            for _ in out_projection(d["w_out_2"]):
                pass
            hT_readers[:] = [pe.last]

            h_ready = to_hT(x3, tok(R[0][:, :]), col["g_ffn"], after=[dve.last])
            n_r = NGRP + EXP
            wr = R[1][:, 0:KD * n_r].rearrange("p (k n) -> p k n", k=KD)
            wr_hi, wr_lo = (a[:, 0:KD * n_r].rearrange("p (k n) -> p k n", k=KD) for a in (y_hi, y_lo))
            loaded = sp.load("r1", [(wr[:, :, 0:NGRP], d["w_group"].rearrange("(k p) n -> p k n", p=P)),
                                       (wr[:, :, NGRP:n_r], d["w_expert"].rearrange("(k p) n -> p k n", p=P))], after=now())
            wr_ready = split((wr_hi, wr_lo), wr, after=[loaded] + yT_readers)
            lg, le = stat(T * NGRP), stat(T * EXP)
            lg3, le3 = lg.rearrange("p (t g) -> p t g", t=T), le.rearrange("p (t g) -> p t g", t=T)
            b_i, bank, readers = work.take()
            for t in range(T):
                for k in range(KD):
                    s = product(bank[:, t * n_r:(t + 1) * n_r], tuple(a[:, k, t * P:(t + 1) * P] for a in hT), (wr_hi[:, k, :], wr_lo[:, k, :]),
                                k == 0, k == KD - 1, wr_ready + h_ready + readers)
            lv = bank[:, 0:T * n_r].rearrange("p (t n) -> p t n", t=T)
            dve.do(lambda e: e.tensor_tensor(lg3, lv[:, :, 0:NGRP], b_grp.unsqueeze(1).to_broadcast([P, T, NGRP]), ADD), after=[s])
            s = dve.do(lambda e: e.tensor_tensor(le3, lv[:, :, NGRP:n_r], b_exp.unsqueeze(1).to_broadcast([P, T, EXP]), ADD))
            work.done(b_i, [s])

            def softmax(x, n, m):
                v = x.rearrange("p (a b) -> p a b", b=m)
                red = stat(n)
                dve.do(lambda e: e.tensor_reduce(red, v, AX, MAX))
                dve.do(lambda e: e.tensor_tensor(v, v, bc(red, m), SUB))
                a = act.do(lambda e: e.activation(x, x, ACT.Exp), after=[dve.last])
                dve.do(lambda e: e.tensor_reduce(red, v, AX, ADD), after=[a])
                dve.do(lambda e: e.reciprocal(red, red))
                dve.do(lambda e: e.tensor_tensor(v, v, bc(red, m), MUL))
            softmax(lg, T, NGRP)
            softmax(le, T * NGRP, EPG)

            def first_of_highest(x3_, m, top, hot):
                order = consts[:, 1056:1056 + m].unsqueeze(1).to_broadcast([P, T, m])
                key = stat(T)
                dve.do(lambda e: e.tensor_reduce(top, x3_, AX, MAX))
                dve.do(lambda e: e.tensor_tensor(hot, x3_, bc(top, m), ALU.is_equal))
                dve.do(lambda e: e.tensor_tensor(hot, hot, order, MUL))
                dve.do(lambda e: e.tensor_reduce(key, hot, AX, MAX))
                dve.do(lambda e: e.tensor_tensor(hot, hot, bc(key, m), ALU.is_equal))
            g_gate, g_hot = stat(T), stat(T * NGRP)
            g_hot3 = g_hot.rearrange("p (t g) -> p t g", t=T)
            first_of_highest(lg3, NGRP, g_gate, g_hot3)
            pr, ep = stat(T * EXP), stat(T * EPG)
            le4 = le.rearrange("p (a b) -> p a b", b=EPG)
            dve.do(lambda e: e.tensor_tensor(pr.rearrange("p (a b) -> p a b", b=EPG), le4, bc(g_hot, EPG), MUL))
            ep3 = ep.rearrange("p (t b) -> p t b", t=T)
            pr4 = pr.rearrange("p (t g b) -> p t g b", t=T, g=NGRP)
            dve.do(lambda e: e.tensor_tensor(ep3, pr4[:, :, 0, :], pr4[:, :, 1, :], ADD))
            for g in (2, 3):
                dve.do(lambda e, g=g: e.tensor_tensor(ep3, ep3, pr4[:, :, g, :], ADD))
            top1, top2, hot1, hot2, tot = stat(T), stat(T), stat(T * EPG), stat(T * EPG), stat(T)
            h1, h2 = (a.rearrange("p (t b) -> p t b", t=T) for a in (hot1, hot2))
            first_of_highest(ep3, EPG, top1, h1)
            dve.do(lambda e: e.scalar_tensor_tensor(ep, hot1, -2.0, ep, MUL, ADD))
            first_of_highest(ep3, EPG, top2, h2)
            dve.do(lambda e: e.tensor_tensor(tot, top1, top2, ADD))
            dve.do(lambda e: e.reciprocal(tot, tot))
            dve.do(lambda e: e.tensor_tensor(tot, tot, g_gate, MUL))
            dve.do(lambda e: e.tensor_tensor(top1, top1, tot, MUL))
            dve.do(lambda e: e.tensor_tensor(top2, top2, tot, MUL))
            dve.do(lambda e: e.tensor_tensor(h1, h1, bc(top1, EPG), MUL))
            dve.do(lambda e: e.tensor_tensor(h2, h2, bc(top2, EPG), MUL))
            dve.do(lambda e: e.tensor_tensor(h1, h1, h2, ADD))
            comb = pr
            comb4 = pr4
            for t in range(T):
                for g in range(NGRP):
                    dve.do(lambda e, t=t, g=g: e.tensor_scalar(comb4[:, t, g, :], h1[:, t, :], g_hot3[:, t, g:g + 1], None, MUL))
            comb3 = comb.rearrange("p (t e) -> p t e", t=T)

            free = now()
            hid_ring = Ring([tuple(a[:, i * D:(i + 1) * D] for a in (y_hi, y_lo)) for i in range(2)])
            hid_ring.readers = [free, free]
            act_ring = Ring([R[2][:, 0:D], R[2][:, D:2 * D]])
            act_ring.readers = [free, free]

            def up(x):
                ai, hid, areaders = act_ring.take()
                hi_i, pair, hreaders = hid_ring.take()
                for w_name in ("w_gate", "w_up"):
                    out = [bulk.take() for _ in range(2)]
                    for k0 in range(0, KD, PK):
                        i, hi, lo, ready = piece(d[w_name][x][k0 * P:(k0 + PK) * P, :], FF)
                        for jj, (b, bank, readers) in enumerate(out):
                            for j in range(2):
                                cols = slice((2 * jj + j) * P, (2 * jj + j + 1) * P)
                                for k in range(PK):
                                    s = product(bank[:, j * S:(j + 1) * S], (hi[:, k, cols], lo[:, k, cols]), tuple(a[:, k0 + k, :] for a in hT),
                                                k0 + k == 0 and j == 0, k0 + k == KD - 1, ready + readers + h_ready, shared=True)
                            if k0 + PK == KD:
                                part = hid[:, jj * CH:(jj + 1) * CH]
                                if w_name == "w_gate":
                                    a = act.do(lambda e, part=part, bank=bank: e.activation(part, bank[:, :], ACT.Silu), after=[s] + areaders)
                                else:
                                    a = dve.do(lambda e, part=part, bank=bank: e.tensor_tensor(part, part, bank[:, :], MUL), after=[s, gated])
                                bulk.done(b, [a])
                        sring.done(i, [s])
                    gated = act.last
                done = split(pair, hid, after=[dve.last] + hreaders)
                act_ring.done(ai, done)
                return hi_i, tuple(a.rearrange("p (j s) -> p j s", j=4) for a in pair), done

            def down(x, hi_i, hid, ready):
                for n0 in range(0, D, CH):
                    def add(t, bank, step):
                        dst, cw = m3[:, t, n0:n0 + CH], comb3[:, t, x:x + 1]
                        if x == 0:
                            return [dve.do(lambda e: e.tensor_scalar(dst, bank[:, :], cw, None, MUL), after=[step] + free)]
                        return [dve.do(lambda e: e.scalar_tensor_tensor(dst, bank[:, :], cw, dst, MUL, ADD), after=[step])]
                    for _ in project(hid, d["w_down"][x][:, n0:n0 + CH], FF, CH, add, after=ready, banks=down_banks):
                        pass
                hid_ring.done(hi_i, [pe.last])
            down_banks = Ring(banks[4:8])
            down_banks.readers = [now() for _ in range(4)]
            pending = None
            for x in range(EXP):
                got = up(x)
                if pending is not None:
                    down(x - 1, *pending)
                pending = got
            down(EXP - 1, *pending)
            stores = []
            for t in range(T):
                s = dve.do(lambda e, t=t: e.tensor_tensor(x3[:, t, :], x3[:, t, :], m3[:, t, :], ADD))
                stores.append((out[t * P:(t + 1) * P, :], x3[:, t, :]))
            return sp.load("out", stores, after=[s])

        pos_rows = sb("positions", T + S)
        rows2 = sb("rows2", 64 * 2 + 128 * 2 + NGRP + EXP)
        selmask = sb("selected_mask", T * S, BF16)
        marks = [(lane, len(lane.queue), lane.last) for lane in (pe, dve, act, pool)]
        loads_mark, sem_marks = len(sp.queue), {n: e[1] for n, e in sp.sems.items()}
        for walk[0] in range(2):
            for lane, n, last in marks:
                del lane.queue[n:]
                lane.last = last
            del sp.queue[loads_mark:]
            for n, e in sp.sems.items():
                e[1] = sem_marks.get(n, 0)
            for ring in (wring, sring, bring, bulk, work, mixed, scr, gates):
                ring.at, ring.readers = 0, [[] for _ in ring.slots]
            hT_readers[:], yT_readers[:], merged_readers[:] = [], [], []
            for l in range(LAYERS):
                layer(l)
            final = second()
        for lane in (pe, dve, act, pool):
            lane.count()
        block = ctx.enter_context(nc.Block())

        @block.sync
        def _(e):
            sp.emit(e)
            e.wait_ge(final.sem, final.value)

        @block.tensor
        def _(e):
            pe.emit(e)

        @block.vector
        def _(e):
            dve.emit(e)

        @block.scalar
        def _(e):
            act.emit(e)

        @block.gpsimd
        def _(e):
            pool.emit(e)




def shape_constants():
    i = np.arange(P)
    c = np.zeros((P, 1408), np.float32)
    c[:, 0:128] = np.eye(P)
    c[:, 128:256] = i[:, None] <= i[None, :]
    c[:, 256:384] = 1.0
    c[:, 384:512] = i[:, None] > i[None, :]
    c[:, 512:640] = np.where(i[:, None] >= i[None, :], 0.0, NEG)
    c[:, 640:768] = np.where(i[None, :] > i[:, None], 0.0, NEG)
    c[:, 768:896] = np.where(i[:, None] >= i[None, :], 0.0, NEG)
    pos = np.arange(S, dtype=np.float32)
    inv = (np.float32(10000.0) ** (-np.arange(0, HD, 2, dtype=np.float32) / np.float32(HD))).astype(np.float32)
    ang = pos[:, None] * inv[None, :]
    for t in range(T):
        c[:, 896 + 32 * t:928 + 32 * t] = np.cos(ang[t * P:(t + 1) * P])
        c[:, 960 + 32 * t:992 + 32 * t] = np.sin(ang[t * P:(t + 1) * P])
    c[:, 1024:1056] = 1.0 / (np.float32(10000.0) ** (np.arange(0, HD, 2, dtype=np.float32) / np.float32(HD)))
    c[:, 1056:1064] = np.arange(8, 0, -1)
    return c


def kernel(**inputs):
    import concourse.bacc as bacc
    from concourse.bass_utils import run_bass_kernel_spmd as run

    nc = bacc.Bacc("TRN2", target_bir_lowering=False, num_devices=1,
                   dynamic_dma_scratch_size=1024)
    a = {k: np.asarray(v) for k, v in inputs.items()}
    cols, at = [], []

    def add(v):
        c0 = sum(x.shape[1] for x in cols)
        cols.append(v.reshape(-1, P).T)
        return c0
    for l in range(LAYERS):
        e = {"norm": add(a["norm_w"][l])}
        e["conv"] = [add(a["conv_w"][l][w]) for w in range(CONV_W)][0]
        e["conv_b"], e["ssm_norm"] = add(a["conv_b"][l]), add(a["ssm_norm_w"][l])
        at.append(e)
    e = {n: add(a[n + "_2"][0]) for n in ("g_mem", "g_mix", "g_ffn", "lam_re", "lam_im", "d_skip")}
    e["log_dt"] = add(np.repeat(a["log_dt_2"][0], SN))
    at.append(e)
    rows, rat = [], []

    def addr(v):
        r0 = sum(len(x) for x in rows)
        rows.append(v.reshape(-1))
        return r0
    for l in range(LAYERS):
        rat.append(addr(a["dt_bias"][l]))
        for n in ("a_log", "d_skip", "sinks", "f_bias", "gate_bias"):
            addr(a[n][l])
    e = {"final": addr(a["final_norm_w"]), "small": addr(a["g_q_2"][0])}
    for n in ("g_k_2", "g_qm_2", "g_km_2", "b_group_2", "b_expert_2"):
        addr(a[n][0])
    rat.append(e)
    b_pad, c_pad = {}, {}
    for part in ("re", "im"):
        b, c = a["b_" + part + "_2"][0], a["c_" + part + "_2"][0]
        bp, cp = np.zeros((P, ST, P), np.float32), np.zeros((P, ST, P), np.float32)
        for g in range(SG):
            i, g2 = divmod(g, 2)
            ch, st = 32 * (i % 4) + SH * g2, SN * g2
            bp[ch:ch + SH, i, st:st + SN] = b[g].T
            cp[st:st + SN, i, ch:ch + SH] = c[g].T
        b_pad[part], c_pad[part] = bp, cp
    arrays = {"x": a["x"][0], "w_in": a["w_in"], "w_proj": a["w_proj"], "w_out": a["w_out"],
              "consts": shape_constants(), "cols": np.concatenate(cols, 1), "rows": np.concatenate(rows)[None, :],
              "b_re": b_pad["re"], "b_im": b_pad["im"], "c_re": c_pad["re"], "c_im": c_pad["im"],
              "mem": a["mem_2"][0], "pos": a["positions_2"],
              "pos_col": a["positions_2"].reshape(T, P).T}
    for n in ("w_in", "w_out"):
        arrays[n + "_2"] = a[n + "_2"][0]
    for n in ("w_mem_kv", "w_glu", "w_up_ssm", "w_up_dsa", "w_up_mem", "w_group", "w_expert", "w_gate", "w_up", "w_down"):
        arrays[n] = a[n + "_2"][0]
    feed, d = {}, {}
    for n, v in arrays.items():
        v = np.ascontiguousarray(v)
        feed["in_" + n] = v
        d[n] = nc.dram_tensor("in_" + n, v.shape, mybir.dt.from_np(v.dtype), kind="ExternalInput").ap()
    d["cols_at"], d["rows_at"] = at, rat
    out = nc.dram_tensor("out_x", (S, D), F32, kind="ExternalOutput").ap()
    build(nc, d, out)
    r = run(nc, [feed], core_ids=[0])
    return r.results[0]["out_x"].reshape(1, S, D)
```
